# Optimizing a Trainium2 kernel written in Bass

```python
import math
import jax
import jax.numpy as jnp
from jax import lax
import numpy as np

D_MODEL = 1024
BATCH = 1
SEQ = 512
DEPTH = 1
DEC_BATCH = 8
DEC_SEQ = 4
PAST_LEN = 2048
PAGE_SIZE = 128

N_HEADS = 8
HEAD_DIM = 64
D_ATTN = N_HEADS * HEAD_DIM
MOBA_BLOCK = 256
MOBA_TOPK = 3
Q_BLOCK = 128
N_GROUPS = 8
D_SGU = 512
GROUP_DIM = D_SGU // N_GROUPS
CHUNK = 128
N_BUCKETS = 32
MAX_DISTANCE = 128
EPS = 1e-6
LN_EPS = 1e-5
SPLIT_POINTS = (D_ATTN, 2 * D_ATTN, 3 * D_ATTN, 4 * D_ATTN, 4 * D_ATTN + D_SGU, 4 * D_ATTN + 2 * D_SGU, 4 * D_ATTN + 3 * D_SGU, 4 * D_ATTN + 3 * D_SGU + D_MODEL)
D_IN_PROJ = 4 * D_ATTN + 3 * D_SGU + 2 * D_MODEL

kernel_name = 'hybrid_moba_gmlp_decode_step'

def rmsnorm(x, g):
    xf = x.astype(jnp.float32)
    y = xf * lax.rsqrt(jnp.mean(xf * xf, axis=-1, keepdims=True) + EPS)
    return (y * g.astype(jnp.float32)).astype(x.dtype)

def layernorm(x, g, b):
    xf = x.astype(jnp.float32)
    mu = jnp.mean(xf, axis=-1, keepdims=True)
    var = jnp.mean(jnp.square(xf - mu), axis=-1, keepdims=True)
    y = (xf - mu) * lax.rsqrt(var + LN_EPS)
    return (y * g.astype(jnp.float32) + b.astype(jnp.float32)).astype(x.dtype)

def rel_bucket(dist):
    max_exact = N_BUCKETS // 2
    d = jnp.maximum(dist, 0)
    df = jnp.maximum(d, 1).astype(jnp.float32)
    log_b = max_exact + (jnp.log(df / max_exact) / math.log(MAX_DISTANCE / max_exact) * (N_BUCKETS - max_exact)).astype(jnp.int32)
    return jnp.where(d < max_exact, d, jnp.minimum(log_b, N_BUCKETS - 1))

def mixer_inputs(x, norm_g, w_in, ln_g, ln_b):
    b, s = x.shape[0], x.shape[1]
    h = rmsnorm(x, norm_g)
    proj = jnp.einsum('bsd,de->bse', h, w_in)
    q, k, v, g_a, u, v_s, g_b, m_a, m_b = jnp.split(proj, SPLIT_POINTS, axis=-1)
    q = q.reshape(b, s, N_HEADS, HEAD_DIM)
    k = k.reshape(b, s, N_HEADS, HEAD_DIM)
    v = v.reshape(b, s, N_HEADS, HEAD_DIM)
    u = jax.nn.gelu(u)
    v_s = layernorm(jax.nn.gelu(v_s), ln_g, ln_b)
    return q, k, v, g_a, u, v_s, g_b, m_a, m_b

def merge_branches(x, attn, sgu, g_a, g_b, m_a, m_b, w_pa, w_pb, w_o):
    b, s = x.shape[0], x.shape[1]
    y_a = attn.reshape(b, s, D_ATTN) * jax.nn.silu(g_a)
    y_b = sgu * jax.nn.silu(g_b)
    mixed = jax.nn.sigmoid(m_a) * jnp.einsum('bse,ed->bsd', y_a, w_pa) + jax.nn.sigmoid(m_b) * jnp.einsum('bse,ed->bsd', y_b, w_pb)
    return x + jnp.einsum('bsd,de->bse', mixed, w_o)

def moba_prompt(q, k, v, rel_table):
    b, s = q.shape[0], q.shape[1]
    n_blk = -(-s // MOBA_BLOCK)
    n_qb = s // Q_BLOCK
    pad = n_blk * MOBA_BLOCK - s
    kb = jnp.pad(k, ((0, 0), (0, pad), (0, 0), (0, 0))).reshape(b, n_blk, MOBA_BLOCK, N_HEADS, HEAD_DIM).transpose(0, 3, 1, 2, 4)
    vb = jnp.pad(v, ((0, 0), (0, pad), (0, 0), (0, 0))).reshape(b, n_blk, MOBA_BLOCK, N_HEADS, HEAD_DIM).transpose(0, 3, 1, 2, 4)
    k_mean = jnp.mean(kb.astype(jnp.float32), axis=3)
    q_pos = jnp.arange(s)
    q_blk = q_pos // MOBA_BLOCK
    gate = jnp.einsum('bshd,bhnd->bhsn', q.astype(jnp.float32), k_mean)
    gate = jnp.where(jnp.arange(n_blk)[None, :] < q_blk[:, None], gate, -jnp.inf)
    n_sel = min(MOBA_TOPK, n_blk)
    _, sel = lax.top_k(gate, n_sel)
    valid = sel < q_blk[None, None, :, None]

    def to_items(a):
        return a.reshape(b, N_HEADS, n_qb, Q_BLOCK, n_sel).transpose(0, 2, 1, 3, 4).reshape(b * n_qb, N_HEADS, Q_BLOCK, n_sel)

    q_items = q.reshape(b * n_qb, Q_BLOCK, N_HEADS, HEAD_DIM)
    b_idx = jnp.repeat(jnp.arange(b), n_qb)
    qb_idx = jnp.tile(jnp.arange(n_qb), b)
    table_t = rel_table.T.astype(jnp.float32)
    offs = jnp.arange(MOBA_BLOCK)
    h_ar = jnp.arange(N_HEADS)[:, None, None]
    scale = HEAD_DIM ** -0.5
    n_k_sel = n_sel * MOBA_BLOCK

    def step(args):
        q_i, sel_i, valid_i, bi, qbi = args
        kb_i = kb[bi]
        vb_i = vb[bi]
        pos_i = qbi * Q_BLOCK + jnp.arange(Q_BLOCK)
        own = (qbi * Q_BLOCK) // MOBA_BLOCK
        k_sel = kb_i[h_ar, sel_i].astype(jnp.float32)
        v_sel = vb_i[h_ar, sel_i].astype(jnp.float32)
        k_own = lax.dynamic_index_in_dim(kb_i, own, axis=1, keepdims=False).astype(jnp.float32)
        v_own = lax.dynamic_index_in_dim(vb_i, own, axis=1, keepdims=False).astype(jnp.float32)
        qf = q_i.astype(jnp.float32) * scale
        sel_pos = sel_i[..., None] * MOBA_BLOCK + offs
        own_pos = own * MOBA_BLOCK + offs
        s_sel = jnp.einsum('qhd,hqnkd->hqnk', qf, k_sel) + table_t[h_ar[..., None], rel_bucket(pos_i[None, :, None, None] - sel_pos)]
        s_sel = jnp.where(valid_i[..., None], s_sel, -jnp.inf).reshape(N_HEADS, Q_BLOCK, n_k_sel)
        s_own = jnp.einsum('qhd,hkd->hqk', qf, k_own) + table_t[:, rel_bucket(pos_i[:, None] - own_pos[None, :])]
        s_own = jnp.where(own_pos[None, None, :] <= pos_i[None, :, None], s_own, -jnp.inf)
        p = jax.nn.softmax(jnp.concatenate([s_sel, s_own], axis=-1), axis=-1)
        out = jnp.einsum('hqk,hqkd->qhd', p[..., :n_k_sel], v_sel.reshape(N_HEADS, Q_BLOCK, n_k_sel, HEAD_DIM)) + jnp.einsum('hqk,hkd->qhd', p[..., n_k_sel:], v_own)
        return out.astype(q.dtype)

    out = lax.map(step, (q_items, to_items(sel), to_items(valid), b_idx, qb_idx))
    return out.reshape(b, s, N_HEADS, HEAD_DIM)

def moba_sample(q, k, v, cache_k, cache_v, layer, page_table, rel_table):
    db, t = q.shape[0], q.shape[1]
    n_pages = page_table.shape[1]
    past = n_pages * PAGE_SIZE
    ppb = MOBA_BLOCK // PAGE_SIZE
    own = past // MOBA_BLOCK
    n_full = own
    r = past - own * MOBA_BLOCK
    q_pos = past + jnp.arange(t)
    table_t = rel_table.T.astype(jnp.float32)
    scale = HEAD_DIM ** -0.5
    qf = q.astype(jnp.float32) * scale
    offs = jnp.arange(MOBA_BLOCK)
    logit_parts = []
    k_loc, v_loc = k, v
    if r > 0:
        own_pages = page_table[:, own * ppb:]
        k_loc = jnp.concatenate([cache_k[layer, own_pages].reshape(db, r, N_HEADS, HEAD_DIM).astype(k.dtype), k], axis=1)
        v_loc = jnp.concatenate([cache_v[layer, own_pages].reshape(db, r, N_HEADS, HEAD_DIM).astype(v.dtype), v], axis=1)
    loc_pos = own * MOBA_BLOCK + jnp.arange(r + t)
    s_loc = jnp.einsum('bthd,bkhd->bhtk', qf, k_loc.astype(jnp.float32)) + table_t[:, rel_bucket(q_pos[:, None] - loc_pos[None, :])][None]
    s_loc = jnp.where(loc_pos[None, None, None, :] <= q_pos[None, None, :, None], s_loc, -jnp.inf)
    if n_full > 0:
        k_full = cache_k[layer, page_table[:, :n_full * ppb]]
        k_mean = jnp.mean(k_full.astype(jnp.float32).reshape(db, n_full, ppb * PAGE_SIZE, N_HEADS, HEAD_DIM), axis=2)
        gate = jnp.einsum('bthd,bnhd->bhtn', q.astype(jnp.float32), k_mean)
        n_sel = min(MOBA_TOPK, n_full)
        _, sel = lax.top_k(gate, n_sel)
        page_idx = sel[..., None] * ppb + jnp.arange(ppb)
        phys = page_table[jnp.arange(db)[:, None, None, None, None], page_idx]
        h6 = jnp.arange(N_HEADS)[None, :, None, None, None, None]
        rows = jnp.arange(PAGE_SIZE)
        n_k_sel = n_sel * MOBA_BLOCK
        k_sel = cache_k[layer, phys[..., None], rows, h6].reshape(db, N_HEADS, t, n_k_sel, HEAD_DIM).astype(jnp.float32)
        v_sel = cache_v[layer, phys[..., None], rows, h6].reshape(db, N_HEADS, t, n_k_sel, HEAD_DIM).astype(jnp.float32)
        sel_pos = (sel[..., None] * MOBA_BLOCK + offs).reshape(db, N_HEADS, t, n_k_sel)
        h4 = jnp.arange(N_HEADS)[None, :, None, None]
        s_sel = jnp.einsum('bthd,bhtkd->bhtk', qf, k_sel) + table_t[h4, rel_bucket(q_pos[None, None, :, None] - sel_pos)]
        p = jax.nn.softmax(jnp.concatenate([s_sel, s_loc], axis=-1), axis=-1)
        out = jnp.einsum('bhtk,bhtkd->bthd', p[..., :n_k_sel], v_sel) + jnp.einsum('bhtk,bkhd->bthd', p[..., n_k_sel:], v_loc.astype(jnp.float32))
    else:
        p = jax.nn.softmax(s_loc, axis=-1)
        out = jnp.einsum('bhtk,bkhd->bthd', p, v_loc.astype(jnp.float32))
    return out.astype(q.dtype)

def sgu_prompt(u, v_n, w_s, b_s):
    b, s = u.shape[0], u.shape[1]
    nc = s // CHUNK
    vg = v_n.reshape(b, nc, CHUNK, N_GROUPS, GROUP_DIM)
    w = jnp.tril(w_s)
    z = jnp.einsum('gts,bcsgd->bctgd', w, vg) + b_s.T[None, None, :, :, None]
    return u * z.reshape(b, s, D_SGU)

def sgu_sample(u, v_n, w_s, b_s):
    b, t = u.shape[0], u.shape[1]
    vg = v_n.reshape(b, t, N_GROUPS, GROUP_DIM)
    w = jnp.tril(w_s[:, :t, :t])
    z = jnp.einsum('gts,bsgd->btgd', w, vg) + b_s[:, :t].T[None, :, :, None]
    return u * z.reshape(b, t, D_SGU)

def setup_inputs(seed: int = 0) -> dict:
    key = jax.random.key(seed)
    ks = jax.random.split(key, 18)
    n_pages = PAST_LEN // PAGE_SIZE
    n_used = DEC_BATCH * n_pages
    n_phys = (5 * n_used) // 4
    nrm = jax.random.normal
    f32 = jnp.float32
    x_prompt = nrm(ks[0], (BATCH, SEQ, D_MODEL), f32)
    x_sample = nrm(ks[1], (DEC_BATCH, DEC_SEQ, D_MODEL), f32)
    cache_k = nrm(ks[2], (DEPTH, n_phys, PAGE_SIZE, N_HEADS, HEAD_DIM), f32)
    cache_v = nrm(ks[3], (DEPTH, n_phys, PAGE_SIZE, N_HEADS, HEAD_DIM), f32)
    page_table = jax.random.permutation(ks[4], n_phys)[:n_used].reshape(DEC_BATCH, n_pages).astype(jnp.int32)
    rel_bias = 0.5 * nrm(ks[5], (N_BUCKETS, N_HEADS), f32)
    norm_g = 1.0 + 0.1 * nrm(ks[6], (DEPTH, D_MODEL), f32)
    w_in = nrm(ks[7], (DEPTH, D_MODEL, D_IN_PROJ), f32) * D_MODEL ** -0.5
    sgu_ln_g = 1.0 + 0.1 * nrm(ks[8], (DEPTH, D_SGU), f32)
    sgu_ln_b = 0.02 * nrm(ks[9], (DEPTH, D_SGU), f32)
    w_s = nrm(ks[10], (DEPTH, N_GROUPS, CHUNK, CHUNK), f32) * CHUNK ** -0.5
    b_s = 1.0 + 0.1 * nrm(ks[11], (DEPTH, N_GROUPS, CHUNK), f32)
    w_pa = nrm(ks[12], (DEPTH, D_ATTN, D_MODEL), f32) * D_ATTN ** -0.5
    w_pb = nrm(ks[13], (DEPTH, D_SGU, D_MODEL), f32) * D_SGU ** -0.5
    w_o = nrm(ks[14], (DEPTH, D_MODEL, D_MODEL), f32) * D_MODEL ** -0.5
    final_norm_g = 1.0 + 0.1 * nrm(ks[15], (D_MODEL,), f32)
    return {'x_prompt': x_prompt, 'x_sample': x_sample, 'cache_k': cache_k, 'cache_v': cache_v,
            'page_table': page_table, 'rel_bias': rel_bias, 'norm_g': norm_g, 'w_in': w_in,
            'sgu_ln_g': sgu_ln_g, 'sgu_ln_b': sgu_ln_b, 'w_s': w_s, 'b_s': b_s,
            'w_pa': w_pa, 'w_pb': w_pb, 'w_o': w_o, 'final_norm_g': final_norm_g}

def reference(x_prompt, x_sample, cache_k, cache_v, page_table, rel_bias, norm_g, w_in, sgu_ln_g, sgu_ln_b, w_s, b_s, w_pa, w_pb, w_o, final_norm_g):
    xp, xs = x_prompt, x_sample
    k_p_rows, v_p_rows, k_s_rows, v_s_rows, sgu_rows = [], [], [], [], []
    for l in range(DEPTH):
        q, k, v, g_a, u, v_n, g_b, m_a, m_b = mixer_inputs(xp, norm_g[l], w_in[l], sgu_ln_g[l], sgu_ln_b[l])
        attn = moba_prompt(q, k, v, rel_bias)
        sgu = sgu_prompt(u, v_n, w_s[l], b_s[l])
        xp = merge_branches(xp, attn, sgu, g_a, g_b, m_a, m_b, w_pa[l], w_pb[l], w_o[l])
        k_p_rows.append(k)
        v_p_rows.append(v)
        q, k, v, g_a, u, v_n, g_b, m_a, m_b = mixer_inputs(xs, norm_g[l], w_in[l], sgu_ln_g[l], sgu_ln_b[l])
        attn = moba_sample(q, k, v, cache_k, cache_v, l, page_table, rel_bias)
        sgu = sgu_sample(u, v_n, w_s[l], b_s[l])
        xs = merge_branches(xs, attn, sgu, g_a, g_b, m_a, m_b, w_pa[l], w_pb[l], w_o[l])
        k_s_rows.append(k)
        v_s_rows.append(v)
        sgu_rows.append(v_n)
    y_prompt = rmsnorm(xp, final_norm_g)
    y_sample = rmsnorm(xs, final_norm_g)
    k_prompt_new = jnp.stack(k_p_rows)
    v_prompt_new = jnp.stack(v_p_rows)
    k_sample_new = jnp.stack(k_s_rows)
    v_sample_new = jnp.stack(v_s_rows)
    sgu_v_sample_new = jnp.stack(sgu_rows)
    return (y_prompt, y_sample, k_prompt_new, v_prompt_new, k_sample_new, v_sample_new, sgu_v_sample_new)


_drawn_inputs = setup_inputs


def setup_inputs(seed=0):
    import zlib

    import numpy as np

    out = dict(_drawn_inputs(seed))
    spreads = {}
    factors = {'cache_k': 3.185, 'cache_v': 2.94, 'sgu_ln_b': 2.893, 'b_s': 2.74}
    for name, (base, spread) in spreads.items():
        noise = np.random.default_rng([zlib.crc32(name.encode()), seed]).standard_normal(out[name].shape)
        drawn = base * np.exp(spread * noise) if base else spread * noise
        out[name] = jnp.asarray(drawn.astype(out[name].dtype))
    for name, factor in factors.items():
        out[name] = (out[name] * factor).astype(out[name].dtype)
    return out
```

```python
import math
from contextlib import ExitStack

import numpy as np

import concourse.bass as bass
from concourse import mybir

F32 = mybir.dt.float32
F32R = mybir.dt.float32r
I32 = mybir.dt.int32
ALU = mybir.AluOpType
ACT = mybir.ActivationFunctionType
AX = mybir.AxisListType

P = 128
DM = 1024
SEQ = 512
NB = 8
TD = 4
NSR = NB * TD
ROWS = SEQ + NSR
HALF = ROWS // 2
KC = DM // P
NH = 8
HD = 64
DA = NH * HD
PAIRS = DA // P
PAST = 2048
PG = 128
NPG = PAST // PG
NBLK = 8
TOPK = 3
NBUCK = 32
MAXD = 128
EPS = 1e-6
LN_EPS = 1e-5
UNIT = 8.0
NEG = -1e30
N_IN = 44
N_QKV = 12
PER = 4
N_MIX = 8
N_OUT = 8
N_TILES = N_IN + N_MIX + N_OUT
GA, GU, GV, GB, GMA, GMB = 0, 4, 8, 12, 16, 24
GELU_C = math.sqrt(2.0 / math.pi)
VLEN = 384


def bucket(d):
    d = max(int(d), 0)
    if d < NBUCK // 2:
        return d
    half = NBUCK // 2
    return min(half + int(math.log(d / half) / math.log(MAXD / half) * (NBUCK - half)), NBUCK - 1)


def onehot(dists):
    e = np.zeros((NBUCK, len(dists)), np.float32)
    for n, d in enumerate(dists):
        e[bucket(d), n] += UNIT
        e[NBUCK - 1, n] -= UNIT
    return e


C_ID, C_OSEL, C_TRI = 0, 128, 160
C_COLS = 224
I_E15, I_ELOC, I_EVEC, I_VMASK, I_LOCM = 0, 512, 640, 1024, 1408
I_COLS = 1664
T_TRIL, T_REP, T_DIAG = 0, 128, 160
T_COLS = 192
GATE_STEPS = ([("silu", GA), ("silu", GA + 2)]
              + [(kind, g0) for g0 in (GV, GV + 2, GU, GU + 2) for kind in ("square", "gelu")]
              + [("silu", GB), ("silu", GB + 2)])


def constants():
    c = np.zeros((P, C_COLS), np.float32)
    c[:, C_ID:C_ID + P] = np.eye(P)
    row, col = np.arange(P)[:, None], np.arange(P)[None, :]
    c[64:128, C_OSEL:C_OSEL + 32] = row[64:128] % 32 == col[:, 0:32]
    c[:, C_TRI:C_TRI + 64] = (np.arange(8)[None, :] < np.arange(8)[:, None]).reshape(1, 64)
    i = np.zeros((NBUCK, I_COLS), np.float32)
    for t in range(TD):
        i[:, I_E15 + t * P:I_E15 + (t + 1) * P] = onehot([P + t - j for j in range(P)])
        i[:, I_ELOC + t * 32:I_ELOC + (t + 1) * 32] = onehot([t - j for _ in range(NB) for j in range(TD)])
    i[:, I_EVEC:I_EVEC + VLEN] = onehot([255 - u for u in range(VLEN)])
    i[:, I_VMASK:I_VMASK + VLEN] = np.where(np.arange(VLEN) > 255, NEG, 0.0)
    m = np.full((NH, TD, NB, NB, TD), NEG, np.float32)
    for b in range(NB):
        for t in range(TD):
            m[:, t, b, b, :t + 1] = 0.0
    i[:, I_LOCM:I_LOCM + 256] = m.reshape(32, 256)
    s = np.zeros((P, T_COLS), np.float32)
    s[:, T_TRIL:T_TRIL + P] = row <= col
    s[:, T_REP:T_REP + 32] = row == np.arange(32)[None, :] % TD
    s[0:32, T_DIAG:T_DIAG + 32] = np.arange(32)[:, None] // TD == np.arange(32)[None, :] // TD
    return c, i, s


def build(nc, x_p, x_s, cache_k, cache_v, page_table, rel_bias, norm_g, w_in, ln_g, ln_b, w_s, b_s, w_pa, w_pb,
          w_o, fin_g, cst, ini, sgc, y_p, y_s, k_p, v_p, k_s, v_s, sgu_s):
    with ExitStack() as ctx:
        base = (nc.sbuf_base + 31) // 32 * 32
        top = [base]

        def at(name, shape, dt, offset):
            t = nc.alloc_sbuf_tensor_at(name, shape, dt, offset=offset)
            return t

        def sb(name, shape, dt=F32):
            size = 4 * int(np.prod(shape[1:]))
            off = top[0]
            top[0] += (size + 31) // 32 * 32
            return at(name, shape, dt, off)

        def mark():
            return top[0]

        def sem(name):
            return ctx.enter_context(nc.semaphore(name))

        x_at = mark()
        XH = sb("XH", [P, KC, ROWS], F32R)
        XL = sb("XL", [P, KC, ROWS], F32R)
        WRAW = sb("WRAW", [P, 2, KC, 2 * P])
        WH = sb("WH", [P, 2, KC, P], F32R)
        WL = sb("WL", [P, 2, KC, P], F32R)
        kv_at = mark()
        KRAW = sb("KRAW", [P, 2, 4, DA])
        VRAW = sb("VRAW", [P, 2, 4, DA])
        KTH = sb("KTH", [P, 2, DA], F32R)
        KTL = sb("KTL", [P, 2, DA], F32R)
        VH = sb("VH", [P, 2, DA], F32R)
        VL = sb("VL", [P, 2, DA], F32R)
        g_at = mark()
        G = sb("G", [P, 32, ROWS])
        CST = sb("CST", [P, C_COLS])
        PTB = sb("PTB", [1, NB * NPG], I32)
        B15 = sb("B15", [32, P])
        LM = sb("LM", [32, NB, 32])
        Q16 = sb("Q16", [P, PAIRS, NB, 16], F32R)
        QC = sb("QC", [P, PAIRS, 2, 32], F32R)
        KSH = sb("KSH", [P, PAIRS, NSR], F32R)
        KSL = sb("KSL", [P, PAIRS, NSR], F32R)
        VSH = sb("VSH", [NSR, DA], F32R)
        OTS = at("OTS", [P, DA], F32, top[0] - 4 * DA)[64:128, :]
        VSL = sb("VSL", [NSR, DA], F32R)
        tmp_at = mark()
        SC = sb("SC", [32, NPG * P + 32])
        PT = sb("PT", [P, NPG, 64], F32R)
        PTL = sb("PTL", [32, 64], F32R)
        ATS = sb("ATS", [P, PAIRS, NSR])
        KSUM = sb("KSUM", [32, NPG])
        PMX = sb("PMX", [32, NPG])
        GATE = sb("GATE", [32, 8])
        CM1 = sb("CM1", [32, 8, 8])
        CM2 = sb("CM2", [32, 8, 8])
        RANK = sb("RANK", [32, 8])
        SEL = sb("SEL", [32, 8])
        BMX = sb("BMX", [32, 9])
        M1 = sb("M1", [32, 1])
        NEGM = sb("NEGM", [32, 1])
        EB = sb("EB", [32, 8])
        LSUM = sb("LSUM", [32, 9])
        LT = sb("LT", [32, 1])
        RL = sb("RL", [64, 1])
        SS = sb("SS", [P, 8])
        MS = sb("MS", [P, 8])
        RSTD = sb("RSTD", [P, 8])
        NHALF = sb("NHALF", [P, 1])
        NMX = sb("NMX", [P, 4 * NH])
        PLS = sb("PLS", [P, 4 * NH])
        assert top[0] <= nc.sbuf_usable_end, (top[0], nc.sbuf_usable_end)

        o = g_at
        XR = at("XR", [P, 5, DM], F32, o); o += 5 * DM * 4
        GBC = at("GBC", [P, DM], F32, o); o += DM * 4
        JUNK = at("JUNK", [P, DM], F32, o); o += DM * 4
        TS = at("TS", [P, 4, ROWS], F32, o); o += 4 * ROWS * 4
        RS = at("RS", [P, 4, 4, P], F32, o); o += 4 * 4 * P * 4
        RSS = at("RSS", [NSR, 4, P], F32, o); o += 4 * P * 4
        INI = at("INI", [NBUCK, I_COLS], F32, o); o += I_COLS * 4
        TAB = at("TAB", [NBUCK, NH], F32, o); o += NH * 4
        TB = at("TB", [NBUCK, TD, 32], F32, o); o += TD * 32 * 4
        VEC = at("VEC", [NH, VLEN], F32, o); o += VLEN * 4
        assert o <= g_at + 32 * ROWS * 4
        o = kv_at
        PQ = at("PQ", [P, PAIRS, SEQ], F32, o); o += 8192
        PK = at("PK", [P, PAIRS, SEQ], F32, o); o += 8192
        o = kv_at + 32768
        QHS = at("QHS", [P, SEQ], F32R, o); o += 2048
        QLS = at("QLS", [P, SEQ], F32R, o); o += 2048
        KHS = at("KHS", [P, SEQ], F32R, o); o += 2048
        KLS = at("KLS", [P, SEQ], F32R, o); o += 2048
        o = x_at
        PX = at("PX", [P, 2, SEQ], F32, o); o += 4096
        PTH = at("PTH", [P, 2, 4, P], F32R, o); o += 4096
        PTLO = at("PTLO", [P, 2, 4, P], F32R, o); o += 4096
        VPH = at("VPH", [P, 4, 2, P], F32R, o); o += 4096
        VPL = at("VPL", [P, 4, 2, P], F32R, o); o += 4096
        TPZ = at("TPZ", [P, NH, 256], F32, o); o += 8192
        PVB = at("PVB", [P, 2, 4, P], F32, o); o += 4096
        BSB = at("BSB", [P, PAIRS, P], F32, o); o += 2048
        assert o <= x_at + 2 * 17408
        GT = at("GT", [P, 2, ROWS], F32, tmp_at)
        o = kv_at + 16384
        WSR = at("WSR", [P, NH, P], F32, o); o += 4096
        LNG = at("LNG", [P, DA], F32, o); o += 2048
        LNB = at("LNB", [P, DA], F32, o); o += 2048
        WST = at("WST", [P, NH, P], F32, o); o += 4096
        SGC = at("SGC", [P, T_COLS], F32, o); o += T_COLS * 4
        assert o <= kv_at + 32768
        o = kv_at
        VN = at("VN", [P, 4, DA], F32, o); o += 8192
        VNS = at("VNS", [NSR, DA], F32, o); o += 2048
        TZ = at("TZ", [P, 2, PAIRS, P], F32, o); o += 4096
        WSB = at("WSB", [NSR, NH, NSR], F32, o); o += 1024
        BST = at("BST", [P, 2, 8], F32, o); o += 64
        assert o <= kv_at + 16384
        MH = at("MH", [P, KC, ROWS], F32R, kv_at)
        ML = at("ML", [P, KC, ROWS], F32R, kv_at + 17408)
        o = g_at + 8 * ROWS * 4
        FX = at("FX", [P, 5, DM], F32, o); o += 5 * DM * 4
        FG = at("FG", [P, DM], F32, o); o += DM * 4
        FJ = at("FJ", [P, DM], F32, o); o += DM * 4
        assert o <= g_at + 32 * ROWS * 4

        BK = [ctx.enter_context(nc.psum_tensor(f"BK{i}", [P, 512], F32)) for i in range(8)]
        KTP = [BK[2], BK[3]]
        SCB = [BK[4], BK[5]]
        PTP = BK[6][:].rearrange("p (g x) -> p g x", g=NPG)
        OUT = BK[7][0:64, :]
        OTP = BK[7][:, 0:32].rearrange("p (c x) -> p c x", c=PAIRS)
        LOC = BK[7][0:32, 64:96]
        PTLP = BK[7][0:32, 96:128]

        IDN = CST[:, C_ID:C_ID + P]
        OSEL = CST[64:128, C_OSEL:C_OSEL + 32].rearrange("p (c x) -> p c x", c=PAIRS)
        TRI = CST[0:32, C_TRI:C_TRI + 64].rearrange("p (n m) -> p n m", n=8)

        q_d = nc.dram_tensor("q_scratch", [PAIRS, P, SEQ], F32, kind="Internal").ap()
        k_d = nc.dram_tensor("k_scratch", [PAIRS, P, SEQ], F32, kind="Internal").ap()
        skew_d = nc.dram_tensor("skew_scratch", [P, NH, P + VLEN], F32, kind="Internal").ap()

        x_ld = [sem(f"x_ld{r}") for r in range(5)]
        cst_ld, ini_ld, pt_ld, gbc_ld = sem("cst_ld"), sem("ini_ld"), sem("pt_ld"), sem("gbc_ld")
        w_ld = [sem("w_ld0"), sem("w_ld1")]
        k_ld = [sem("k_ld0"), sem("k_ld1")]
        v_ld = [sem("v_ld0"), sem("v_ld1")]
        ss_ok, ms_ok, rstd_ok, xn_ok = sem("ss_ok"), sem("ms_ok"), sem("rstd_ok"), sem("xn_ok")
        xt_pe, xt_hi, xt_lo = sem("xt_pe"), sem("xt_hi"), sem("xt_lo")
        tb_ok, tab_pe, tab_ok, vec_st = sem("tb_ok"), sem("tab_pe"), sem("tab_ok"), sem("vec_st")
        w_hi, w_lo, pj, pj_ev = sem("w_hi"), sem("w_lo"), sem("pj"), sem("pj_ev")
        rows_pe, rs_ev, smp_ok = sem("rows_pe"), sem("rs_ev"), sem("smp_ok")
        ts_st = [sem(f"ts_st{i}") for i in range(4)]
        rs_st = [sem(f"rs_st{i}") for i in range(4)]
        kt_pe, kth, ktl, qk_pe = sem("kt_pe"), sem("kth"), sem("ktl"), sem("qk_pe")
        vh, vl, pv_pe = sem("vh"), sem("vl"), sem("pv_pe")
        qc_ok, loc_pe, sc_ok, eb_ok, ex_ok = sem("qc_ok"), sem("loc_pe"), sem("sc_ok"), sem("eb_ok"), sem("ex_ok")
        ptt_pe, pth_ok, ptl_ok = sem("ptt_pe"), sem("pth_ok"), sem("ptl_ok")
        ots_ok, ot_ev = sem("ots_ok"), sem("ot_ev")
        dchain, pchain, zero_ok = sem("dchain"), sem("pchain"), sem("zero_ok")
        att_ld, tpz_ld, sgw_ld, ln_ld, bs_ld = sem("att_ld"), sem("tpz_ld"), sem("sgw_ld"), sem("ln_ld"), sem("bs_ld")
        stg_hi, stg_lo = sem("stg_hi"), sem("stg_lo")
        aq_pe, am_ok, ae_ok, ap_ok, at_pe, ath_ok, atl_ok, av_pe, ao_ok = (sem(n) for n in (
            "aq_pe", "am_ok", "ae_ok", "ap_ok", "at_pe", "ath_ok", "atl_ok", "av_pe", "ao_ok"))
        el_act, el_dve, m_ok, y_ok = sem("el_act"), sem("el_dve"), sem("m_ok"), sem("y_ok")
        pvb_ld = [sem("pvb_ld0"), sem("pvb_ld1")]
        wst_pe, wst_ok, wsb_pe, wsb_ok = sem("wst_pe"), sem("wst_ok"), sem("wsb_pe"), sem("wsb_ok")
        vr_pe, var_ok, vrs_ok, vn_ok, sgu_st = sem("vr_pe"), sem("var_ok"), sem("vrs_ok"), sem("vn_ok"), sem("sgu_st")
        z_pe, z_ev, y_hi, y_lo = sem("z_pe"), sem("z_ev"), sem("y_hi"), sem("y_lo")
        mix_ok, mx_hi, mx_lo = sem("mix_ok"), sem("mx_hi"), sem("mx_lo")
        fx_ld, fg_ld, fr_pe, h_ok, fss_ok, fms_ok, frs_ok, fy_ok, y_st = (sem(n) for n in (
            "fx_ld", "fg_ld", "fr_pe", "h_ok", "fss_ok", "fms_ok", "frs_ok", "fy_ok", "y_st"))

        def wait(eng, s, v):
            if not isinstance(v, int) or v > 0:
                eng.wait_ge(s, v)

        def w_need(m):
            if not isinstance(m, int):
                return None
            return sum(32 if N_IN <= 2 * i < N_IN + N_MIX else 16 for i in range(m % 2, m + 1, 2))

        block = ctx.enter_context(nc.Block())

        def load_w(sp, m, slot, before):
            wait(sp, w_lo, before)
            if isinstance(m, int) and m >= N_IN // 2:
                if m < (N_IN + N_MIX) // 2:
                    c = (m - N_IN // 2) * 2 * P
                    for k0, src in ((0, w_pa), (4, w_pb)):
                        sp.dma_start(WRAW[:, slot, k0:k0 + 4, :],
                                     src[0, :, c:c + 2 * P].rearrange("(k p) n -> p k n", p=P)).then_inc(w_ld[slot], 16)
                else:
                    c = (m - (N_IN + N_MIX) // 2) * 2 * P
                    sp.dma_start(WRAW[:, slot], w_o[0, :, c:c + 2 * P].rearrange("(k p) n -> p k n", p=P)).then_inc(w_ld[slot], 16)
            else:
                sp.dma_start(WRAW[:, slot], w_in[0, :, bass.ds(m * 2 * P, 2 * P)].rearrange("(k p) n -> p k n", p=P)).then_inc(w_ld[slot], 16)

        @block.sync
        def _(sp):
            for r in range(5):
                if r < 4:
                    sp.dma_start(XR[:, r, :], x_p[0, r * P:(r + 1) * P, :]).then_inc(x_ld[r], 16)
                else:
                    sp.dma_start(XR[0:NSR, r, :], x_s.rearrange("b t d -> (b t) d")).then_inc(x_ld[r], 16)
                if r == 0:
                    sp.dma_start(GBC[:], bass.AP(norm_g.tensor, norm_g.offset, [[0, P], [1, DM]])).then_inc(gbc_ld, 16)
                    sp.dma_start(CST[:], cst).then_inc(cst_ld, 16)
                if r == 2:
                    load_w(sp, 0, 0, 0)
            load_w(sp, 1, 1, 0)
            sp.dma_start(PTB[:], page_table.rearrange("(a b) n -> a (b n)", a=1)).then_inc(pt_ld, 16)
            sp.dma_start(INI[:], ini).then_inc(ini_ld, 16)
            sp.dma_start(TAB[:], rel_bias).then_inc(ini_ld, 16)
            for m in range(2, N_QKV // 2 + 1):
                load_w(sp, m, m % 2, 2 * m - 2)
            sp.wait_ge(pt_ld, 16)
            regs = [sp.alloc_register(f"page{j}") for j in range(4)]

            def load_pages(pool, ring, sems, b, q):
                sp.load(regs, PTB[0:1, bass.ds(NPG * b + 4 * q, 4)])
                for j in range(4):
                    page = sp.snap(regs[j], min_val=0, max_val=cache_k.shape[1] - 1)
                    src = pool[0, bass.ds(page, 1)].rearrange("a p h d -> (a p) (h d)")
                    sp.dma_start(ring[:, q % 2, j, :], src).then_inc(sems[q % 2], 16)

            def sample(b, pv, kk, quads=range(4)):
                for q in quads:
                    if kk:
                        wait(sp, kt_pe, 16 * b + 4 * (q - 1))
                        load_pages(cache_k, KRAW, k_ld, b, q)
                    if pv:
                        wait(sp, vl, 16 * (b - 1) + 4 * (q - 1))
                        load_pages(cache_v, VRAW, v_ld, b - 1, q)
                    if kk and q == 0:
                        load_w(sp, 2 * b + 7, 1, 4 * b + 12)
                    if kk and q == 2:
                        load_w(sp, 2 * b + 8, 0, 4 * b + 14)

            sample(0, False, True)
            sample(1, True, True)
            with sp.Fori(2, NB - 1) as b:
                sample(b, True, True)
            sample(NB - 1, True, True)
            sample(NB, True, False, range(2))
            for i in range(4):
                sp.wait_ge(ts_st[i], 16 * 2)
                sp.wait_ge(rs_st[i], 32 * 2)
            sp.wait_ge(vec_st, 16)
            sp.wait_ge(kt_pe, 16 * NB)
            sp.dma_start(PQ[:], q_d.rearrange("c p n -> p c n")).then_inc(att_ld, 16)
            sp.dma_start(PK[:], k_d.rearrange("c p n -> p c n")).then_inc(att_ld, 16)
            sp.wait_ge(pj, 2 * N_IN)
            sp.dma_start(TPZ[:], skew_d[:, :, P - 1:P - 1 + 256]).then_inc(tpz_ld, 16)

            def load_pair(c):
                wait(sp, stg_hi, 6 * c - 6)
                wait(sp, stg_lo, 6 * c - 6)
                src = v_p[0, 0].rearrange("(r p) h d -> p r (h d)", p=P)[:, :, c * P:(c + 1) * P]
                sp.dma_start(PVB[:, c % 2], src).then_inc(pvb_ld[c % 2], 16)

            load_pair(0)
            load_pair(1)
            sample(NB, True, False, range(2, 4))
            for e in range(2):
                sp.dma_start(BSB[e * HD:(e + 1) * HD], bass.AP(b_s.tensor, b_s.offset + e * P, [[0, HD], [2 * P, PAIRS], [1, P]])).then_inc(bs_ld, 16)
            sp.wait_ge(vl, 16 * NB)
            sp.dma_start(WSR[:], w_s[0].rearrange("g t s -> t g s")).then_inc(sgw_ld, 16)
            sp.dma_start(SGC[:], sgc).then_inc(sgw_ld, 16)
            sp.dma_start(LNG[:], bass.AP(ln_g.tensor, ln_g.offset, [[0, P], [1, DA]])).then_inc(ln_ld, 16)
            sp.dma_start(LNB[:], bass.AP(ln_b.tensor, ln_b.offset, [[0, P], [1, DA]])).then_inc(ln_ld, 16)
            load_pair(2)
            load_pair(3)
            for m in range(23, N_TILES // 2):
                load_w(sp, m, m % 2, 2 * m - 2)
            sp.wait_ge(mx_lo, 2 * N_MIX)
            for r in range(4):
                sp.dma_start(FX[:, r, :], x_p[0, r * P:(r + 1) * P, :]).then_inc(fx_ld, 16)
            sp.dma_start(FX[0:NSR, 4, :], x_s.rearrange("b t d -> (b t) d")).then_inc(fx_ld, 16)
            sp.dma_start(FG[:], bass.AP(fin_g.tensor, fin_g.offset, [[0, P], [1, DM]])).then_inc(fg_ld, 16)
            for r in range(5):
                sp.wait_ge(fy_ok, r + 1)
                if r < 4:
                    sp.dma_start(y_p[0, r * P:(r + 1) * P, :], FX[:, r, :]).then_inc(y_st, 16)
                else:
                    sp.dma_start(y_s.rearrange("b t d -> (b t) d"), FX[0:NSR, 4, :]).then_inc(y_st, 16)
            sp.wait_ge(y_st, 16 * 5)
            sp.wait_ge(sgu_st, 16)

        @block.tensor
        def _(pe):
            mm = pe.matmul

            def half(n, par, h, XA=XH, XB=XL, read=None):
                if h == 0:
                    pe.wait_ge(w_lo, n + 1)
                wait(pe, pj_ev, 2 * n + h - 1 if read is None else read)
                cols = slice(h * HALF, (h + 1) * HALF)
                for k in range(KC):
                    for w, x in ((WH, XA), (WH, XB), (WL, XA)):
                        last = mm(BK[h][:, 0:HALF], w[:, par, k, :], x[:, k, cols], start=(k == 0 and w is WH and x is XA),
                                  stop=(k == KC - 1 and w is WL))
                    if k == KC - 1:
                        last.then_inc(pj, 1)
                    yield

            def run(g, steps=99):
                for _ in range(steps):
                    if next(g, 0) == 0:
                        break

            pe.wait_ge(cst_ld, 16)
            for u in range(10):
                r, kk = u // 2, u % 2
                n = P if r < 4 else NSR
                wait(pe, xn_ok, r + 1)
                wait(pe, xt_lo, u - 3)
                for j in range(4):
                    k = 4 * kk + j
                    last = pe.transpose(BK[4 + u % 4][:, j * n:(j + 1) * n], XR[0:n, r, k * P:(k + 1) * P], IDN[0:n, 0:n])
                last.then_inc(xt_pe, 1)

            def rows(n):
                i = n - 4
                pe.wait_ge(pj_ev, 2 * n + 2)
                wait(pe, rs_ev, i - 1)
                bp, bs = BK[4 + 2 * (i % 2)], BK[5 + 2 * (i % 2)]
                for r in range(4):
                    pe.transpose(bp[:, r * P:(r + 1) * P], TS[:, n % 4, r * P:(r + 1) * P], IDN)
                pe.transpose(bs[0:NSR, 0:P], TS[:, n % 4, SEQ:ROWS], IDN).then_inc(rows_pe, 1)

            pe.wait_ge(xt_lo, 10)
            for n in range(N_QKV):
                run(half(n, n % 2, 0))
                if n == 1:
                    pe.wait_ge(tb_ok, 1)
                    for t in range(TD):
                        mm(BK[2][0:32, 0:P], TB[:, t, :], INI[:, I_E15 + t * P:I_E15 + (t + 1) * P], start=(t == 0), stop=(t == 3))
                    for t in range(TD):
                        mm(BK[3][0:32, 0:32], TB[:, t, :], INI[:, I_ELOC + t * 32:I_ELOC + (t + 1) * 32], start=(t == 0), stop=(t == 3))
                    mm(BK[3][0:NH, 64:64 + VLEN], TAB[:], INI[:, I_EVEC:I_EVEC + VLEN], start=True, stop=True).then_inc(tab_pe, 1)
                if n - 1 >= 4:
                    rows(n - 1)
                run(half(n, n % 2, 1))
            rows(N_QKV - 1)

            def turn_page(b, p):
                q, i = p // 4, 16 * b + p
                if p % 4 == 0:
                    pe.wait_ge(k_ld[q % 2], 64 * (2 * b + q // 2 + 1))
                wait(pe, ktl, i - 1)
                if isinstance(b, int) and b == 0 and p == 0:
                    pe.wait_ge(tab_ok, 1)
                for c in range(PAIRS):
                    last = pe.transpose(KTP[p % 2][:, c * P:(c + 1) * P], KRAW[:, q % 2, p % 4, c * P:(c + 1) * P], IDN)
                last.then_inc(kt_pe, 1)

            def scores(out, hi, lo):
                for c in range(PAIRS):
                    for w, x in ((0, hi), (0, lo), (1, hi)):
                        last = mm(out, QC[:, c, w, :], x[c], start=(c == 0 and w == 0 and x is hi), stop=(c == PAIRS - 1 and w == 1))
                return last

            def score_page(b, p):
                if p == 0:
                    pe.wait_ge(qc_ok, b + 1)
                    if isinstance(b, int) and b == 0:
                        pe.wait_ge(rs_ev, 8)
                        pe.wait_ge(smp_ok, 12)
                if p % 4 == 0:
                    wait(pe, sc_ok, 4 * b + p // 4 - 1)
                pe.wait_ge(ktl, 16 * b + p + 1)
                hi, lo = ([w[:, p % 2, c * P:(c + 1) * P] for c in range(PAIRS)] for w in (KTH, KTL))
                scores(SCB[p // 4 % 2][0:32, p % 4 * P:(p % 4 + 1) * P], hi, lo).then_inc(qk_pe, 1)

            def value_page(b, p):
                if p == 0:
                    pe.wait_ge(ptl_ok, b + 1)
                    mm(OUT, PTL[:], VSH[:], start=True, stop=False)
                    mm(OUT, PTL[:], VSL[:], start=False, stop=False)
                pe.wait_ge(vl, 16 * b + p + 1)
                mm(OUT, PT[:, p, :], VH[:, p % 2, :], start=False, stop=False)
                mm(OUT, PT[:, p, :], VL[:, p % 2, :], start=False, stop=(p == NPG - 1)).then_inc(pv_pe, 1)

            def turn_out():
                for c in range(PAIRS):
                    last = mm(OTP[:, c, :], OTS[:, c * P:(c + 1) * P], OSEL[:, c, :], start=True, stop=True, skip_group_check=True)
                return last

            def sample(b, pv):
                n0 = N_QKV + PER * b
                gens = {}

                def g(j, h, steps):
                    if (j, h) not in gens:
                        gens[j, h] = half(n0 + j, j % 2, h)
                    run(gens[j, h], steps)

                for p in range(NPG):
                    turn_page(b, p)
                    g(p // 8, p % 8 // 4, 2)
                    if p:
                        score_page(b, p - 1)
                    if pv:
                        value_page(b - 1, p)
                g(2, 0, 2)
                score_page(b, NPG - 1)
                g(2, 0, 3)
                if pv:
                    pe.wait_ge(ots_ok, b)
                    turn_out()
                scores(LOC, [KSH[:, c, :] for c in range(PAIRS)], [KSL[:, c, :] for c in range(PAIRS)]).then_inc(loc_pe, 1)
                g(2, 0, 3)
                g(2, 1, 8)
                pe.wait_ge(ex_ok, 2 * b + 1)
                wait(pe, ptl_ok, b)
                g(3, 0, 1)
                for p in range(8):
                    pe.transpose(PTP[:, p, :], SC[:, p * P:(p + 1) * P], IDN[0:32, 0:32])
                g(3, 0, 2)
                pe.wait_ge(ex_ok, 2 * b + 2)
                g(3, 0, 1)
                for p in range(8, NPG):
                    pe.transpose(PTP[:, p, :], SC[:, p * P:(p + 1) * P], IDN[0:32, 0:32])
                pe.transpose(PTLP, SC[:, NPG * P:NPG * P + 32], IDN[0:32, 0:32]).then_inc(ptt_pe, 1)
                g(3, 0, 4)
                g(3, 1, 8)

            sample(0, False)
            with pe.Fori(1, NB) as b:
                sample(b, True)

            def a_scores(v):
                hd, i = v // 4, v % 4
                e = hd % 2
                if i == 0:
                    pe.wait_ge(stg_lo, 3 * hd + 2)
                if v < 3:
                    pe.wait_ge(pj_ev, 2 * N_IN)
                    pe.wait_ge(ktl, 16 * NB)
                wait(pe, ae_ok, v - 2)
                rr = slice(e * HD, (e + 1) * HD)
                n = (i + 1) * P
                for w, x in ((QHS, KHS), (QHS, KLS), (QLS, KHS)):
                    last = mm(BK[v % 3][:, 0:n], w[rr, i * P:(i + 1) * P], x[rr, 0:n], start=(w is QHS and x is KHS), stop=(w is QLS))
                last.then_inc(aq_pe, 1)

            def a_turn(v):
                i = v % 4
                pe.wait_ge(ap_ok, v + 1)
                wait(pe, atl_ok, v - 1)
                for j in range(i + 1):
                    last = pe.transpose(BK[3 + v % 2][:, j * P:(j + 1) * P], PX[:, v % 2, j * P:(j + 1) * P], IDN)
                last.then_inc(at_pe, 1)

            def a_values(v):
                hd, i = v // 4, v % 4
                c, e = hd // 2, hd % 2
                if i == 0:
                    pe.wait_ge(stg_lo, 3 * hd + 3)
                if i == 0 and e == 0:
                    wait(pe, ao_ok, c - 1)
                pe.wait_ge(atl_ok, v + 1)
                ob = BK[5 + c % 2]
                for j in range(i + 1):
                    for w, x in ((VPH, PTH), (VPH, PTLO), (VPL, PTH)):
                        last = mm(ob[:, i * P:(i + 1) * P], w[:, j, e, :], x[:, v % 2, j, :],
                                  start=(e == 0 and i == 0 and j == 0 and w is VPH and x is PTH), stop=True, skip_group_check=True)
                last.then_inc(av_pe, 1)

            NU = 4 * NH
            for v in range(-2, NU + 1):
                if v + 2 < NU:
                    a_scores(v + 2)
                if 0 <= v + 2 < NPG:
                    value_page(NB - 1, v + 2)
                if 0 <= v < NU:
                    a_turn(v)
                if 1 <= v:
                    a_values(v - 1)
                if v == 19:
                    pe.wait_ge(ots_ok, NB)
                    turn_out().then_inc(loc_pe, 1)

            pe.wait_ge(sgw_ld, 32)
            for g in range(NH):
                last = pe.transpose(BK[g // 4][:, g % 4 * P:(g % 4 + 1) * P], WSR[:, g, :], IDN)
            last.then_inc(wst_pe, 1)
            pe.wait_ge(el_dve, 6)
            for r in range(5):
                n = P if r < 4 else NSR
                wait(pe, vn_ok, r - 1)
                for c in range(PAIRS):
                    last = pe.transpose(BK[2 + r % 2][0:n, c * P:(c + 1) * P], G[:, GV + c, r * P:r * P + n], IDN)
                last.then_inc(vr_pe, 1)
            pe.wait_ge(wst_ok, 1)
            rep = SGC[:, T_REP:T_REP + 32]
            mm(BK[4][0:32, 0:256], rep, bass.AP(WST[:].tensor, WST[:].offset, [list(WST[:].ap[0]), [P, NH], [0, NB], [1, TD]]), start=True, stop=True).then_inc(wsb_pe, 1)
            pe.wait_ge(ao_ok, 4)
            pe.wait_ge(ot_ev, NB)
            for r in range(4):
                pe.wait_ge(vn_ok, r + 1)
                wait(pe, z_ev, r - 1)
                for c in range(PAIRS):
                    bk = BK[(6, 0)[r % 2] + c // 2]
                    last = mm(bk[:, c % 2 * 256:c % 2 * 256 + 256], VN[:, r, c * P:(c + 1) * P], WST[:, 2 * c:2 * c + 2, :],
                              start=True, stop=True, skip_group_check=True)
                last.then_inc(z_pe, 1)
            pe.wait_ge(vn_ok, 5)
            pe.wait_ge(wsb_ok, 1)
            for c in range(PAIRS):
                last = mm(BK[5][:, c * 64:(c + 1) * 64], VNS[:, c * P:(c + 1) * P], WSB[:, 2 * c:2 * c + 2, :],
                          start=True, stop=True, skip_group_check=True)
            last.then_inc(z_pe, 1)

            pe.wait_ge(y_lo, 2)
            for j in range(N_MIX):
                n = N_IN + j
                pe.wait_ge(w_lo, n + 1)
                for h in range(2):
                    wait(pe, mix_ok, 2 * j + h - 1)
                    for br in range(2):
                        for k in range(4 * br, 4 * br + 4):
                            for w, x in ((WH, XH), (WH, XL), (WL, XH)):
                                last = mm(BK[h + 2 * br][:, 0:HALF], w[:, n % 2, k, :], x[:, k, h * HALF:(h + 1) * HALF],
                                          start=(k % 4 == 0 and w is WH and x is XH), stop=(k % 4 == 3 and w is WL))
                    last.then_inc(pj, 1)
            def out_rows(u):
                kk, r = u // 5, u % 5
                n = P if r < 4 else NSR
                wait(pe, h_ok, u - 3)
                for j in range(4):
                    last = pe.transpose(BK[4 + u % 4][0:n, j * P:(j + 1) * P], G[:, 4 * kk + j, r * P:r * P + n], IDN)
                last.then_inc(fr_pe, 1)

            pe.wait_ge(mx_lo, 2 * N_MIX)
            for j in range(N_OUT):
                n = N_IN + N_MIX + j
                run(half(n, n % 2, 0, MH, ML, 2 * (N_IN + j) - 1))
                if j == 4:
                    pe.wait_ge(pj_ev, 2 * (N_IN + j))
                    for u in range(5):
                        out_rows(u)
                run(half(n, n % 2, 1, MH, ML, 2 * (N_IN + j)))
            pe.wait_ge(pj_ev, 2 * (N_IN + N_OUT))
            for u in range(5, 10):
                out_rows(u)

        @block.scalar
        def _(act):
            def copy(o, i):
                return act.activation(o, i, ACT.Copy)

            def split_hi(n, slot, side, par, need):
                act.wait_ge(w_ld[slot], need)
                wait(act, pj, 2 * n - 2)
                copy(WH[:, par], WRAW[:, slot, :, side * P:(side + 1) * P]).then_inc(w_hi, 1)

            for r in range(5):
                n = P if r < 4 else NSR
                act.wait_ge(x_ld[r], 16)
                if r:
                    act.wait_ge(ss_ok, r)
                act.activation(JUNK[0:n], XR[0:n, r, :], ACT.Square, accum_out=SS[0:n, r:r + 1]).then_inc(ss_ok, 1)
            for n in range(2):
                split_hi(n, 0, n, n, w_need(0))
            for u in range(10):
                r, kk = u // 2, u % 2
                n = P if r < 4 else NSR
                act.wait_ge(xt_pe, u + 1)
                copy(XH[:, 4 * kk:4 * kk + 4, r * P:r * P + n], BK[4 + u % 4][:, 0:4 * n].rearrange("p (k n) -> p k n", k=4)).then_inc(xt_hi, 1)
            for n in range(N_QKV):
                for h in range(2):
                    act.wait_ge(pj, 2 * n + h + 1)
                    if h == 0 and n >= 4:
                        if n - 4 < 8:
                            act.wait_ge(ts_st[n % 4], 16 * ((n - 4) // 4 + 1))
                        wait(act, rows_pe, n - 4 - 4 + 1)
                        wait(act, smp_ok, min(n - 3, 8))
                    copy(TS[:, n % 4, h * HALF:(h + 1) * HALF], BK[h][:, 0:HALF]).then_inc(pj_ev, 1)
                m = (n + 2) // 2
                split_hi(n + 2, m % 2, n % 2, n % 2, w_need(m))

            def page_hi(b, p):
                i = 16 * b + p
                act.wait_ge(kt_pe, i + 1)
                wait(act, qk_pe, i - 1)
                copy(KTH[:, p % 2, :], KTP[p % 2][:]).then_inc(kth, 1)

            def page_scores(b, q):
                act.wait_ge(qk_pe, 16 * b + 4 * q + 4)
                if q == 0:
                    wait(act, ptt_pe, b)
                for p in range(4 * q, 4 * q + 4):
                    last = act.activation(SC[:, p * P:(p + 1) * P], SCB[q % 2][0:32, p % 4 * P:(p % 4 + 1) * P], ACT.Copy,
                                          accum_out=KSUM[:, p:p + 1])
                last.then_inc(sc_ok, 1)

            def evac(b, j, h):
                n = N_QKV + PER * b + j
                act.wait_ge(pj, 2 * n + h + 1)
                copy(G[:, bass.ds(PER * b + j, 1), h * HALF:(h + 1) * HALF].rearrange("p a n -> p (a n)"), BK[h][:, 0:HALF]).then_inc(pj_ev, 1)

            def split_loop(b, j):
                m2 = j // 2
                if isinstance(b, int) and b == NB - 1 and j >= 4:
                    need = w_need(N_IN // 2)
                else:
                    need = 16 * (b + 3 + m2)
                split_hi(N_QKV + PER * b + j, m2 % 2, j % 2, j % 2, need)

            def sample(b, pv):
                if isinstance(b, int) and b == 0:
                    for i in range(4):
                        act.wait_ge(ts_st[i], 32)
                        act.wait_ge(rs_st[i], 64)
                    act.wait_ge(rs_ev, 8)
                    act.wait_ge(smp_ok, 12)
                    act.wait_ge(tab_ok, 1)
                    act.wait_ge(vec_st, 16)
                for p in range(NPG):
                    page_hi(b, p)
                    if p == 4:
                        evac(b, 0, 0)
                    if p == 8:
                        evac(b, 0, 1)
                    if p == 9:
                        split_loop(b, 2)
                    if p == 12:
                        evac(b, 1, 0)
                    if p in (5, 9, 13):
                        page_scores(b, (p - 5) // 4)
                evac(b, 1, 1)
                page_scores(b, 3)
                split_loop(b, 3)
                evac(b, 2, 0)
                evac(b, 2, 1)
                act.wait_ge(eb_ok, b + 1)
                for n in range(8):
                    blk = SC[:, 2 * n * P:2 * (n + 1) * P]
                    e = act.activation(blk, blk, ACT.Exp, bias=EB[:, n:n + 1], scale=1.0 / UNIT, accum_out=LSUM[:, n:n + 1])
                    if n == 3:
                        e.then_inc(ex_ok, 1)
                loc = SC[:, NPG * P:NPG * P + 32]
                act.activation(loc, loc, ACT.Exp, bias=NEGM[:], scale=1.0 / UNIT, accum_out=LSUM[:, 8:9]).then_inc(ex_ok, 1)
                split_loop(b, 4)
                act.wait_ge(ptt_pe, b + 1)
                copy(PT[:, :, 0:32], PTP)
                copy(PTL[:, 0:32], PTLP).then_inc(pth_ok, 1)
                evac(b, 3, 0)
                evac(b, 3, 1)
                split_loop(b, 5)

            sample(0, False)
            with act.Fori(1, NB - 1) as b:
                sample(b, True)
            sample(NB - 1, True)

            def stage_qk(hd):
                c, rr = hd // 2, slice(hd % 2 * HD, (hd % 2 + 1) * HD)
                if hd == 0:
                    act.wait_ge(att_ld, 32)
                wait(act, aq_pe, 4 * (hd - 1))
                copy(QHS[rr, :], PQ[rr, c, :]).then_inc(stg_hi, 1)
                copy(KHS[rr, :], PK[rr, c, :]).then_inc(stg_hi, 1)

            def stage_v(hd):
                c, e = hd // 2, hd % 2
                if hd == 0:
                    act.wait_ge(zero_ok, 5)
                act.wait_ge(pvb_ld[c % 2], 16 * (c // 2 + 1))
                wait(act, av_pe, 4 * (hd - 1))
                copy(VPH[:, :, e, e * HD:(e + 1) * HD], PVB[:, c % 2, :, e * HD:(e + 1) * HD]).then_inc(stg_hi, 1)

            def gate_step(s):
                kind, g0 = GATE_STEPS[s]
                wait(act, el_dve, s)
                if kind == "square":
                    act.activation(GT[:], G[:, g0:g0 + 2, :], ACT.Square, scale=math.sqrt(0.044715)).then_inc(el_act, 1)
                elif kind == "gelu":
                    act.activation(GT[:], GT[:], ACT.Tanh, scale=GELU_C).then_inc(el_act, 1)
                else:
                    act.activation(GT[:], G[:, g0:g0 + 2, :], ACT.Tanh, scale=0.5).then_inc(el_act, 1)

            NU = 4 * NH
            for hd in range(2):
                stage_qk(hd)
                stage_v(hd)
            for v in range(-1, NU):
                if v + 1 < NU:
                    n = ((v + 1) % 4 + 1) * P
                    act.wait_ge(am_ok, v + 2)
                    wait(act, at_pe, v)
                    act.activation(PX[:, (v + 1) % 2, 0:n], BK[(v + 1) % 3][:, 0:n], ACT.Exp, bias=NMX[:, v + 1:v + 2],
                                   scale=1.0 / UNIT, accum_out=PLS[:, v + 1:v + 2]).then_inc(ae_ok, 1)
                if v >= 0:
                    i, nxt = v % 4, v // 4 + 1
                    act.wait_ge(at_pe, v + 1)
                    wait(act, av_pe, v - 1)
                    copy(PTH[:, v % 2, 0:i + 1, :], BK[3 + v % 2][:, 0:(i + 1) * P].rearrange("p (j n) -> p j n", j=i + 1)).then_inc(ath_ok, 1)
                    if 2 <= nxt < NH:
                        if i == 0:
                            stage_qk(nxt)
                        if i == 1:
                            stage_v(nxt)
                    if v % 2 == 0 and v // 2 < len(GATE_STEPS):
                        gate_step(v // 2)
                    if v >= 24:
                        g0 = GMA + (v - 24) * 2
                        act.activation(G[:, g0:g0 + 2, :], G[:, g0:g0 + 2, :], ACT.Tanh, scale=0.5).then_inc(m_ok, 1)
            act.wait_ge(y_ok, 1)
            act.wait_ge(av_pe, NU)
            copy(XH[:, 0:4, :], G[:, GA:GA + 4, :]).then_inc(y_hi, 1)
            act.wait_ge(y_ok, 2)
            copy(XH[:, 4:8, :], G[:, GB:GB + 4, :]).then_inc(y_hi, 1)
            act.wait_ge(sgu_st, 16)
            for j in range(N_MIX):
                for h in range(2):
                    act.wait_ge(mix_ok, 2 * j + h + 1)
                    copy(MH[:, j, h * HALF:(h + 1) * HALF], G[:, GMA + j, h * HALF:(h + 1) * HALF]).then_inc(mx_hi, 1)
                n = N_IN + j + 2
                split_hi(n, n // 2 % 2, n % 2, n % 2, w_need(n // 2))
            for j in range(N_OUT):
                n = N_IN + N_MIX + j
                for h in range(2):
                    act.wait_ge(pj, 2 * n + h + 1)
                    copy(G[:, j, h * HALF:(h + 1) * HALF], BK[h][:, 0:HALF]).then_inc(pj_ev, 1)
                if j + 2 < N_OUT:
                    split_hi(n + 2, (n + 2) // 2 % 2, n % 2, n % 2, w_need((n + 2) // 2))
            for r in range(5):
                n = P if r < 4 else NSR
                act.wait_ge(h_ok, 5 + r + 1)
                if r:
                    act.wait_ge(fss_ok, r)
                act.activation(FJ[0:n], FX[0:n, r, :], ACT.Square, accum_out=SS[0:n, r:r + 1]).then_inc(fss_ok, 1)

        @block.vector
        def _(dve):
            chain, loop_links, first_links = [0], [0], [0]

            def link(ins, b=None):
                ins.then_inc(dchain, 1)
                chain[0] += 1
                dve.wait_ge(dchain, chain[0] if b is None else (b - 1) * loop_links[0] + chain[0])

            def f32(t):
                return t.bitcast(F32)

            def split_lo(n, slot, side, par):
                dve.wait_ge(w_hi, n + 1)
                dve.tensor_tensor(WL[:, par], WRAW[:, slot, :, side * P:(side + 1) * P], f32(WH[:, par]), ALU.subtract).then_inc(w_lo, 1)

            dve.memset(TB[:], 0.0).then_inc(zero_ok, 1)
            dve.memset(NHALF[:], -0.5).then_inc(zero_ok, 1)
            dve.memset(Q16[:].bitcast(F32), 0.0).then_inc(zero_ok, 1)
            dve.memset(QC[:].bitcast(F32), 0.0).then_inc(zero_ok, 1)
            dve.wait_ge(zero_ok, 4)
            for r in range(5):
                n = P if r < 4 else NSR
                dve.wait_ge(ss_ok, r + 1)
                dve.tensor_scalar(MS[0:n, r:r + 1], SS[0:n, r:r + 1], 1.0 / DM, EPS, ALU.mult, ALU.add).then_inc(ms_ok, 1)
            dve.wait_ge(gbc_ld, 16)
            for r in range(5):
                n = P if r < 4 else NSR
                dve.wait_ge(rstd_ok, r + 1)
                dve.scalar_tensor_tensor(out=XR[0:n, r, :], in0=XR[0:n, r, :], scalar=RSTD[0:n, r:r + 1], in1=GBC[0:n], op0=ALU.mult,
                                         op1=ALU.mult).then_inc(xn_ok, 1)
            for n in range(2):
                split_lo(n, 0, n, n)
            for u in range(10):
                r, kk = u // 2, u % 2
                n = P if r < 4 else NSR
                dve.wait_ge(xt_hi, u + 1)
                dst = slice(r * P, r * P + n)
                dve.tensor_tensor(XL[:, 4 * kk:4 * kk + 4, dst], BK[4 + u % 4][:, 0:4 * n].rearrange("p (k n) -> p k n", k=4),
                                  f32(XH[:, 4 * kk:4 * kk + 4, dst]), ALU.subtract).then_inc(xt_lo, 1)
            dve.wait_ge(ini_ld, 32)
            for t in range(TD):
                last = dve.tensor_copy(TB[:, t, t:t + 29:4], TAB[:])
            last.then_inc(tb_ok, 1)
            dve.wait_ge(tab_pe, 1)
            dve.tensor_copy(B15[:], BK[2][0:32, 0:P])
            lmo = LM[:]
            src = BK[3][0:32, 0:32]
            dve.tensor_tensor(lmo, bass.AP(src.tensor, src.offset, [list(src.ap[0]), [0, NB], [1, 32]]),
                              INI[:, I_LOCM:I_LOCM + 256].rearrange("p (b n) -> p b n", b=NB), ALU.add)
            dve.tensor_tensor(VEC[:], BK[3][0:NH, 64:64 + VLEN], INI[0:NH, I_VMASK:I_VMASK + VLEN], ALU.add).then_inc(tab_ok, 1)

            def rows_out(n):
                i, c = n - 4, n % 4
                bp, bs = BK[4 + 2 * (i % 2)], BK[5 + 2 * (i % 2)]
                dve.wait_ge(rows_pe, i + 1)
                wait(dve, rs_st[n % 4], 32 * (i // 4))
                dve.tensor_copy(RS[:, n % 4], bp[:].rearrange("p (r n) -> p r n", r=4))
                link(dve.tensor_copy(RSS[:, n % 4], bs[0:NSR, 0:P]))
                dve.sem_inc(rs_ev, 1)
                if n >= 8:
                    vc = slice(c * P, (c + 1) * P)
                    link(dve.tensor_copy(VSH[:, vc], RSS[:, n % 4]))
                    dve.tensor_tensor(VSL[:, vc], RSS[:, n % 4], f32(VSH[:, vc]), ALU.subtract).then_inc(smp_ok, 1)

            for n in range(N_QKV):
                c = n % 4
                if n < 8:
                    dve.wait_ge(pj_ev, 2 * n + 2)
                    smp = TS[:, n % 4, SEQ:ROWS]
                    if n < 4:
                        for e in range(2):
                            rr = slice(e * HD, (e + 1) * HD)
                            sv = TS[rr, n % 4, SEQ:ROWS].rearrange("p (b t) -> p b t", t=TD)
                            link(dve.tensor_copy(Q16[rr, c, :, 4 * e:4 * e + 4], sv))
                            last = dve.tensor_tensor(Q16[rr, c, :, 8 + 4 * e:12 + 4 * e], sv, f32(Q16[rr, c, :, 4 * e:4 * e + 4]), ALU.subtract)
                        last.then_inc(smp_ok, 1)
                    else:
                        link(dve.tensor_copy(KSH[:, c, :], smp))
                        dve.tensor_tensor(KSL[:, c, :], smp, f32(KSH[:, c, :]), ALU.subtract).then_inc(smp_ok, 1)
                if n - 1 >= 4:
                    rows_out(n - 1)
                m = (n + 2) // 2
                split_lo(n + 2, m % 2, n % 2, n % 2)
            rows_out(N_QKV - 1)

            def page_lo(b, p):
                i = 16 * b + p
                dve.wait_ge(kth, i + 1)
                dve.tensor_tensor(KTL[:, p % 2, :], KTP[p % 2][:], f32(KTH[:, p % 2, :]), ALU.subtract).then_inc(ktl, 1)

            def value_hi(b, p):
                q, i = p // 4, 16 * b + p
                if p % 4 == 0:
                    dve.wait_ge(v_ld[q % 2], 64 * (2 * b + q // 2 + 1))
                wait(dve, pv_pe, i - 1)
                dve.tensor_copy(VH[:, p % 2, :], VRAW[:, q % 2, p % 4, :]).then_inc(vh, 1)

            def split_loop(b, j):
                m2 = j // 2
                split_lo(N_QKV + PER * b + j, m2 % 2, j % 2, j % 2)

            def page_maxima(b, q, lb):
                dve.wait_ge(sc_ok, 4 * b + q + 1)
                if q == 3:
                    last_page = SC[:, (NPG - 1) * P:NPG * P]
                    link(dve.tensor_tensor(last_page, last_page, B15[:], ALU.add), lb)
                return dve.tensor_reduce(PMX[:, 4 * q:4 * q + 4], SC[:, 4 * q * P:4 * (q + 1) * P].rearrange("p (g n) -> p g n", g=4), AX.X, ALU.max)

            def scale_out(b):
                dve.wait_ge(pv_pe, 16 * (b + 1))
                dve.tensor_scalar(OTS, OUT, RL[:], None, ALU.mult).then_inc(ots_ok, 1)

            def out_sample(b):
                for e in range(2):
                    rr = slice(e * HD, (e + 1) * HD)
                    last = dve.tensor_copy(ATS[rr, :, bass.ds(TD * b, TD)], OTP[rr, :, 4 * e:4 * e + 4])
                last.then_inc(ot_ev, 1)

            def sample(b, pv):
                lb = None if isinstance(b, int) and b == 0 else b
                if lb is not None:
                    chain[0] = first_links[0]
                for p in range(NPG):
                    page_lo(b, p)
                    if pv and p + 1 < NPG:
                        value_hi(b - 1, p + 1)
                    if p == 10:
                        split_loop(b, 2)
                    if p in (6, 10, 14):
                        page_maxima(b, (p - 6) // 4, lb)
                if pv:
                    scale_out(b - 1)
                link(page_maxima(b, 3, lb), lb)
                dve.wait_ge(loc_pe, b + 1)
                loc = SC[:, NPG * P:NPG * P + 32]
                link(dve.tensor_tensor(loc, LOC, LM[:, bass.ds(b, 1), :].rearrange("p a n -> p (a n)"), ALU.add), lb)
                dve.tensor_reduce(BMX[:, 8:9], loc, AX.X, ALU.max)
                if pv:
                    out_sample(b - 1)
                dve.tensor_tensor(BMX[:, 0:8], PMX[:, 0::2], PMX[:, 1::2], ALU.max)
                link(dve.tensor_tensor(GATE[:], KSUM[:, 0::2], KSUM[:, 1::2], ALU.add), lb)
                ga = GATE[:]
                by_m = bass.AP(ga.tensor, ga.offset, [list(ga.ap[0]), [0, 8], [1, 8]])
                by_n = bass.AP(ga.tensor, ga.offset, [list(ga.ap[0]), [1, 8], [0, 8]])
                dve.tensor_tensor(CM1[:], by_m, by_n, ALU.is_gt)
                link(dve.tensor_tensor(CM2[:], by_m, by_n, ALU.is_equal), lb)
                link(dve.tensor_tensor(CM2[:], CM2[:], TRI, ALU.mult), lb)
                link(dve.tensor_tensor(CM1[:], CM1[:], CM2[:], ALU.add), lb)
                link(dve.tensor_reduce(RANK[:], CM1[:], AX.X, ALU.add), lb)
                link(dve.tensor_scalar(SEL[:], RANK[:], TOPK - 0.5, NEG, ALU.is_ge, ALU.mult), lb)
                link(dve.tensor_tensor(BMX[:, 0:8], BMX[:, 0:8], SEL[:], ALU.add), lb)
                link(dve.tensor_reduce(M1[:], BMX[:], AX.X, ALU.max), lb)
                link(dve.tensor_scalar(NEGM[:], M1[:], -1.0 / UNIT, None, ALU.mult), lb)
                dve.tensor_scalar(EB[:], SEL[:], NEGM[:], None, ALU.add).then_inc(eb_ok, 1)
                split_loop(b, 3)
                value_hi(b, 0)
                split_loop(b, 4)
                dve.wait_ge(ex_ok, 2 * b + 2)
                link(dve.tensor_reduce(LT[:], LSUM[:], AX.X, ALU.add), lb)
                dve.reciprocal(RL[0:32, :], LT[:])
                dve.reciprocal(RL[32:64, :], LT[:])
                dve.wait_ge(pth_ok, b + 1)
                dve.tensor_tensor(PT[:, :, 32:64], PTP, f32(PT[:, :, 0:32]), ALU.subtract)
                dve.tensor_tensor(PTL[:, 32:64], PTLP, f32(PTL[:, 0:32]), ALU.subtract).then_inc(ptl_ok, 1)
                split_loop(b, 5)
                if lb is not None:
                    assert chain[0] - first_links[0] == loop_links[0]

            start = chain[0]
            sample(0, False)
            first_links[0] = chain[0]
            loop_links[0] = chain[0] - start
            with dve.Fori(1, NB) as b:
                sample(b, True)
            chain[0] = first_links[0] + loop_links[0] * (NB - 1)

            NU = 4 * NH
            v_next = [1]

            def more_values(n):
                for _ in range(n):
                    if v_next[0] < NPG:
                        value_hi(NB - 1, v_next[0])
                        v_next[0] += 1

            def attended(c):
                dve.wait_ge(av_pe, 8 * (c + 1))
                dve.wait_ge(el_dve, 2)
                dve.tensor_tensor(G[:, GA + c, 0:SEQ], BK[5 + c % 2][:], G[:, GA + c, 0:SEQ], ALU.mult).then_inc(ao_ok, 1)

            more_values(1)
            for v in range(-1, NU + 1):
                if v + 1 < NU:
                    hd, i = (v + 1) // 4, (v + 1) % 4
                    n = (i + 1) * P
                    bk = BK[(v + 1) % 3]
                    dve.wait_ge(aq_pe, v + 2)
                    if v == -1:
                        dve.wait_ge(tpz_ld, 16)
                    w = min(n, 2 * P)
                    link(dve.tensor_tensor(bk[:, n - w:n], bk[:, n - w:n], TPZ[:, hd, 256 - w:256], ALU.add))
                    link(dve.tensor_reduce(NMX[:, v + 1:v + 2], bk[:, 0:n], AX.X, ALU.max))
                    dve.tensor_scalar(NMX[:, v + 1:v + 2], NMX[:, v + 1:v + 2], -1.0 / UNIT, None, ALU.mult).then_inc(am_ok, 1)
                if v < NPG - 1:
                    more_values(1)
                if 0 <= v < NU:
                    n = (v % 4 + 1) * P
                    dve.wait_ge(ae_ok, v + 1)
                    link(dve.reciprocal(PLS[:, v:v + 1], PLS[:, v:v + 1]))
                    dve.tensor_scalar(PX[:, v % 2, 0:n], PX[:, v % 2, 0:n], PLS[:, v:v + 1], None, ALU.mult).then_inc(ap_ok, 1)
                if v >= 0 and v < NU:
                    i = v % 4
                    dve.wait_ge(ath_ok, v + 1)
                    dve.tensor_tensor(PTLO[:, v % 2, 0:i + 1, :], BK[3 + v % 2][:, 0:(i + 1) * P].rearrange("p (j n) -> p j n", j=i + 1),
                                      f32(PTH[:, v % 2, 0:i + 1, :]), ALU.subtract).then_inc(atl_ok, 1)
                if v % 2 == 1 and 0 <= v // 2 < len(GATE_STEPS):
                    kind, g0 = GATE_STEPS[v // 2]
                    dve.wait_ge(el_act, v // 2 + 1)
                    gx = G[:, g0:g0 + 2, :]
                    dve.scalar_tensor_tensor(out=GT[:] if kind == "square" else gx, in0=GT[:], scalar=1.0, in1=gx, op0=ALU.add,
                                             op1=ALU.mult).then_inc(el_dve, 1)
                if v == 17:
                    scale_out(NB - 1)
                if v == 21:
                    dve.wait_ge(loc_pe, NB + 1)
                    out_sample(NB - 1)
                if v >= 9 and v % 8 == 1:
                    attended(v // 8 - 1)

            attended(PAIRS - 1)
            dve.wait_ge(ot_ev, NB)
            dve.tensor_tensor(G[:, GA:GA + 4, SEQ:ROWS], G[:, GA:GA + 4, SEQ:ROWS], ATS[:], ALU.mult).then_inc(y_ok, 1)
            dve.wait_ge(wst_pe, 1)
            dve.wait_ge(sgw_ld, 32)
            tr = SGC[:, T_TRIL:T_TRIL + P]
            trb = bass.AP(tr.tensor, tr.offset, [list(tr.ap[0]), [0, 4], [1, P]])
            for x in range(2):
                last = dve.tensor_tensor(WST[:, 4 * x:4 * x + 4, :], BK[x][:].rearrange("p (g n) -> p g n", g=4), trb, ALU.mult)
            last.then_inc(wst_ok, 1)
            dve.wait_ge(ln_ld, 32)
            for r in range(5):
                n = P if r < 4 else NSR
                bk = BK[2 + r % 2]
                dst = VN[:, r, :] if r < 4 else VNS[:]
                dve.wait_ge(vr_pe, r + 1)
                link(dve.bn_stats(BST[0:n, 0, 0:6], bk[0:n, :]))
                link(dve.bn_aggr(BST[0:n, 1, 0:2], BST[0:n, 0, 0:6]))
                dve.tensor_scalar(MS[0:n, r:r + 1], BST[0:n, 1, 1:2], 4.0 * LN_EPS, None, ALU.add).then_inc(var_ok, 1)
                dve.wait_ge(vrs_ok, r + 1)
                link(dve.tensor_scalar(dst, bk[0:n, :], BST[0:n, 1, 0:1], RSTD[0:n, r:r + 1], ALU.subtract, ALU.mult))
                link(dve.tensor_tensor(dst, dst, LNG[0:n], ALU.mult))
                dve.tensor_tensor(dst, dst, LNB[0:n], ALU.add).then_inc(vn_ok, 1)
            dve.wait_ge(wsb_pe, 1)
            dg = SGC[0:32, T_DIAG:T_DIAG + 32]
            dve.tensor_tensor(WSB[:], BK[4][0:32, 0:256].rearrange("p (g n) -> p g n", g=NH),
                              bass.AP(dg.tensor, dg.offset, [list(dg.ap[0]), [0, NH], [1, 32]]), ALU.mult).then_inc(wsb_ok, 1)
            dve.wait_ge(bs_ld, 32)
            dve.wait_ge(el_dve, len(GATE_STEPS))
            for r in range(4):
                dve.wait_ge(z_pe, r + 1)
                tz = TZ[:, r % 2]
                for e in range(2):
                    rr = slice(e * HD, (e + 1) * HD)
                    for x in range(2):
                        bv = BK[(6, 0)[r % 2] + x][rr, :].rearrange("p (c e n) -> p c e n", c=2, e=2)[:, :, e, :]
                        last = dve.tensor_tensor(tz[rr, 2 * x:2 * x + 2, :], bv, BSB[rr, 2 * x:2 * x + 2, :], ALU.add)
                last.then_inc(z_ev, 1)
                dve.wait_ge(z_ev, r + 1)
                link(dve.tensor_tensor(tz, tz, G[:, GU:GU + 4, r * P:(r + 1) * P], ALU.mult))
                gb = G[:, GB:GB + 4, r * P:(r + 1) * P]
                link(dve.scalar_tensor_tensor(out=gb, in0=tz, scalar=0.5, in1=gb, op0=ALU.mult, op1=ALU.mult))
            dve.wait_ge(z_pe, 5)
            for e in range(2):
                rr = slice(e * HD, (e + 1) * HD)
                for c in range(PAIRS):
                    bv = BK[5][rr, 64 * c + 32 * e:64 * c + 32 * e + 32].rearrange("p (b t) -> p b t", t=TD)
                    bsv = BSB[rr, c, 0:TD]
                    last = dve.tensor_tensor(TZ[rr, 0, c, 0:32].rearrange("p (b t) -> p b t", t=TD), bv,
                                             bass.AP(bsv.tensor, bsv.offset, [list(bsv.ap[0]), [0, NB], [1, TD]]), ALU.add)
            link(last)
            link(dve.tensor_tensor(TZ[:, 0, :, 0:32], TZ[:, 0, :, 0:32], G[:, GU:GU + 4, SEQ:ROWS], ALU.mult))
            gb = G[:, GB:GB + 4, SEQ:ROWS]
            dve.scalar_tensor_tensor(out=gb, in0=TZ[:, 0, :, 0:32], scalar=0.5, in1=gb, op0=ALU.mult, op1=ALU.mult).then_inc(y_ok, 1)
            for k in range(2):
                dve.wait_ge(y_hi, k + 1)
                g0 = (GA, GB)[k]
                dve.tensor_tensor(XL[:, 4 * k:4 * k + 4, :], G[:, g0:g0 + 4, :], f32(XH[:, 4 * k:4 * k + 4, :]), ALU.subtract).then_inc(y_lo, 1)
            dve.wait_ge(m_ok, 8)
            for j in range(N_MIX):
                n = N_IN + j
                for h in range(2):
                    cs = slice(h * HALF, (h + 1) * HALF)
                    dve.wait_ge(pj, 2 * n + h + 1)
                    ga, gb = G[:, GMA + j, cs], G[:, GMB + j, cs]
                    dve.scalar_tensor_tensor(out=ga, in0=ga, scalar=1.0, in1=BK[h][:, 0:HALF], op0=ALU.add, op1=ALU.mult)
                    link(dve.scalar_tensor_tensor(out=gb, in0=gb, scalar=1.0, in1=BK[2 + h][:, 0:HALF], op0=ALU.add, op1=ALU.mult))
                    dve.tensor_tensor(ga, ga, gb, ALU.add).then_inc(mix_ok, 1)
                    dve.wait_ge(mx_hi, 2 * j + h + 1)
                    dve.tensor_tensor(ML[:, j, cs], ga, f32(MH[:, j, cs]), ALU.subtract).then_inc(mx_lo, 1)
                n += 2
                split_lo(n, n // 2 % 2, n % 2, n % 2)
            def residual(u):
                kk, r = u // 5, u % 5
                n = P if r < 4 else NSR
                dve.wait_ge(fr_pe, u + 1)
                if u == 0:
                    dve.wait_ge(fx_ld, 16 * 5)
                hx = FX[0:n, r, 512 * kk:512 * kk + 512]
                dve.scalar_tensor_tensor(out=hx, in0=BK[4 + u % 4][0:n, :], scalar=0.25, in1=hx, op0=ALU.mult, op1=ALU.add).then_inc(h_ok, 1)

            for j in range(N_OUT):
                n = N_IN + N_MIX + j + 2
                if j == 4:
                    for u in range(5):
                        residual(u)
                if j + 2 < N_OUT:
                    split_lo(n, n // 2 % 2, n % 2, n % 2)
            for u in range(5, 10):
                residual(u)
            for r in range(5):
                n = P if r < 4 else NSR
                dve.wait_ge(fss_ok, r + 1)
                dve.tensor_scalar(MS[0:n, r:r + 1], SS[0:n, r:r + 1], 1.0 / DM, EPS, ALU.mult, ALU.add).then_inc(fms_ok, 1)
            dve.wait_ge(fg_ld, 16)
            for r in range(5):
                n = P if r < 4 else NSR
                dve.wait_ge(frs_ok, r + 1)
                dve.scalar_tensor_tensor(out=FX[0:n, r, :], in0=FX[0:n, r, :], scalar=RSTD[0:n, r:r + 1], in1=FG[0:n], op0=ALU.mult,
                                         op1=ALU.mult).then_inc(fy_ok, 1)

        @block.gpsimd
        def _(pool):
            def f32(t):
                return t.bitcast(F32)

            pool.wait_ge(zero_ok, 4)
            for r in range(5):
                n = P if r < 4 else NSR
                pool.wait_ge(ms_ok, r + 1)
                pool.tensor_tensor(RSTD[0:n, r:r + 1], MS[0:n, r:r + 1], NHALF[0:n], ALU.pow).then_inc(rstd_ok, 1)
            pool.wait_ge(tab_ok, 1)
            vec = VEC[:]
            pitch = NH * (P + VLEN)
            pool.dma_start(bass.AP(skew_d.tensor, skew_d.offset, [[P + VLEN, NH], [pitch + 1, P], [1, VLEN]]),
                           bass.AP(vec.tensor, vec.offset, [list(vec.ap[0]), [0, P], [1, VLEN]])).then_inc(vec_st, 16)
            def store_rows(n):
                pool.wait_ge(rs_ev, n - 4 + 1)
                to_p, to_s = ((k_p, k_s), (v_p, v_s))[n // 4 - 1]
                cols = slice(n % 4 * P, (n % 4 + 1) * P)
                pool.dma_start(to_p[0, 0].rearrange("(r p) h d -> p r (h d)", p=P)[:, :, cols], RS[:, n % 4]).then_inc(rs_st[n % 4], 16)
                pool.dma_start(to_s[0].rearrange("b t h d -> (b t) (h d)")[:, cols], RSS[:, n % 4]).then_inc(rs_st[n % 4], 16)

            for n in range(N_QKV):
                c = n % 4
                if n < 8:
                    pool.wait_ge(pj_ev, 2 * n + 2)
                    pool.dma_start((q_d, k_d)[n // 4][c], TS[:, n % 4, 0:SEQ]).then_inc(ts_st[n % 4], 16)
                if n >= 5:
                    store_rows(n - 1)
            store_rows(N_QKV - 1)
            pool.wait_ge(smp_ok, 4)

            def place_q(b):
                qc = QC[:]
                out = bass.AP(qc.tensor, qc.offset, [list(qc.ap[0]), [64 + 8, PAIRS], [32, 2], [1, 8]])
                pool.tensor_copy(out, Q16[:, :, bass.ds(b, 1), :].rearrange("p c a (w x) -> p c (a w) x", w=2)).then_inc(qc_ok, 1)

            place_q(0)

            def value_lo(b, p):
                pool.wait_ge(vh, 16 * b + p + 1)
                pool.tensor_tensor(VL[:, p % 2, :], VRAW[:, p // 4 % 2, p % 4, :], f32(VH[:, p % 2, :]), ALU.subtract).then_inc(vl, 1)

            def sample(b, pv):
                if pv:
                    for p in range(1, NPG):
                        value_lo(b - 1, p)
                if not (isinstance(b, int) and b == NB - 1):
                    pool.wait_ge(loc_pe, b + 1)
                    place_q(b + 1)
                value_lo(b, 0)

            sample(0, False)
            with pool.Fori(1, NB - 1) as b:
                sample(b, True)
            sample(NB - 1, True)

            def stage_lo(hd, what):
                c, e = hd // 2, hd % 2
                rr = slice(e * HD, (e + 1) * HD)
                pool.wait_ge(stg_hi, 3 * hd + what + 1)
                wait(pool, stg_lo, 3 * hd + what)
                pool.wait_ge(vl, values_done[0])
                if what == 0:
                    pool.tensor_tensor(QLS[rr, :], PQ[rr, c, :], f32(QHS[rr, :]), ALU.subtract).then_inc(stg_lo, 1)
                elif what == 1:
                    pool.tensor_tensor(KLS[rr, :], PK[rr, c, :], f32(KHS[rr, :]), ALU.subtract).then_inc(stg_lo, 1)
                else:
                    pool.tensor_tensor(VPL[:, :, e, rr], PVB[:, c % 2, :, rr], f32(VPH[:, :, e, rr]), ALU.subtract).then_inc(stg_lo, 1)

            values_done, stages_done = [16 * (NB - 1) + 1], [6]
            pool.wait_ge(pj, 2 * N_IN)
            pool.memset(f32(VPL[:]), 0.0).then_inc(pchain, 1)
            pool.memset(f32(VPH[:]), 0.0).then_inc(zero_ok, 1)
            pool.wait_ge(pchain, 1)
            for hd in range(2):
                for what in range(3):
                    stage_lo(hd, what)
            for v in range(-1, 4 * NH):
                if 1 <= v + 2 < NPG:
                    pool.wait_ge(stg_lo, stages_done[0])
                    value_lo(NB - 1, v + 2)
                    values_done[0] += 1
                i, nxt = v % 4, v // 4 + 1
                if v >= 0 and 2 <= nxt < NH:
                    if i == 0:
                        stage_lo(nxt, 0)
                        stage_lo(nxt, 1)
                        stages_done[0] += 2
                    if i == 1:
                        stage_lo(nxt, 2)
                        stages_done[0] += 1

            def inverse_root(ready, done):
                for r in range(5):
                    n = P if r < 4 else NSR
                    pool.wait_ge(ready, r + 1)
                    wait(pool, done, r)
                    pool.tensor_tensor(RSTD[0:n, r:r + 1], MS[0:n, r:r + 1], NHALF[0:n], ALU.pow).then_inc(done, 1)

            inverse_root(var_ok, vrs_ok)
            pool.wait_ge(vn_ok, 5)
            pool.dma_start(sgu_s.rearrange("a b t d -> (a b t) d"), VNS[:]).then_inc(sgu_st, 16)
            inverse_root(fms_ok, frs_ok)


_INS = ["x_prompt", "x_sample", "cache_k", "cache_v", "page_table", "rel_bias", "norm_g", "w_in", "sgu_ln_g", "sgu_ln_b",
        "w_s", "b_s", "w_pa", "w_pb", "w_o", "final_norm_g"]
_OUTS = [(1, SEQ, DM), (NB, TD, DM), (1, 1, SEQ, NH, HD), (1, 1, SEQ, NH, HD), (1, NB, TD, NH, HD), (1, NB, TD, NH, HD), (1, NB, TD, DA)]


def kernel(**inputs):
    import concourse.bacc as _bacc
    from concourse.bass_utils import run_bass_kernel_spmd as _run

    nc = _bacc.Bacc("TRN2", target_bir_lowering=False, num_devices=1)
    arrays, args = {}, []
    named = [(n, np.ascontiguousarray(inputs[n])) for n in _INS]
    named += list(zip(("constants", "setup_constants", "gating_constants"), constants()))
    for name, a in named:
        arrays[f"in_{name}"] = a
        args.append(nc.dram_tensor(f"in_{name}", a.shape, mybir.dt.from_np(a.dtype), kind="ExternalInput").ap())
    for i, shape in enumerate(_OUTS):
        args.append(nc.dram_tensor(f"out_{i}", shape, F32, kind="ExternalOutput").ap())
    build(nc, *args)
    r = _run(nc, [arrays], core_ids=[0])
    return tuple(r.results[0][f"out_{i}"] for i in range(len(_OUTS)))
```

```python
import math
from contextlib import ExitStack

import numpy as np

import concourse.bass as bass
from concourse import mybir

F32 = mybir.dt.float32
F32R = mybir.dt.float32r
I32 = mybir.dt.int32
ALU = mybir.AluOpType
ACT = mybir.ActivationFunctionType
AX = mybir.AxisListType

P = 128
DM = 1024
SEQ = 512
NB = 8
TD = 4
NSR = NB * TD
ROWS = SEQ + NSR
HALF = ROWS // 2
KC = DM // P
NH = 8
HD = 64
DA = NH * HD
PAIRS = DA // P
PAST = 2048
PG = 128
NPG = PAST // PG
NBLK = 8
TOPK = 3
NBUCK = 32
MAXD = 128
EPS = 1e-6
LN_EPS = 1e-5
UNIT = 8.0
NEG = -1e30
N_IN = 44
N_QKV = 12
PER = 4
N_MIX = 8
N_OUT = 8
N_TILES = N_IN + N_MIX + N_OUT
GA, GU, GV, GB, GMA, GMB = 0, 4, 8, 12, 16, 24
GELU_C = math.sqrt(2.0 / math.pi)
VLEN = 384


def bucket(d):
    d = max(int(d), 0)
    if d < NBUCK // 2:
        return d
    half = NBUCK // 2
    return min(half + int(math.log(d / half) / math.log(MAXD / half) * (NBUCK - half)), NBUCK - 1)


def onehot(dists):
    e = np.zeros((NBUCK, len(dists)), np.float32)
    for n, d in enumerate(dists):
        e[bucket(d), n] += UNIT
        e[NBUCK - 1, n] -= UNIT
    return e


C_ID, C_OSEL, C_TRI = 0, 128, 160
C_COLS = 224
I_E15, I_ELOC, I_EVEC, I_VMASK, I_LOCM = 0, 512, 640, 1024, 1408
I_COLS = 1664
T_TRIL, T_REP, T_DIAG = 0, 128, 160
T_COLS = 192
GATE_STEPS = ([(kind, g0 + x) for g0 in (GV, GU) for kind in ("square", "gelu") for x in (0, 2)]
              + [("silu", g0 + x) for g0 in (GB, GA) for x in (0, 2)])


FILL = [2] * 8 + [1] * 8
HALVES_DONE = {p: [h for h in range(8) if sum(FILL[:p]) < 8 * (h + 1) <= sum(FILL[:p + 1])] for p in range(16)}
REST = 64 - sum(FILL)
HALVES_IN_PAGES = sum(len(h) for h in HALVES_DONE.values())


def constants():
    c = np.zeros((P, C_COLS), np.float32)
    c[:, C_ID:C_ID + P] = np.eye(P)
    row, col = np.arange(P)[:, None], np.arange(P)[None, :]
    c[64:128, C_OSEL:C_OSEL + 32] = row[64:128] % 32 == col[:, 0:32]
    c[:, C_TRI:C_TRI + 64] = (np.arange(8)[None, :] < np.arange(8)[:, None]).reshape(1, 64)
    i = np.zeros((NBUCK, I_COLS), np.float32)
    for t in range(TD):
        i[:, I_E15 + t * P:I_E15 + (t + 1) * P] = onehot([P + t - j for j in range(P)])
        i[:, I_ELOC + t * 32:I_ELOC + (t + 1) * 32] = onehot([t - j for _ in range(NB) for j in range(TD)])
    i[:, I_EVEC:I_EVEC + VLEN] = onehot([255 - u for u in range(VLEN)])
    i[:, I_VMASK:I_VMASK + VLEN] = np.where(np.arange(VLEN) > 255, NEG, 0.0)
    m = np.full((NH, TD, NB, NB, TD), NEG, np.float32)
    for b in range(NB):
        for t in range(TD):
            m[:, t, b, b, :t + 1] = 0.0
    i[:, I_LOCM:I_LOCM + 256] = m.reshape(32, 256)
    s = np.zeros((P, T_COLS), np.float32)
    s[:, T_TRIL:T_TRIL + P] = row <= col
    s[:, T_REP:T_REP + 32] = row == np.arange(32)[None, :] % TD
    s[0:32, T_DIAG:T_DIAG + 32] = np.arange(32)[:, None] // TD == np.arange(32)[None, :] // TD
    return c, i, s


def build(nc, x_p, x_s, cache_k, cache_v, page_table, rel_bias, norm_g, w_in, ln_g, ln_b, w_s, b_s, w_pa, w_pb,
          w_o, fin_g, cst, ini, sgc, y_p, y_s, k_p, v_p, k_s, v_s, sgu_s):
    with ExitStack() as ctx:
        base = (nc.sbuf_base + 31) // 32 * 32
        top = [base]

        def at(name, shape, dt, offset):
            t = nc.alloc_sbuf_tensor_at(name, shape, dt, offset=offset)
            return t

        def sb(name, shape, dt=F32):
            size = 4 * int(np.prod(shape[1:]))
            off = top[0]
            top[0] += (size + 31) // 32 * 32
            return at(name, shape, dt, off)

        def mark():
            return top[0]

        def sem(name):
            return ctx.enter_context(nc.semaphore(name))

        x_at = mark()
        XH = sb("XH", [P, KC, ROWS], F32R)
        XL = sb("XL", [P, KC, ROWS], F32R)
        WRAW = sb("WRAW", [P, 2, KC, 2 * P])
        WH = sb("WH", [P, 2, KC, P], F32R)
        WL = sb("WL", [P, 2, KC, P], F32R)
        kv_at = mark()
        KRAW = sb("KRAW", [P, 2, 4, DA])
        VRAW = sb("VRAW", [P, 2, 2, DA])
        KTH = sb("KTH", [P, 2, DA], F32R)
        KTL = sb("KTL", [P, 2, DA], F32R)
        VH = sb("VH", [P, 2, DA], F32R)
        VL = sb("VL", [P, 2, DA], F32R)
        g_at = mark()
        G = sb("G", [P, 32, ROWS])
        CST = sb("CST", [P, C_COLS])
        PTB = sb("PTB", [1, NB * NPG], I32)
        B15 = sb("B15", [32, P])
        LM = sb("LM", [32, NB, 32])
        Q16 = sb("Q16", [P, PAIRS, NB, 16], F32R)
        QC = sb("QC", [P, PAIRS, 2, 32], F32R)
        KSH = sb("KSH", [P, PAIRS, NSR], F32R)
        KSL = sb("KSL", [P, PAIRS, NSR], F32R)
        VSH = sb("VSH", [NSR, DA], F32R)
        OTS = at("OTS", [P, DA], F32, top[0] - 4 * DA)[64:128, :]
        VSL = sb("VSL", [NSR, DA], F32R)
        AO = at("AO", [P, SEQ], F32, top[0] - 4 * DA)[64:128, :]
        SC = sb("SC", [32, NPG * P + 32])
        o = top[0] - 4 * (NPG * P + 32)
        QKH = at("QKH", [P, 2, SEQ], F32R, o)[64:128]
        QKR = at("QKR", [P, 2, SEQ], F32, o + 8 * SEQ)[64:128]
        QKL = at("QKL", [P, 2, SEQ], F32R, o + 8 * SEQ)[64:128]
        AVH = sb("AVH", [P, 4, HD], F32R)
        AVR = sb("AVR", [P, 4, HD])
        AVL = at("AVL", [P, 4, HD], F32R, top[0] - 4 * 4 * HD)
        TPH = sb("TPH", [P, 2 * P])
        APX = sb("APX", [P, SEQ])
        APH = at("APH", [P, SEQ], F32R, top[0] - 4 * SEQ)
        APL = sb("APL", [P, SEQ], F32R)
        PT = sb("PT", [P, NPG, 64], F32R)
        PTL = sb("PTL", [32, 64], F32R)
        ATS = sb("ATS", [P, PAIRS, NSR])
        KSUM = sb("KSUM", [32, NPG])
        PMX = sb("PMX", [32, NPG])
        GATE = sb("GATE", [32, 8])
        CM1 = sb("CM1", [32, 8, 8])
        CM2 = sb("CM2", [32, 8, 8])
        RANK = sb("RANK", [32, 8])
        SEL = sb("SEL", [32, 8])
        BMX = sb("BMX", [32, 9])
        M1 = sb("M1", [32, 1])
        NEGM = sb("NEGM", [32, 1])
        EB = sb("EB", [32, 8])
        LSUM = sb("LSUM", [32, 9])
        LT = sb("LT", [32, 1])
        RL = sb("RL", [64, 1])
        SS = sb("SS", [P, 8])
        MS = sb("MS", [P, 8])
        RSTD = sb("RSTD", [P, 8])
        NHALF = sb("NHALF", [P, 1])
        NMX = sb("NMX", [P, 4])
        PLS = sb("PLS", [P, 4])
        assert top[0] <= nc.sbuf_usable_end, (top[0], nc.sbuf_usable_end)

        o = g_at
        XR = at("XR", [P, 5, DM], F32, o); o += 5 * DM * 4
        GBC = at("GBC", [P, DM], F32, o); o += DM * 4
        JUNK = at("JUNK", [P, DM], F32, o); o += DM * 4
        TS = at("TS", [P, 4, ROWS], F32, o); o += 4 * ROWS * 4
        RS = at("RS", [P, 4, 4, P], F32, o); o += 4 * 4 * P * 4
        RSS = at("RSS", [NSR, 4, P], F32, o); o += 4 * P * 4
        INI = at("INI", [NBUCK, I_COLS], F32, o); o += I_COLS * 4
        TAB = at("TAB", [NBUCK, NH], F32, o); o += NH * 4
        TB = at("TB", [NBUCK, TD, 32], F32, o); o += TD * 32 * 4
        VEC = at("VEC", [NH, VLEN], F32, o); o += VLEN * 4
        assert o <= g_at + 32 * ROWS * 4
        GT = at("GT", [P, 2, 2, ROWS], F32, x_at)
        AT = at("AT", [P, PAIRS, SEQ], F32, x_at + 17408)
        BSB = at("BSB", [P, PAIRS, P], F32, x_at + 32768)
        o = kv_at + 16384
        WSR = at("WSR", [P, NH, P], F32, o); o += 4096
        LNG = at("LNG", [P, DA], F32, o); o += 2048
        LNB = at("LNB", [P, DA], F32, o); o += 2048
        WST = at("WST", [P, NH, P], F32, o); o += 4096
        SGC = at("SGC", [P, T_COLS], F32, o); o += T_COLS * 4
        assert o <= kv_at + 32768
        o = kv_at
        VN = at("VN", [P, 4, DA], F32, o); o += 8192
        VNS = at("VNS", [NSR, DA], F32, o); o += 2048
        TZ = at("TZ", [P, 2, PAIRS, P], F32, o); o += 4096
        WSB = at("WSB", [NSR, NH, NSR], F32, o); o += 1024
        BST = at("BST", [P, 2, 8], F32, o); o += 64
        assert o <= kv_at + 16384
        MH = at("MH", [P, KC, ROWS], F32R, kv_at)
        ML = at("ML", [P, KC, ROWS], F32R, kv_at + 17408)
        o = g_at + 8 * ROWS * 4
        FX = at("FX", [P, 5, DM], F32, o); o += 5 * DM * 4
        FG = at("FG", [P, DM], F32, o); o += DM * 4
        FJ = at("FJ", [P, DM], F32, o); o += DM * 4
        assert o <= g_at + 32 * ROWS * 4

        BK = [ctx.enter_context(nc.psum_tensor(f"BK{i}", [P, 512], F32)) for i in range(8)]
        KTP = [BK[2], BK[3]]
        SCB = [BK[4], BK[5]]
        PTP = BK[6][:].rearrange("p (g x) -> p g x", g=NPG)
        OUT = BK[7][0:64, :]
        OTP = BK[7][:, 0:32].rearrange("p (c x) -> p c x", c=PAIRS)
        LOC = BK[7][0:32, 64:96]
        PTLP = BK[7][0:32, 96:128]

        IDN = CST[:, C_ID:C_ID + P]
        OSEL = CST[64:128, C_OSEL:C_OSEL + 32].rearrange("p (c x) -> p c x", c=PAIRS)
        TRI = CST[0:32, C_TRI:C_TRI + 64].rearrange("p (n m) -> p n m", n=8)

        q_d = nc.dram_tensor("q_scratch", [NH, HD, SEQ], F32, kind="Internal").ap()
        k_d = nc.dram_tensor("k_scratch", [NH, HD, SEQ], F32, kind="Internal").ap()
        attn_d = nc.dram_tensor("attn_scratch", [NH, HD, SEQ], F32, kind="Internal").ap()
        skew_d = nc.dram_tensor("skew_scratch", [P, NH, P + VLEN], F32, kind="Internal").ap()

        x_ld = [sem(f"x_ld{r}") for r in range(5)]
        cst_ld, ini_ld, pt_ld, gbc_ld = sem("cst_ld"), sem("ini_ld"), sem("pt_ld"), sem("gbc_ld")
        w_ld = [sem("w_ld0"), sem("w_ld1")]
        k_ld = [sem("k_ld0"), sem("k_ld1")]
        v_ld = [sem("v_ld0"), sem("v_ld1")]
        ss_ok, ms_ok, rstd_ok, xn_ok = sem("ss_ok"), sem("ms_ok"), sem("rstd_ok"), sem("xn_ok")
        xt_pe, xt_hi, xt_lo = sem("xt_pe"), sem("xt_hi"), sem("xt_lo")
        tb_ok, tab_pe, tab_ok, vec_st = sem("tb_ok"), sem("tab_pe"), sem("tab_ok"), sem("vec_st")
        w_hi, w_lo, pj, pj_ev = sem("w_hi"), sem("w_lo"), sem("pj"), sem("pj_ev")
        rows_pe, rs_ev, smp_ok = sem("rows_pe"), sem("rs_ev"), sem("smp_ok")
        ts_st = [sem(f"ts_st{i}") for i in range(4)]
        rs_st = [sem(f"rs_st{i}") for i in range(4)]
        kt_pe, kth, ktl, qk_pe = sem("kt_pe"), sem("kth"), sem("ktl"), sem("qk_pe")
        vh, vl, pv_pe = sem("vh"), sem("vl"), sem("pv_pe")
        qc_ok, loc_pe, sc_ok, eb_ok, ex_ok = sem("qc_ok"), sem("loc_pe"), sem("sc_ok"), sem("eb_ok"), sem("ex_ok")
        ptt_pe, pth_ok, ptl_ok = sem("ptt_pe"), sem("pth_ok"), sem("ptl_ok")
        ots_ok, ot_ev = sem("ots_ok"), sem("ot_ev")
        dchain, pchain, zero_ok = sem("dchain"), sem("pchain"), sem("zero_ok")
        at_ld, qk_ld, av_ld, tp_ld, sgw_ld, ln_ld, bs_ld = (sem(n) for n in ("at_ld", "qk_ld", "av_ld", "tp_ld", "sgw_ld", "ln_ld", "bs_ld"))
        stg_hi, stg_lo = sem("stg_hi"), sem("stg_lo")
        aq_pe, am_ok, ae_ok, ap_ok, at_pe, ath_ok, atl_ok, av_pe, ao_ok = (sem(n) for n in (
            "aq_pe", "am_ok", "ae_ok", "ap_ok", "at_pe", "ath_ok", "atl_ok", "av_pe", "ao_ok"))
        ao_st = sem("ao_st")
        el_act, el_dve, m_ok, y_ok = sem("el_act"), sem("el_dve"), sem("m_ok"), sem("y_ok")
        wst_pe, wst_ok, wsb_pe, wsb_ok = sem("wst_pe"), sem("wst_ok"), sem("wsb_pe"), sem("wsb_ok")
        vr_pe, var_ok, vrs_ok, vn_ok, sgu_st = sem("vr_pe"), sem("var_ok"), sem("vrs_ok"), sem("vn_ok"), sem("sgu_st")
        z_pe, z_ev, y_hi, y_lo = sem("z_pe"), sem("z_ev"), sem("y_hi"), sem("y_lo")
        mix_ok, mx_hi, mx_lo = sem("mix_ok"), sem("mx_hi"), sem("mx_lo")
        fx_ld, fg_ld, fr_pe, h_ok, fss_ok, fms_ok, frs_ok, fy_ok, y_st = (sem(n) for n in (
            "fx_ld", "fg_ld", "fr_pe", "h_ok", "fss_ok", "fms_ok", "frs_ok", "fy_ok", "y_st"))

        def wait(eng, s, v):
            if not isinstance(v, int) or v > 0:
                eng.wait_ge(s, v)

        def w_need(m):
            if not isinstance(m, int):
                return None
            return sum(32 if N_IN <= 2 * i < N_IN + N_MIX else 16 for i in range(m % 2, m + 1, 2))

        block = ctx.enter_context(nc.Block())

        def load_w(sp, m, slot, before):
            wait(sp, w_lo, before)
            if isinstance(m, int) and m >= N_IN // 2:
                if m < (N_IN + N_MIX) // 2:
                    c = (m - N_IN // 2) * 2 * P
                    for k0, src in ((0, w_pa), (4, w_pb)):
                        sp.dma_start(WRAW[:, slot, k0:k0 + 4, :],
                                     src[0, :, c:c + 2 * P].rearrange("(k p) n -> p k n", p=P)).then_inc(w_ld[slot], 16)
                else:
                    c = (m - (N_IN + N_MIX) // 2) * 2 * P
                    sp.dma_start(WRAW[:, slot], w_o[0, :, c:c + 2 * P].rearrange("(k p) n -> p k n", p=P)).then_inc(w_ld[slot], 16)
            else:
                sp.dma_start(WRAW[:, slot], w_in[0, :, bass.ds(m * 2 * P, 2 * P)].rearrange("(k p) n -> p k n", p=P)).then_inc(w_ld[slot], 16)

        @block.sync
        def _(sp):
            for r in range(5):
                if r < 4:
                    sp.dma_start(XR[:, r, :], x_p[0, r * P:(r + 1) * P, :]).then_inc(x_ld[r], 16)
                else:
                    sp.dma_start(XR[0:NSR, r, :], x_s.rearrange("b t d -> (b t) d")).then_inc(x_ld[r], 16)
                if r == 0:
                    sp.dma_start(GBC[:], bass.AP(norm_g.tensor, norm_g.offset, [[0, P], [1, DM]])).then_inc(gbc_ld, 16)
                    sp.dma_start(CST[:], cst).then_inc(cst_ld, 16)
                if r == 2:
                    load_w(sp, 0, 0, 0)
            load_w(sp, 1, 1, 0)
            sp.dma_start(PTB[:], page_table.rearrange("(a b) n -> a (b n)", a=1)).then_inc(pt_ld, 16)
            sp.dma_start(INI[:], ini).then_inc(ini_ld, 16)
            sp.dma_start(TAB[:], rel_bias).then_inc(ini_ld, 16)
            for m in range(2, N_QKV // 2 + 1):
                load_w(sp, m, m % 2, 2 * m - 2)
            sp.wait_ge(pt_ld, 16)
            k_regs = [sp.alloc_register(f"k_page{j}") for j in range(4)]
            v_regs = [sp.alloc_register(f"v_page{j}") for j in range(4)]

            def load_k(b, q):
                wait(sp, kt_pe, 16 * b + 4 * (q - 1))
                sp.load(k_regs, PTB[0:1, bass.ds(NPG * b + 4 * q, 4)])
                for j in range(4):
                    page = sp.snap(k_regs[j], min_val=0, max_val=cache_k.shape[1] - 1)
                    sp.dma_start(KRAW[:, q % 2, j, :], cache_k[0, bass.ds(page, 1)].rearrange("a p h d -> (a p) (h d)")).then_inc(k_ld[q % 2], 16)

            def load_v(b, q):
                sp.load(v_regs, PTB[0:1, bass.ds(NPG * b + 4 * q, 4)])
                for j in range(4):
                    if j % 2 == 0:
                        wait(sp, vl, 16 * b + 2 * (2 * q + j // 2 - 1))
                    page = sp.snap(v_regs[j], min_val=0, max_val=cache_v.shape[1] - 1)
                    sp.dma_start(VRAW[:, j // 2, j % 2, :], cache_v[0, bass.ds(page, 1)].rearrange("a p h d -> (a p) (h d)")).then_inc(v_ld[j // 2], 16)

            def store_head(a):
                sp.wait_ge(ao_ok, 4 * a + 4)
                sp.dma_start(attn_d[bass.ds(a, 1)].rearrange("a p n -> (a p) n"), AO).then_inc(ao_st, 16)

            def load_head(a):
                wait(sp, aq_pe, 4 * a)
                for x, src in enumerate((q_d, k_d)):
                    sp.dma_start(QKR[:, x, :], src[bass.ds(a, 1)].rearrange("a p n -> (a p) n")).then_inc(qk_ld, 16)
                wait(sp, am_ok, 4 * a)
                sp.dma_start(TPH[:], skew_d[:, bass.ds(a, 1), P - 1:P - 1 + 2 * P].rearrange("p a n -> p (a n)")).then_inc(tp_ld, 16)
                wait(sp, av_pe, 4 * a)
                sp.dma_start(AVR[:], v_p[0, 0].rearrange("(r p) h d -> p r h d", p=P)[:, :, bass.ds(a, 1), :].rearrange("p r a d -> p r (a d)")).then_inc(av_ld, 16)

            def sample(b, pv):
                for q in range(4):
                    if q:
                        load_k(b, q)
                    if pv and q:
                        load_v(b - 1, q)
                    if q == 0:
                        load_w(sp, 2 * b + 7, 1, 4 * b + 12)
                    if q == 2:
                        load_w(sp, 2 * b + 8, 0, 4 * b + 14)
                if not (isinstance(b, int) and b == NB - 1):
                    load_k(b + 1, 0)
                load_v(b, 0)
                if pv:
                    store_head(b - 1)
                else:
                    for i in range(4):
                        sp.wait_ge(ts_st[i], 16 * 2)
                        sp.wait_ge(rs_st[i], 32 * 2)
                    sp.wait_ge(vec_st, 16)
                load_head(b)

            load_k(0, 0)
            sample(0, False)
            sample(1, True)
            with sp.Fori(2, NB - 1) as b:
                sample(b, True)
            sample(NB - 1, True)
            for q in range(1, 4):
                load_v(NB - 1, q)
            sp.wait_ge(pj, 2 * N_IN)
            for e in range(2):
                sp.dma_start(BSB[e * HD:(e + 1) * HD], bass.AP(b_s.tensor, b_s.offset + e * P, [[0, HD], [2 * P, PAIRS], [1, P]])).then_inc(bs_ld, 16)
            sp.wait_ge(vl, 16 * NB)
            sp.dma_start(WSR[:], w_s[0].rearrange("g t s -> t g s")).then_inc(sgw_ld, 16)
            sp.dma_start(SGC[:], sgc).then_inc(sgw_ld, 16)
            sp.dma_start(LNG[:], bass.AP(ln_g.tensor, ln_g.offset, [[0, P], [1, DA]])).then_inc(ln_ld, 16)
            sp.dma_start(LNB[:], bass.AP(ln_b.tensor, ln_b.offset, [[0, P], [1, DA]])).then_inc(ln_ld, 16)
            store_head(NH - 1)
            sp.wait_ge(ao_st, 16 * NH)
            sp.dma_start(AT[:], attn_d.rearrange("(c e) p n -> (e p) c n", e=2)).then_inc(at_ld, 16)
            for m in range(23, N_TILES // 2):
                load_w(sp, m, m % 2, 2 * m - 2)
            sp.wait_ge(mx_lo, 2 * N_MIX)
            for r in range(4):
                sp.dma_start(FX[:, r, :], x_p[0, r * P:(r + 1) * P, :]).then_inc(fx_ld, 16)
            sp.dma_start(FX[0:NSR, 4, :], x_s.rearrange("b t d -> (b t) d")).then_inc(fx_ld, 16)
            sp.dma_start(FG[:], bass.AP(fin_g.tensor, fin_g.offset, [[0, P], [1, DM]])).then_inc(fg_ld, 16)
            for r in range(5):
                sp.wait_ge(fy_ok, r + 1)
                if r < 4:
                    sp.dma_start(y_p[0, r * P:(r + 1) * P, :], FX[:, r, :]).then_inc(y_st, 16)
                else:
                    sp.dma_start(y_s.rearrange("b t d -> (b t) d"), FX[0:NSR, 4, :]).then_inc(y_st, 16)
            sp.wait_ge(y_st, 16 * 5)
            sp.wait_ge(sgu_st, 16)

        @block.tensor
        def _(pe):
            mm = pe.matmul

            def half(n, par, h, XA=XH, XB=XL, read=None):
                if h == 0:
                    pe.wait_ge(w_lo, n + 1)
                wait(pe, pj_ev, 2 * n + h - 1 if read is None else read)
                cols = slice(h * HALF, (h + 1) * HALF)
                for k in range(KC):
                    for w, x in ((WH, XA), (WH, XB), (WL, XA)):
                        last = mm(BK[h][:, 0:HALF], w[:, par, k, :], x[:, k, cols], start=(k == 0 and w is WH and x is XA),
                                  stop=(k == KC - 1 and w is WL))
                    if k == KC - 1:
                        last.then_inc(pj, 1)
                    yield

            def run(g, steps=99):
                for _ in range(steps):
                    if next(g, 0) == 0:
                        break

            pe.wait_ge(cst_ld, 16)
            def turn_x(u):
                r, kk = u // 2, u % 2
                n = P if r < 4 else NSR
                wait(pe, xn_ok, r + 1)
                wait(pe, xt_lo, u - 3)
                for j in range(4):
                    k = 4 * kk + j
                    last = pe.transpose(BK[4 + u % 4][:, j * n:(j + 1) * n], XR[0:n, r, k * P:(k + 1) * P], IDN[0:n, 0:n])
                last.then_inc(xt_pe, 1)

            for u in range(6):
                turn_x(u)

            def rows(n):
                i = n - 4
                pe.wait_ge(pj_ev, 2 * n + 2)
                wait(pe, rs_ev, i - 1)
                bp, bs = BK[4 + 2 * (i % 2)], BK[5 + 2 * (i % 2)]
                for r in range(4):
                    pe.transpose(bp[:, r * P:(r + 1) * P], TS[:, n % 4, r * P:(r + 1) * P], IDN)
                pe.transpose(bs[0:NSR, 0:P], TS[:, n % 4, SEQ:ROWS], IDN).then_inc(rows_pe, 1)

            pe.wait_ge(xt_lo, 6)
            for n in range(N_QKV):
                first = half(n, n % 2, 0)
                if n == 0:
                    for u in range(6, 10):
                        run(first, 2 if u > 7 else 1)
                        turn_x(u)
                run(first)
                if n == 0:
                    pe.wait_ge(xt_lo, 10)
                if n == 1:
                    pe.wait_ge(tb_ok, 1)
                    for t in range(TD):
                        mm(BK[2][0:32, 0:P], TB[:, t, :], INI[:, I_E15 + t * P:I_E15 + (t + 1) * P], start=(t == 0), stop=(t == 3))
                    for t in range(TD):
                        mm(BK[3][0:32, 0:32], TB[:, t, :], INI[:, I_ELOC + t * 32:I_ELOC + (t + 1) * 32], start=(t == 0), stop=(t == 3))
                    mm(BK[3][0:NH, 64:64 + VLEN], TAB[:], INI[:, I_EVEC:I_EVEC + VLEN], start=True, stop=True).then_inc(tab_pe, 1)
                if n - 1 >= 4:
                    rows(n - 1)
                run(half(n, n % 2, 1))
            rows(N_QKV - 1)

            def turn_page(b, p):
                q, i = p // 4, 16 * b + p
                if p % 4 == 0:
                    pe.wait_ge(k_ld[q % 2], 64 * (2 * b + q // 2 + 1))
                wait(pe, ktl, i - 1)
                if isinstance(b, int) and b == 0 and p == 0:
                    pe.wait_ge(tab_ok, 1)
                for c in range(PAIRS):
                    last = pe.transpose(KTP[p % 2][:, c * P:(c + 1) * P], KRAW[:, q % 2, p % 4, c * P:(c + 1) * P], IDN)
                last.then_inc(kt_pe, 1)

            def scores(out, hi, lo):
                for c in range(PAIRS):
                    for w, x in ((0, hi), (0, lo), (1, hi)):
                        last = mm(out, QC[:, c, w, :], x[c], start=(c == 0 and w == 0 and x is hi), stop=(c == PAIRS - 1 and w == 1))
                return last

            def score_page(b, p):
                if p == 0:
                    pe.wait_ge(qc_ok, b + 1)
                    if isinstance(b, int) and b == 0:
                        pe.wait_ge(rs_ev, 8)
                        pe.wait_ge(smp_ok, 12)
                if p % 4 == 0:
                    wait(pe, sc_ok, 4 * b + p // 4 - 1)
                pe.wait_ge(ktl, 16 * b + p + 1)
                hi, lo = ([w[:, p % 2, c * P:(c + 1) * P] for c in range(PAIRS)] for w in (KTH, KTL))
                scores(SCB[p // 4 % 2][0:32, p % 4 * P:(p % 4 + 1) * P], hi, lo).then_inc(qk_pe, 1)

            def value_page(b, p):
                if p == 0:
                    pe.wait_ge(ptl_ok, b + 1)
                    mm(OUT, PTL[:], VSH[:], start=True, stop=False)
                    mm(OUT, PTL[:], VSL[:], start=False, stop=False)
                pe.wait_ge(vl, 16 * b + p + 1)
                mm(OUT, PT[:, p, :], VH[:, p % 2, :], start=False, stop=False)
                mm(OUT, PT[:, p, :], VL[:, p % 2, :], start=False, stop=(p == NPG - 1)).then_inc(pv_pe, 1)

            def turn_out():
                for c in range(PAIRS):
                    last = mm(OTP[:, c, :], OTS[:, c * P:(c + 1) * P], OSEL[:, c, :], start=True, stop=True, skip_group_check=True)
                return last

            def a_scores(a, p):
                i = p // 4
                if p % 4 == 0:
                    if i == 0:
                        pe.wait_ge(stg_lo, 2 * a + 1)
                        pe.wait_ge(ptl_ok, a + 1)
                    else:
                        pe.wait_ge(ao_ok, 4 * a + i)
                    n = (i + 1) * P
                    for w, x in ((QKH, QKH), (QKH, QKL), (QKL, QKH)):
                        last = mm(BK[6][:, 0:n], w[:, 0, i * P:(i + 1) * P], x[:, 1, 0:n], start=(w is QKH and x is QKH), stop=(w is QKL))
                    last.then_inc(aq_pe, 1)

            def a_turn(a, p):
                i = p // 4
                if p % 4 == 2:
                    pe.wait_ge(ap_ok, 4 * a + i + 1)
                    for j in range(i + 1):
                        last = pe.transpose(BK[6][:, j * P:(j + 1) * P], APX[:, j * P:(j + 1) * P], IDN)
                    last.then_inc(at_pe, 1)

            def a_values(a, p):
                i = p // 4
                if p % 4 == 3:
                    if i == 0:
                        pe.wait_ge(stg_lo, 2 * a + 2)
                    pe.wait_ge(atl_ok, 4 * a + i + 1)
                    for j in range(i + 1):
                        for w, x in ((AVH, APH), (AVH, APL), (AVL, APH)):
                            last = mm(BK[6][0:64, 0:P], w[:, j, :], x[:, j * P:(j + 1) * P], start=(j == 0 and w is AVH and x is APH),
                                      stop=(j == i and w is AVL))
                    last.then_inc(av_pe, 1)

            def sample(b, pv):
                n0 = N_QKV + PER * b
                steps_of = (step for j in range(PER) for h in range(2) for step in half(n0 + j, j % 2, h))

                def fill(steps):
                    run(steps_of, steps)

                for p in range(NPG):
                    turn_page(b, p)
                    if pv:
                        a_turn(b - 1, p)
                    fill(FILL[p])
                    if p:
                        score_page(b, p - 1)
                    if pv:
                        a_scores(b - 1, p)
                        a_values(b - 1, p)
                    if p == NPG - 1:
                        fill(1)
                        score_page(b, p)
                    if pv:
                        value_page(b - 1, p)
                fill(5)
                if pv:
                    pe.wait_ge(ots_ok, b)
                    turn_out()
                scores(LOC, [KSH[:, c, :] for c in range(PAIRS)], [KSL[:, c, :] for c in range(PAIRS)]).then_inc(loc_pe, 1)
                fill(REST - 16)
                pe.wait_ge(ex_ok, 2 * b + 1)
                if pv:
                    pe.wait_ge(ao_ok, 4 * b)
                fill(1)
                for p in range(8):
                    pe.transpose(PTP[:, p, :], SC[:, p * P:(p + 1) * P], IDN[0:32, 0:32])
                fill(2)
                pe.wait_ge(ex_ok, 2 * b + 2)
                fill(1)
                for p in range(8, NPG):
                    pe.transpose(PTP[:, p, :], SC[:, p * P:(p + 1) * P], IDN[0:32, 0:32])
                pe.transpose(PTLP, SC[:, NPG * P:NPG * P + 32], IDN[0:32, 0:32]).then_inc(ptt_pe, 1)
                fill(64)

            sample(0, False)
            with pe.Fori(1, NB) as b:
                sample(b, True)

            for p in range(NPG):
                a_turn(NH - 1, p)
                a_scores(NH - 1, p)
                a_values(NH - 1, p)
                value_page(NB - 1, p)
            pe.wait_ge(ots_ok, NB)
            turn_out().then_inc(loc_pe, 1)

            pe.wait_ge(sgw_ld, 32)
            for g in range(NH):
                last = pe.transpose(BK[g // 4][:, g % 4 * P:(g % 4 + 1) * P], WSR[:, g, :], IDN)
            last.then_inc(wst_pe, 1)
            pe.wait_ge(el_dve, 4)
            for r in range(5):
                n = P if r < 4 else NSR
                wait(pe, vn_ok, r - 1)
                for c in range(PAIRS):
                    last = pe.transpose(BK[2 + r % 2][0:n, c * P:(c + 1) * P], G[:, GV + c, r * P:r * P + n], IDN)
                last.then_inc(vr_pe, 1)
            pe.wait_ge(wst_ok, 1)
            rep = SGC[:, T_REP:T_REP + 32]
            mm(BK[4][0:32, 0:256], rep, bass.AP(WST[:].tensor, WST[:].offset, [list(WST[:].ap[0]), [P, NH], [0, NB], [1, TD]]), start=True, stop=True).then_inc(wsb_pe, 1)
            pe.wait_ge(ao_ok, 4 * NH)
            pe.wait_ge(ot_ev, NB)
            for r in range(4):
                pe.wait_ge(vn_ok, r + 1)
                wait(pe, z_ev, r - 1)
                for c in range(PAIRS):
                    bk = BK[(6, 0)[r % 2] + c // 2]
                    last = mm(bk[:, c % 2 * 256:c % 2 * 256 + 256], VN[:, r, c * P:(c + 1) * P], WST[:, 2 * c:2 * c + 2, :],
                              start=True, stop=True, skip_group_check=True)
                last.then_inc(z_pe, 1)
            pe.wait_ge(vn_ok, 5)
            pe.wait_ge(wsb_ok, 1)
            for c in range(PAIRS):
                last = mm(BK[5][:, c * 64:(c + 1) * 64], VNS[:, c * P:(c + 1) * P], WSB[:, 2 * c:2 * c + 2, :],
                          start=True, stop=True, skip_group_check=True)
            last.then_inc(z_pe, 1)

            pe.wait_ge(y_lo, 2)
            for j in range(N_MIX):
                n = N_IN + j
                pe.wait_ge(w_lo, n + 1)
                for h in range(2):
                    wait(pe, mix_ok, 2 * j + h - 1)
                    for br in range(2):
                        for k in range(4 * br, 4 * br + 4):
                            for w, x in ((WH, XH), (WH, XL), (WL, XH)):
                                last = mm(BK[h + 2 * br][:, 0:HALF], w[:, n % 2, k, :], x[:, k, h * HALF:(h + 1) * HALF],
                                          start=(k % 4 == 0 and w is WH and x is XH), stop=(k % 4 == 3 and w is WL))
                    last.then_inc(pj, 1)
            def out_rows(u):
                kk, r = u // 5, u % 5
                n = P if r < 4 else NSR
                wait(pe, h_ok, u - 3)
                for j in range(4):
                    last = pe.transpose(BK[4 + u % 4][0:n, j * P:(j + 1) * P], G[:, 4 * kk + j, r * P:r * P + n], IDN)
                last.then_inc(fr_pe, 1)

            pe.wait_ge(mx_lo, 2 * N_MIX)
            for j in range(N_OUT):
                n = N_IN + N_MIX + j
                run(half(n, n % 2, 0, MH, ML, 2 * (N_IN + j) - 1))
                if j == 4:
                    pe.wait_ge(pj_ev, 2 * (N_IN + j))
                    for u in range(5):
                        out_rows(u)
                run(half(n, n % 2, 1, MH, ML, 2 * (N_IN + j)))
            pe.wait_ge(pj_ev, 2 * (N_IN + N_OUT))
            for u in range(5, 10):
                out_rows(u)

        @block.scalar
        def _(act):
            def copy(o, i):
                return act.activation(o, i, ACT.Copy)

            def split_hi(n, slot, side, par, need):
                act.wait_ge(w_ld[slot], need)
                wait(act, pj, 2 * n - 2)
                copy(WH[:, par], WRAW[:, slot, :, side * P:(side + 1) * P]).then_inc(w_hi, 1)

            def squares(r):
                n = P if r < 4 else NSR
                act.wait_ge(x_ld[r], 16)
                if r:
                    act.wait_ge(ss_ok, r)
                act.activation(JUNK[0:n], XR[0:n, r, :], ACT.Square, accum_out=SS[0:n, r:r + 1]).then_inc(ss_ok, 1)

            def x_hi(r):
                n = P if r < 4 else NSR
                for kk in range(2):
                    u = 2 * r + kk
                    act.wait_ge(xt_pe, u + 1)
                    copy(XH[:, 4 * kk:4 * kk + 4, r * P:r * P + n], BK[4 + u % 4][:, 0:4 * n].rearrange("p (k n) -> p k n", k=4)).then_inc(xt_hi, 1)

            squares(0)
            squares(1)
            x_hi(0)
            squares(2)
            x_hi(1)
            split_hi(0, 0, 0, 0, w_need(0))
            x_hi(2)
            squares(3)
            squares(4)
            split_hi(1, 0, 1, 1, w_need(0))
            x_hi(3)
            x_hi(4)
            for n in range(N_QKV):
                for h in range(2):
                    act.wait_ge(pj, 2 * n + h + 1)
                    if h == 0 and n >= 4:
                        if n - 4 < 8:
                            act.wait_ge(ts_st[n % 4], 16 * ((n - 4) // 4 + 1))
                        wait(act, rows_pe, n - 4 - 4 + 1)
                        wait(act, smp_ok, min(n - 3, 8))
                    copy(TS[:, n % 4, h * HALF:(h + 1) * HALF], BK[h][:, 0:HALF]).then_inc(pj_ev, 1)
                m = (n + 2) // 2
                split_hi(n + 2, m % 2, n % 2, n % 2, w_need(m))

            def page_hi(b, p):
                i = 16 * b + p
                act.wait_ge(kt_pe, i + 1)
                wait(act, qk_pe, i - 1)
                copy(KTH[:, p % 2, :], KTP[p % 2][:]).then_inc(kth, 1)

            def a_out(a, i):
                act.wait_ge(av_pe, 4 * a + i + 1)
                if i == 0:
                    wait(act, ao_st, 16 * a)
                copy(AO[:, i * P:(i + 1) * P], BK[6][0:64, 0:P]).then_inc(ao_ok, 1)

            def a_step(a, p):
                i = p // 4
                n = (i + 1) * P
                if p % 4 == 0 and i:
                    a_out(a, i - 1)
                if p % 4 == 1:
                    act.wait_ge(am_ok, 4 * a + i + 1)
                    act.activation(APX[:, 0:n], BK[6][:, 0:n], ACT.Exp, bias=NMX[:, i:i + 1], scale=1.0 / UNIT,
                                   accum_out=PLS[:, i:i + 1]).then_inc(ae_ok, 1)
                if p % 4 == 2:
                    act.wait_ge(at_pe, 4 * a + i + 1)
                    copy(APH[:, 0:n], BK[6][:, 0:n]).then_inc(ath_ok, 1)

            def stage_hi(a):
                act.wait_ge(qk_ld, 32 * (a + 1))
                copy(QKH, QKR).then_inc(stg_hi, 1)
                act.wait_ge(av_ld, 16 * (a + 1))
                copy(AVH[:], AVR[:]).then_inc(stg_hi, 1)

            def page_scores(b, q):
                act.wait_ge(qk_pe, 16 * b + 4 * q + 4)
                if q == 0:
                    wait(act, ptt_pe, b)
                for p in range(4 * q, 4 * q + 4):
                    last = act.activation(SC[:, p * P:(p + 1) * P], SCB[q % 2][0:32, p % 4 * P:(p % 4 + 1) * P], ACT.Copy,
                                          accum_out=KSUM[:, p:p + 1])
                last.then_inc(sc_ok, 1)

            def evac(b, j, h):
                n = N_QKV + PER * b + j
                act.wait_ge(pj, 2 * n + h + 1)
                copy(G[:, bass.ds(PER * b + j, 1), h * HALF:(h + 1) * HALF].rearrange("p a n -> p (a n)"), BK[h][:, 0:HALF]).then_inc(pj_ev, 1)

            def split_loop(b, j):
                m2 = j // 2
                if isinstance(b, int) and b == NB - 1 and j >= 4:
                    need = w_need(N_IN // 2)
                else:
                    need = 16 * (b + 3 + m2)
                split_hi(N_QKV + PER * b + j, m2 % 2, j % 2, j % 2, need)

            def sample(b, pv):
                for p in range(NPG):
                    page_hi(b, p)
                    if pv and p == 0:
                        evac(b - 1, 3, 1)
                    if pv and p == 3:
                        split_loop(b - 1, 5)
                    if pv:
                        a_step(b - 1, p)
                    if isinstance(b, int) and b == 0 and p == 4:
                        for i in range(4):
                            act.wait_ge(ts_st[i], 32)
                            act.wait_ge(rs_st[i], 64)
                        act.wait_ge(rs_ev, 8)
                        act.wait_ge(smp_ok, 12)
                        act.wait_ge(tab_ok, 1)
                        act.wait_ge(vec_st, 16)
                    for h in HALVES_DONE.get(p - 1, ()):
                        evac(b, h // 2, h % 2)
                    if p == 10:
                        split_loop(b, 2)
                    if p in (5, 9, 13):
                        page_scores(b, (p - 5) // 4)
                page_scores(b, 3)
                if pv:
                    a_out(b - 1, 3)
                for h in HALVES_DONE[NPG - 1] + list(range(HALVES_IN_PAGES, 5)):
                    evac(b, h // 2, h % 2)
                    if h == 3:
                        split_loop(b, 3)
                stage_hi(b)
                act.wait_ge(eb_ok, b + 1)
                for n in range(8):
                    blk = SC[:, 2 * n * P:2 * (n + 1) * P]
                    e = act.activation(blk, blk, ACT.Exp, bias=EB[:, n:n + 1], scale=1.0 / UNIT, accum_out=LSUM[:, n:n + 1])
                    if n == 3:
                        e.then_inc(ex_ok, 1)
                loc = SC[:, NPG * P:NPG * P + 32]
                act.activation(loc, loc, ACT.Exp, bias=NEGM[:], scale=1.0 / UNIT, accum_out=LSUM[:, 8:9]).then_inc(ex_ok, 1)
                evac(b, 2, 1)
                split_loop(b, 4)
                act.wait_ge(ptt_pe, b + 1)
                copy(PT[:, :, 0:32], PTP)
                copy(PTL[:, 0:32], PTLP).then_inc(pth_ok, 1)
                evac(b, 3, 0)

            sample(0, False)
            with act.Fori(1, NB - 1) as b:
                sample(b, True)
            sample(NB - 1, True)

            def gate_step(s):
                kind, g0 = GATE_STEPS[s]
                gt = GT[:, s % 2]
                wait(act, el_dve, s - 1)
                if s == 0:
                    act.wait_ge(pj, 2 * N_IN)
                if kind == "square":
                    act.activation(gt, G[:, g0:g0 + 2, :], ACT.Square, scale=math.sqrt(0.044715)).then_inc(el_act, 1)
                elif kind == "gelu":
                    act.activation(gt, gt, ACT.Tanh, scale=GELU_C).then_inc(el_act, 1)
                else:
                    act.activation(gt, G[:, g0:g0 + 2, :], ACT.Tanh, scale=0.5).then_inc(el_act, 1)

            evac(NB - 1, 3, 1)
            split_loop(NB - 1, 5)
            for p in range(NPG):
                a_step(NH - 1, p)
                if p < len(GATE_STEPS):
                    gate_step(p)
            a_out(NH - 1, 3)
            for v in range(8):
                g0 = GMA + v * 2
                act.activation(G[:, g0:g0 + 2, :], G[:, g0:g0 + 2, :], ACT.Tanh, scale=0.5).then_inc(m_ok, 1)
            act.wait_ge(y_ok, 1)
            copy(XH[:, 0:4, :], G[:, GA:GA + 4, :]).then_inc(y_hi, 1)
            act.wait_ge(y_ok, 2)
            copy(XH[:, 4:8, :], G[:, GB:GB + 4, :]).then_inc(y_hi, 1)
            act.wait_ge(sgu_st, 16)
            for j in range(N_MIX):
                for h in range(2):
                    act.wait_ge(mix_ok, 2 * j + h + 1)
                    copy(MH[:, j, h * HALF:(h + 1) * HALF], G[:, GMA + j, h * HALF:(h + 1) * HALF]).then_inc(mx_hi, 1)
                n = N_IN + j + 2
                split_hi(n, n // 2 % 2, n % 2, n % 2, w_need(n // 2))
            for j in range(N_OUT):
                n = N_IN + N_MIX + j
                for h in range(2):
                    act.wait_ge(pj, 2 * n + h + 1)
                    copy(G[:, j, h * HALF:(h + 1) * HALF], BK[h][:, 0:HALF]).then_inc(pj_ev, 1)
                if j + 2 < N_OUT:
                    split_hi(n + 2, (n + 2) // 2 % 2, n % 2, n % 2, w_need((n + 2) // 2))
            for r in range(5):
                n = P if r < 4 else NSR
                act.wait_ge(h_ok, 5 + r + 1)
                if r:
                    act.wait_ge(fss_ok, r)
                act.activation(FJ[0:n], FX[0:n, r, :], ACT.Square, accum_out=SS[0:n, r:r + 1]).then_inc(fss_ok, 1)

        @block.vector
        def _(dve):
            chain, loop_links, first_links = [0], [0], [0]

            def link(ins, b=None):
                ins.then_inc(dchain, 1)
                chain[0] += 1
                dve.wait_ge(dchain, chain[0] if b is None else (b - 1) * loop_links[0] + chain[0])

            def f32(t):
                return t.bitcast(F32)

            def split_lo(n, slot, side, par):
                dve.wait_ge(w_hi, n + 1)
                dve.tensor_tensor(WL[:, par], WRAW[:, slot, :, side * P:(side + 1) * P], f32(WH[:, par]), ALU.subtract).then_inc(w_lo, 1)

            dve.memset(TB[:], 0.0).then_inc(zero_ok, 1)
            dve.memset(NHALF[:], -0.5).then_inc(zero_ok, 1)
            dve.memset(Q16[:].bitcast(F32), 0.0).then_inc(zero_ok, 1)
            dve.memset(QC[:].bitcast(F32), 0.0).then_inc(zero_ok, 1)
            dve.wait_ge(zero_ok, 4)
            def mean_square(r):
                n = P if r < 4 else NSR
                dve.wait_ge(ss_ok, r + 1)
                dve.tensor_scalar(MS[0:n, r:r + 1], SS[0:n, r:r + 1], 1.0 / DM, EPS, ALU.mult, ALU.add).then_inc(ms_ok, 1)

            def normalise(r):
                n = P if r < 4 else NSR
                if r == 0:
                    dve.wait_ge(gbc_ld, 16)
                dve.wait_ge(rstd_ok, r + 1)
                dve.scalar_tensor_tensor(out=XR[0:n, r, :], in0=XR[0:n, r, :], scalar=RSTD[0:n, r:r + 1], in1=GBC[0:n], op0=ALU.mult,
                                         op1=ALU.mult).then_inc(xn_ok, 1)

            def x_lo(r):
                n = P if r < 4 else NSR
                for kk in range(2):
                    u = 2 * r + kk
                    dve.wait_ge(xt_hi, u + 1)
                    dst = slice(r * P, r * P + n)
                    dve.tensor_tensor(XL[:, 4 * kk:4 * kk + 4, dst], BK[4 + u % 4][:, 0:4 * n].rearrange("p (k n) -> p k n", k=4),
                                      f32(XH[:, 4 * kk:4 * kk + 4, dst]), ALU.subtract).then_inc(xt_lo, 1)

            for r in range(3):
                mean_square(r)
                if r == 2:
                    x_lo(0)
                normalise(r)
            x_lo(1)
            x_lo(2)
            for r in range(3, 5):
                mean_square(r)
                normalise(r)
            x_lo(3)
            x_lo(4)
            dve.wait_ge(ini_ld, 32)
            for t in range(TD):
                last = dve.tensor_copy(TB[:, t, t:t + 29:4], TAB[:])
            last.then_inc(tb_ok, 1)
            dve.wait_ge(tab_pe, 1)
            dve.tensor_copy(B15[:], BK[2][0:32, 0:P])
            lmo = LM[:]
            src = BK[3][0:32, 0:32]
            dve.tensor_tensor(lmo, bass.AP(src.tensor, src.offset, [list(src.ap[0]), [0, NB], [1, 32]]),
                              INI[:, I_LOCM:I_LOCM + 256].rearrange("p (b n) -> p b n", b=NB), ALU.add)
            dve.tensor_tensor(VEC[:], BK[3][0:NH, 64:64 + VLEN], INI[0:NH, I_VMASK:I_VMASK + VLEN], ALU.add).then_inc(tab_ok, 1)

            def rows_out(n):
                i, c = n - 4, n % 4
                bp, bs = BK[4 + 2 * (i % 2)], BK[5 + 2 * (i % 2)]
                dve.wait_ge(rows_pe, i + 1)
                wait(dve, rs_st[n % 4], 32 * (i // 4))
                dve.tensor_copy(RS[:, n % 4], bp[:].rearrange("p (r n) -> p r n", r=4))
                link(dve.tensor_copy(RSS[:, n % 4], bs[0:NSR, 0:P]))
                dve.sem_inc(rs_ev, 1)
                if n >= 8:
                    vc = slice(c * P, (c + 1) * P)
                    link(dve.tensor_copy(VSH[:, vc], RSS[:, n % 4]))
                    dve.tensor_tensor(VSL[:, vc], RSS[:, n % 4], f32(VSH[:, vc]), ALU.subtract).then_inc(smp_ok, 1)

            for n in range(N_QKV):
                c = n % 4
                if n < 8:
                    dve.wait_ge(pj_ev, 2 * n + 2)
                    smp = TS[:, n % 4, SEQ:ROWS]
                    if n < 4:
                        for e in range(2):
                            rr = slice(e * HD, (e + 1) * HD)
                            sv = TS[rr, n % 4, SEQ:ROWS].rearrange("p (b t) -> p b t", t=TD)
                            link(dve.tensor_copy(Q16[rr, c, :, 4 * e:4 * e + 4], sv))
                            last = dve.tensor_tensor(Q16[rr, c, :, 8 + 4 * e:12 + 4 * e], sv, f32(Q16[rr, c, :, 4 * e:4 * e + 4]), ALU.subtract)
                        last.then_inc(smp_ok, 1)
                    else:
                        link(dve.tensor_copy(KSH[:, c, :], smp))
                        dve.tensor_tensor(KSL[:, c, :], smp, f32(KSH[:, c, :]), ALU.subtract).then_inc(smp_ok, 1)
                if n - 1 >= 4:
                    rows_out(n - 1)
                m = (n + 2) // 2
                split_lo(n + 2, m % 2, n % 2, n % 2)
            rows_out(N_QKV - 1)

            before_samples = chain[0]

            def page_lo(b, p):
                i = 16 * b + p
                dve.wait_ge(kth, i + 1)
                dve.tensor_tensor(KTL[:, p % 2, :], KTP[p % 2][:], f32(KTH[:, p % 2, :]), ALU.subtract).then_inc(ktl, 1)

            def value_hi(b, p):
                q, i = p // 2, 16 * b + p
                if p % 2 == 0:
                    dve.wait_ge(v_ld[q % 2], 32 * (4 * b + q // 2 + 1))
                wait(dve, pv_pe, i - 1)
                dve.tensor_copy(VH[:, p % 2, :], VRAW[:, q % 2, p % 2, :]).then_inc(vh, 1)

            def split_loop(b, j):
                m2 = j // 2
                split_lo(N_QKV + PER * b + j, m2 % 2, j % 2, j % 2)

            def a_step(a, p, lb=None):
                i = p // 4
                n = (i + 1) * P
                bk = BK[6]
                if p % 4 == 0:
                    dve.wait_ge(aq_pe, 4 * a + i + 1)
                    if i == 0:
                        dve.wait_ge(tp_ld, 16 * (a + 1))
                    w = min(n, 2 * P)
                    link(dve.tensor_tensor(bk[:, n - w:n], bk[:, n - w:n], TPH[:, 2 * P - w:2 * P], ALU.add), lb)
                    link(dve.tensor_reduce(NMX[:, i:i + 1], bk[:, 0:n], AX.X, ALU.max), lb)
                    dve.tensor_scalar(NMX[:, i:i + 1], NMX[:, i:i + 1], -1.0 / UNIT, None, ALU.mult).then_inc(am_ok, 1)
                if p % 4 == 1:
                    dve.wait_ge(ae_ok, 4 * a + i + 1)
                    link(dve.reciprocal(PLS[:, i:i + 1], PLS[:, i:i + 1]), lb)
                    dve.tensor_scalar(APX[:, 0:n], APX[:, 0:n], PLS[:, i:i + 1], None, ALU.mult).then_inc(ap_ok, 1)
                if p % 4 == 2:
                    dve.wait_ge(ath_ok, 4 * a + i + 1)
                    dve.tensor_tensor(APL[:, 0:n], bk[:, 0:n], f32(APH[:, 0:n]), ALU.subtract).then_inc(atl_ok, 1)

            def page_maxima(b, q, lb):
                dve.wait_ge(sc_ok, 4 * b + q + 1)
                if q == 3:
                    last_page = SC[:, (NPG - 1) * P:NPG * P]
                    link(dve.tensor_tensor(last_page, last_page, B15[:], ALU.add), lb)
                return dve.tensor_reduce(PMX[:, 4 * q:4 * q + 4], SC[:, 4 * q * P:4 * (q + 1) * P].rearrange("p (g n) -> p g n", g=4), AX.X, ALU.max)

            def scale_out(b):
                dve.wait_ge(pv_pe, 16 * (b + 1))
                dve.tensor_scalar(OTS, OUT, RL[:], None, ALU.mult).then_inc(ots_ok, 1)

            def out_sample(b):
                for e in range(2):
                    rr = slice(e * HD, (e + 1) * HD)
                    last = dve.tensor_copy(ATS[rr, :, bass.ds(TD * b, TD)], OTP[rr, :, 4 * e:4 * e + 4])
                last.then_inc(ot_ev, 1)

            def sample(b, pv):
                lb = None if isinstance(b, int) and b == 0 else b
                if lb is not None:
                    chain[0] = first_links[0]
                for p in range(NPG):
                    page_lo(b, p)
                    if pv and p + 1 < NPG:
                        value_hi(b - 1, p + 1)
                    if pv:
                        a_step(b - 1, p, lb)
                        if p == 3:
                            split_loop(b - 1, 5)
                    if p == 11:
                        split_loop(b, 2)
                    if p in (7, 10, 15):
                        page_maxima(b, (p - 6) // 4, lb)
                if pv:
                    scale_out(b - 1)
                link(page_maxima(b, 3, lb), lb)
                dve.wait_ge(loc_pe, b + 1)
                loc = SC[:, NPG * P:NPG * P + 32]
                link(dve.tensor_tensor(loc, LOC, LM[:, bass.ds(b, 1), :].rearrange("p a n -> p (a n)"), ALU.add), lb)
                dve.tensor_reduce(BMX[:, 8:9], loc, AX.X, ALU.max)
                if pv:
                    out_sample(b - 1)
                dve.tensor_tensor(BMX[:, 0:8], PMX[:, 0::2], PMX[:, 1::2], ALU.max)
                link(dve.tensor_tensor(GATE[:], KSUM[:, 0::2], KSUM[:, 1::2], ALU.add), lb)
                ga = GATE[:]
                by_m = bass.AP(ga.tensor, ga.offset, [list(ga.ap[0]), [0, 8], [1, 8]])
                by_n = bass.AP(ga.tensor, ga.offset, [list(ga.ap[0]), [1, 8], [0, 8]])
                dve.tensor_tensor(CM1[:], by_m, by_n, ALU.is_gt)
                link(dve.tensor_tensor(CM2[:], by_m, by_n, ALU.is_equal), lb)
                link(dve.tensor_tensor(CM2[:], CM2[:], TRI, ALU.mult), lb)
                link(dve.tensor_tensor(CM1[:], CM1[:], CM2[:], ALU.add), lb)
                link(dve.tensor_reduce(RANK[:], CM1[:], AX.X, ALU.add), lb)
                link(dve.tensor_scalar(SEL[:], RANK[:], TOPK - 0.5, NEG, ALU.is_ge, ALU.mult), lb)
                link(dve.tensor_tensor(BMX[:, 0:8], BMX[:, 0:8], SEL[:], ALU.add), lb)
                link(dve.tensor_reduce(M1[:], BMX[:], AX.X, ALU.max), lb)
                link(dve.tensor_scalar(NEGM[:], M1[:], -1.0 / UNIT, None, ALU.mult), lb)
                dve.tensor_scalar(EB[:], SEL[:], NEGM[:], None, ALU.add).then_inc(eb_ok, 1)
                split_loop(b, 3)
                value_hi(b, 0)
                split_loop(b, 4)
                dve.wait_ge(ex_ok, 2 * b + 2)
                link(dve.tensor_reduce(LT[:], LSUM[:], AX.X, ALU.add), lb)
                dve.reciprocal(RL[0:32, :], LT[:])
                dve.reciprocal(RL[32:64, :], LT[:])
                dve.wait_ge(pth_ok, b + 1)
                dve.tensor_tensor(PT[:, :, 32:64], PTP, f32(PT[:, :, 0:32]), ALU.subtract)
                dve.tensor_tensor(PTL[:, 32:64], PTLP, f32(PTL[:, 0:32]), ALU.subtract).then_inc(ptl_ok, 1)
                if lb is not None:
                    assert chain[0] - first_links[0] == loop_links[0]

            sample(0, False)
            first_links[0] = chain[0]
            loop_links[0] = chain[0] - before_samples + 12
            with dve.Fori(1, NB) as b:
                sample(b, True)
            chain[0] = first_links[0] + loop_links[0] * (NB - 1)

            split_loop(NB - 1, 5)
            for p in range(NPG):
                if p + 1 < NPG:
                    value_hi(NB - 1, p + 1)
                a_step(NH - 1, p)
                if p < len(GATE_STEPS):
                    kind, g0 = GATE_STEPS[p]
                    dve.wait_ge(el_act, p + 1)
                    gx, gt = G[:, g0:g0 + 2, :], GT[:, p % 2]
                    dve.scalar_tensor_tensor(out=gt if kind == "square" else gx, in0=gt, scalar=1.0, in1=gx, op0=ALU.add,
                                             op1=ALU.mult).then_inc(el_dve, 1)
            scale_out(NB - 1)
            dve.wait_ge(at_ld, 16)
            dve.wait_ge(el_dve, len(GATE_STEPS))
            dve.tensor_tensor(G[:, GA:GA + 4, 0:SEQ], G[:, GA:GA + 4, 0:SEQ], AT[:], ALU.mult)
            dve.wait_ge(loc_pe, NB + 1)
            out_sample(NB - 1)
            dve.wait_ge(ot_ev, NB)
            dve.tensor_tensor(G[:, GA:GA + 4, SEQ:ROWS], G[:, GA:GA + 4, SEQ:ROWS], ATS[:], ALU.mult).then_inc(y_ok, 1)
            dve.wait_ge(wst_pe, 1)
            dve.wait_ge(sgw_ld, 32)
            tr = SGC[:, T_TRIL:T_TRIL + P]
            trb = bass.AP(tr.tensor, tr.offset, [list(tr.ap[0]), [0, 4], [1, P]])
            for x in range(2):
                last = dve.tensor_tensor(WST[:, 4 * x:4 * x + 4, :], BK[x][:].rearrange("p (g n) -> p g n", g=4), trb, ALU.mult)
            last.then_inc(wst_ok, 1)
            dve.wait_ge(ln_ld, 32)
            for r in range(5):
                n = P if r < 4 else NSR
                bk = BK[2 + r % 2]
                dst = VN[:, r, :] if r < 4 else VNS[:]
                dve.wait_ge(vr_pe, r + 1)
                link(dve.bn_stats(BST[0:n, 0, 0:6], bk[0:n, :]))
                link(dve.bn_aggr(BST[0:n, 1, 0:2], BST[0:n, 0, 0:6]))
                dve.tensor_scalar(MS[0:n, r:r + 1], BST[0:n, 1, 1:2], 4.0 * LN_EPS, None, ALU.add).then_inc(var_ok, 1)
                dve.wait_ge(vrs_ok, r + 1)
                link(dve.tensor_scalar(dst, bk[0:n, :], BST[0:n, 1, 0:1], RSTD[0:n, r:r + 1], ALU.subtract, ALU.mult))
                link(dve.tensor_tensor(dst, dst, LNG[0:n], ALU.mult))
                dve.tensor_tensor(dst, dst, LNB[0:n], ALU.add).then_inc(vn_ok, 1)
            dve.wait_ge(wsb_pe, 1)
            dg = SGC[0:32, T_DIAG:T_DIAG + 32]
            dve.tensor_tensor(WSB[:], BK[4][0:32, 0:256].rearrange("p (g n) -> p g n", g=NH),
                              bass.AP(dg.tensor, dg.offset, [list(dg.ap[0]), [0, NH], [1, 32]]), ALU.mult).then_inc(wsb_ok, 1)
            dve.wait_ge(bs_ld, 32)
            dve.wait_ge(el_dve, len(GATE_STEPS))
            for r in range(4):
                dve.wait_ge(z_pe, r + 1)
                tz = TZ[:, r % 2]
                for e in range(2):
                    rr = slice(e * HD, (e + 1) * HD)
                    for x in range(2):
                        bv = BK[(6, 0)[r % 2] + x][rr, :].rearrange("p (c e n) -> p c e n", c=2, e=2)[:, :, e, :]
                        last = dve.tensor_tensor(tz[rr, 2 * x:2 * x + 2, :], bv, BSB[rr, 2 * x:2 * x + 2, :], ALU.add)
                last.then_inc(z_ev, 1)
                dve.wait_ge(z_ev, r + 1)
                link(dve.tensor_tensor(tz, tz, G[:, GU:GU + 4, r * P:(r + 1) * P], ALU.mult))
                gb = G[:, GB:GB + 4, r * P:(r + 1) * P]
                link(dve.scalar_tensor_tensor(out=gb, in0=tz, scalar=0.5, in1=gb, op0=ALU.mult, op1=ALU.mult))
            dve.wait_ge(z_pe, 5)
            for e in range(2):
                rr = slice(e * HD, (e + 1) * HD)
                for c in range(PAIRS):
                    bv = BK[5][rr, 64 * c + 32 * e:64 * c + 32 * e + 32].rearrange("p (b t) -> p b t", t=TD)
                    bsv = BSB[rr, c, 0:TD]
                    last = dve.tensor_tensor(TZ[rr, 0, c, 0:32].rearrange("p (b t) -> p b t", t=TD), bv,
                                             bass.AP(bsv.tensor, bsv.offset, [list(bsv.ap[0]), [0, NB], [1, TD]]), ALU.add)
            link(last)
            link(dve.tensor_tensor(TZ[:, 0, :, 0:32], TZ[:, 0, :, 0:32], G[:, GU:GU + 4, SEQ:ROWS], ALU.mult))
            gb = G[:, GB:GB + 4, SEQ:ROWS]
            dve.scalar_tensor_tensor(out=gb, in0=TZ[:, 0, :, 0:32], scalar=0.5, in1=gb, op0=ALU.mult, op1=ALU.mult).then_inc(y_ok, 1)
            for k in range(2):
                dve.wait_ge(y_hi, k + 1)
                g0 = (GA, GB)[k]
                dve.tensor_tensor(XL[:, 4 * k:4 * k + 4, :], G[:, g0:g0 + 4, :], f32(XH[:, 4 * k:4 * k + 4, :]), ALU.subtract).then_inc(y_lo, 1)
            dve.wait_ge(m_ok, 8)
            for j in range(N_MIX):
                n = N_IN + j
                for h in range(2):
                    cs = slice(h * HALF, (h + 1) * HALF)
                    dve.wait_ge(pj, 2 * n + h + 1)
                    ga, gb = G[:, GMA + j, cs], G[:, GMB + j, cs]
                    dve.scalar_tensor_tensor(out=ga, in0=ga, scalar=1.0, in1=BK[h][:, 0:HALF], op0=ALU.add, op1=ALU.mult)
                    link(dve.scalar_tensor_tensor(out=gb, in0=gb, scalar=1.0, in1=BK[2 + h][:, 0:HALF], op0=ALU.add, op1=ALU.mult))
                    dve.tensor_tensor(ga, ga, gb, ALU.add).then_inc(mix_ok, 1)
                    dve.wait_ge(mx_hi, 2 * j + h + 1)
                    dve.tensor_tensor(ML[:, j, cs], ga, f32(MH[:, j, cs]), ALU.subtract).then_inc(mx_lo, 1)
                n += 2
                split_lo(n, n // 2 % 2, n % 2, n % 2)
            def residual(u):
                kk, r = u // 5, u % 5
                n = P if r < 4 else NSR
                dve.wait_ge(fr_pe, u + 1)
                if u == 0:
                    dve.wait_ge(fx_ld, 16 * 5)
                hx = FX[0:n, r, 512 * kk:512 * kk + 512]
                dve.scalar_tensor_tensor(out=hx, in0=BK[4 + u % 4][0:n, :], scalar=0.25, in1=hx, op0=ALU.mult, op1=ALU.add).then_inc(h_ok, 1)

            for j in range(N_OUT):
                n = N_IN + N_MIX + j + 2
                if j == 4:
                    for u in range(5):
                        residual(u)
                if j + 2 < N_OUT:
                    split_lo(n, n // 2 % 2, n % 2, n % 2)
            for u in range(5, 10):
                residual(u)
            for r in range(5):
                n = P if r < 4 else NSR
                dve.wait_ge(fss_ok, r + 1)
                dve.tensor_scalar(MS[0:n, r:r + 1], SS[0:n, r:r + 1], 1.0 / DM, EPS, ALU.mult, ALU.add).then_inc(fms_ok, 1)
            dve.wait_ge(fg_ld, 16)
            for r in range(5):
                n = P if r < 4 else NSR
                dve.wait_ge(frs_ok, r + 1)
                dve.scalar_tensor_tensor(out=FX[0:n, r, :], in0=FX[0:n, r, :], scalar=RSTD[0:n, r:r + 1], in1=FG[0:n], op0=ALU.mult,
                                         op1=ALU.mult).then_inc(fy_ok, 1)

        @block.gpsimd
        def _(pool):
            def f32(t):
                return t.bitcast(F32)

            pool.wait_ge(zero_ok, 4)
            for r in range(5):
                n = P if r < 4 else NSR
                pool.wait_ge(ms_ok, r + 1)
                pool.tensor_tensor(RSTD[0:n, r:r + 1], MS[0:n, r:r + 1], NHALF[0:n], ALU.pow).then_inc(rstd_ok, 1)
                if r == 2 or r == 4:
                    n = r // 2 - 1
                    if n:
                        pool.wait_ge(rstd_ok, 5)
                    pool.wait_ge(w_hi, n + 1)
                    pool.tensor_tensor(WL[:, n], WRAW[:, 0, :, n * P:(n + 1) * P], f32(WH[:, n]), ALU.subtract).then_inc(w_lo, 1)
            pool.wait_ge(tab_ok, 1)
            vec = VEC[:]
            pitch = NH * (P + VLEN)
            pool.dma_start(bass.AP(skew_d.tensor, skew_d.offset, [[P + VLEN, NH], [pitch + 1, P], [1, VLEN]]),
                           bass.AP(vec.tensor, vec.offset, [list(vec.ap[0]), [0, P], [1, VLEN]])).then_inc(vec_st, 16)
            def store_rows(n):
                pool.wait_ge(rs_ev, n - 4 + 1)
                to_p, to_s = ((k_p, k_s), (v_p, v_s))[n // 4 - 1]
                cols = slice(n % 4 * P, (n % 4 + 1) * P)
                pool.dma_start(to_p[0, 0].rearrange("(r p) h d -> p r (h d)", p=P)[:, :, cols], RS[:, n % 4]).then_inc(rs_st[n % 4], 16)
                pool.dma_start(to_s[0].rearrange("b t h d -> (b t) (h d)")[:, cols], RSS[:, n % 4]).then_inc(rs_st[n % 4], 16)

            for n in range(N_QKV):
                c = n % 4
                if n < 8:
                    pool.wait_ge(pj_ev, 2 * n + 2)
                    pool.dma_start((q_d, k_d)[n // 4][2 * c:2 * c + 2].rearrange("e p n -> (e p) n"), TS[:, n % 4, 0:SEQ]).then_inc(ts_st[n % 4], 16)
                if n >= 5:
                    store_rows(n - 1)
            store_rows(N_QKV - 1)
            pool.wait_ge(smp_ok, 4)

            def place_q(b):
                qc = QC[:]
                out = bass.AP(qc.tensor, qc.offset, [list(qc.ap[0]), [64 + 8, PAIRS], [32, 2], [1, 8]])
                pool.tensor_copy(out, Q16[:, :, bass.ds(b, 1), :].rearrange("p c a (w x) -> p c (a w) x", w=2)).then_inc(qc_ok, 1)

            place_q(0)

            def value_lo(b, p):
                pool.wait_ge(vh, 16 * b + p + 1)
                pool.tensor_tensor(VL[:, p % 2, :], VRAW[:, p // 2 % 2, p % 2, :], f32(VH[:, p % 2, :]), ALU.subtract).then_inc(vl, 1)

            def stage_lo(a):
                pool.wait_ge(stg_hi, 2 * a + 1)
                pool.wait_ge(qc_ok, a + 1 if isinstance(a, int) and a == NH - 1 else a + 2)
                wait(pool, vl, 16 * a)
                pool.tensor_tensor(QKL, QKR, f32(QKH), ALU.subtract).then_inc(stg_lo, 1)
                pool.wait_ge(stg_hi, 2 * a + 2)
                pool.wait_ge(stg_lo, 2 * a + 1)
                pool.tensor_tensor(AVL[:], AVR[:], f32(AVH[:]), ALU.subtract).then_inc(stg_lo, 1)

            def sample(b, pv):
                if pv:
                    for p in range(1, NPG):
                        value_lo(b - 1, p)
                if not (isinstance(b, int) and b == NB - 1):
                    pool.wait_ge(loc_pe, b + 1)
                    place_q(b + 1)
                stage_lo(b)
                value_lo(b, 0)

            sample(0, False)
            with pool.Fori(1, NB - 1) as b:
                sample(b, True)
            sample(NB - 1, True)

            for p in range(1, NPG):
                value_lo(NB - 1, p)

            def inverse_root(ready, done):
                for r in range(5):
                    n = P if r < 4 else NSR
                    pool.wait_ge(ready, r + 1)
                    wait(pool, done, r)
                    pool.tensor_tensor(RSTD[0:n, r:r + 1], MS[0:n, r:r + 1], NHALF[0:n], ALU.pow).then_inc(done, 1)

            inverse_root(var_ok, vrs_ok)
            pool.wait_ge(vn_ok, 5)
            pool.dma_start(sgu_s.rearrange("a b t d -> (a b t) d"), VNS[:]).then_inc(sgu_st, 16)
            inverse_root(fms_ok, frs_ok)


_INS = ["x_prompt", "x_sample", "cache_k", "cache_v", "page_table", "rel_bias", "norm_g", "w_in", "sgu_ln_g", "sgu_ln_b",
        "w_s", "b_s", "w_pa", "w_pb", "w_o", "final_norm_g"]
_OUTS = [(1, SEQ, DM), (NB, TD, DM), (1, 1, SEQ, NH, HD), (1, 1, SEQ, NH, HD), (1, NB, TD, NH, HD), (1, NB, TD, NH, HD), (1, NB, TD, DA)]


def kernel(**inputs):
    import concourse.bacc as _bacc
    from concourse.bass_utils import run_bass_kernel_spmd as _run

    nc = _bacc.Bacc("TRN2", target_bir_lowering=False, num_devices=1)
    arrays, args = {}, []
    named = [(n, np.ascontiguousarray(inputs[n])) for n in _INS]
    named += list(zip(("constants", "setup_constants", "gating_constants"), constants()))
    for name, a in named:
        arrays[f"in_{name}"] = a
        args.append(nc.dram_tensor(f"in_{name}", a.shape, mybir.dt.from_np(a.dtype), kind="ExternalInput").ap())
    for i, shape in enumerate(_OUTS):
        args.append(nc.dram_tensor(f"out_{i}", shape, F32, kind="ExternalOutput").ap())
    build(nc, *args)
    r = _run(nc, [arrays], core_ids=[0])
    return tuple(r.results[0][f"out_{i}"] for i in range(len(_OUTS)))
```

```python
import math
from contextlib import ExitStack

import numpy as np

import concourse.bass as bass
from concourse import mybir

F32 = mybir.dt.float32
F32R = mybir.dt.float32r
I32 = mybir.dt.int32
ALU = mybir.AluOpType
ACT = mybir.ActivationFunctionType
AX = mybir.AxisListType

P = 128
DM = 1024
SEQ = 512
NB = 8
TD = 4
NSR = NB * TD
ROWS = SEQ + NSR
HALF = ROWS // 2
KC = DM // P
NH = 8
HD = 64
DA = NH * HD
PAIRS = DA // P
PAST = 2048
PG = 128
NPG = PAST // PG
NBLK = 8
TOPK = 3
NBUCK = 32
MAXD = 128
EPS = 1e-6
LN_EPS = 1e-5
UNIT = 8.0
NEG = -1e30
N_IN = 44
N_QKV = 12
PER = 4
N_MIX = 8
N_OUT = 8
N_TILES = N_IN + N_MIX + N_OUT
GA, GU, GV, GB, GMA, GMB = 0, 4, 8, 12, 16, 24
GELU_C = math.sqrt(2.0 / math.pi)
VLEN = 384


def bucket(d):
    d = max(int(d), 0)
    if d < NBUCK // 2:
        return d
    half = NBUCK // 2
    return min(half + int(math.log(d / half) / math.log(MAXD / half) * (NBUCK - half)), NBUCK - 1)


def onehot(dists):
    e = np.zeros((NBUCK, len(dists)), np.float32)
    for n, d in enumerate(dists):
        e[bucket(d), n] += UNIT
        e[NBUCK - 1, n] -= UNIT
    return e


C_ID, C_OSEL, C_TRI = 0, 128, 160
C_COLS = 224
I_E15, I_ELOC, I_EVEC, I_VMASK, I_LOCM = 0, 512, 640, 1024, 1408
I_COLS = 1664
T_TRIL, T_REP, T_DIAG = 0, 128, 160
T_COLS = 192
GATE_STEPS = ([(kind, g0 + x) for g0 in (GV, GU) for kind in ("square", "gelu") for x in (0, 2)]
              + [("silu", g0 + x) for g0 in (GB, GA) for x in (0, 2)])


FILL = [2] * 8 + [1] * 8
HALVES_DONE = {p: [h for h in range(8) if sum(FILL[:p]) < 8 * (h + 1) <= sum(FILL[:p + 1])] for p in range(16)}
REST = 64 - sum(FILL)
HALVES_IN_PAGES = sum(len(h) for h in HALVES_DONE.values())


def constants():
    c = np.zeros((P, C_COLS), np.float32)
    c[:, C_ID:C_ID + P] = np.eye(P)
    row, col = np.arange(P)[:, None], np.arange(P)[None, :]
    c[64:128, C_OSEL:C_OSEL + 32] = row[64:128] % 32 == col[:, 0:32]
    c[:, C_TRI:C_TRI + 64] = (np.arange(8)[None, :] < np.arange(8)[:, None]).reshape(1, 64)
    i = np.zeros((NBUCK, I_COLS), np.float32)
    for t in range(TD):
        i[:, I_E15 + t * P:I_E15 + (t + 1) * P] = onehot([P + t - j for j in range(P)])
        i[:, I_ELOC + t * 32:I_ELOC + (t + 1) * 32] = onehot([t - j for _ in range(NB) for j in range(TD)])
    i[:, I_EVEC:I_EVEC + VLEN] = onehot([255 - u for u in range(VLEN)])
    i[:, I_VMASK:I_VMASK + VLEN] = np.where(np.arange(VLEN) > 255, NEG, 0.0)
    m = np.full((NH, TD, NB, NB, TD), NEG, np.float32)
    for b in range(NB):
        for t in range(TD):
            m[:, t, b, b, :t + 1] = 0.0
    i[:, I_LOCM:I_LOCM + 256] = m.reshape(32, 256)
    s = np.zeros((P, T_COLS), np.float32)
    s[:, T_TRIL:T_TRIL + P] = row <= col
    s[:, T_REP:T_REP + 32] = row == np.arange(32)[None, :] % TD
    s[0:32, T_DIAG:T_DIAG + 32] = np.arange(32)[:, None] // TD == np.arange(32)[None, :] // TD
    return c, i, s


def build(nc, x_p, x_s, cache_k, cache_v, page_table, rel_bias, norm_g, w_in, ln_g, ln_b, w_s, b_s, w_pa, w_pb,
          w_o, fin_g, cst, ini, sgc, y_p, y_s, k_p, v_p, k_s, v_s, sgu_s):
    with ExitStack() as ctx:
        base = (nc.sbuf_base + 31) // 32 * 32
        top = [base]

        def at(name, shape, dt, offset):
            t = nc.alloc_sbuf_tensor_at(name, shape, dt, offset=offset)
            return t

        def sb(name, shape, dt=F32):
            size = 4 * int(np.prod(shape[1:]))
            off = top[0]
            top[0] += (size + 31) // 32 * 32
            return at(name, shape, dt, off)

        def mark():
            return top[0]

        def sem(name):
            return ctx.enter_context(nc.semaphore(name))

        x_at = mark()
        XH = sb("XH", [P, KC, ROWS], F32R)
        XL = sb("XL", [P, KC, ROWS], F32R)
        WRAW = sb("WRAW", [P, 2, KC, 2 * P])
        WH = sb("WH", [P, 2, KC, P], F32R)
        WL = sb("WL", [P, 2, KC, P], F32R)
        kv_at = mark()
        KRAW = sb("KRAW", [P, 2, 4, DA])
        VRAW = sb("VRAW", [P, 2, 2, DA])
        KTH = sb("KTH", [P, 2, DA], F32R)
        KTL = sb("KTL", [P, 2, DA], F32R)
        VH = sb("VH", [P, 2, DA], F32R)
        VL = sb("VL", [P, 2, DA], F32R)
        g_at = mark()
        G = sb("G", [P, 32, ROWS])
        CST = sb("CST", [P, C_COLS])
        PTB = sb("PTB", [1, NB * NPG], I32)
        B15 = sb("B15", [32, P])
        LM = sb("LM", [32, NB, 32])
        Q16 = sb("Q16", [P, PAIRS, NB, 16], F32R)
        QC = sb("QC", [P, PAIRS, 2, 32], F32R)
        KSH = sb("KSH", [P, PAIRS, NSR], F32R)
        KSL = sb("KSL", [P, PAIRS, NSR], F32R)
        VSH = sb("VSH", [NSR, DA], F32R)
        OTS = at("OTS", [P, DA], F32, top[0] - 4 * DA)[64:128, :]
        VSL = sb("VSL", [NSR, DA], F32R)
        AO = at("AO", [P, SEQ], F32, top[0] - 4 * DA)[64:128, :]
        SC = sb("SC", [32, NPG * P + 32])
        o = top[0] - 4 * (NPG * P + 32)
        QKH = at("QKH", [P, 2, SEQ], F32R, o)[64:128]
        QKR = at("QKR", [P, 2, SEQ], F32, o + 8 * SEQ)[64:128]
        QKL = at("QKL", [P, 2, SEQ], F32R, o + 8 * SEQ)[64:128]
        AVH = sb("AVH", [P, 4, HD], F32R)
        AVR = sb("AVR", [P, 4, HD])
        AVL = at("AVL", [P, 4, HD], F32R, top[0] - 4 * 4 * HD)
        TPH = sb("TPH", [P, 2 * P])
        APX = sb("APX", [P, SEQ])
        APH = at("APH", [P, SEQ], F32R, top[0] - 4 * SEQ)
        APL = sb("APL", [P, SEQ], F32R)
        PT = sb("PT", [P, NPG, 64], F32R)
        PTL = sb("PTL", [32, 64], F32R)
        ATS = sb("ATS", [P, PAIRS, NSR])
        KSUM = sb("KSUM", [32, NPG])
        PMX = sb("PMX", [32, NPG])
        GATE = sb("GATE", [32, 8])
        CM1 = sb("CM1", [32, 8, 8])
        CM2 = sb("CM2", [32, 8, 8])
        RANK = sb("RANK", [32, 8])
        SEL = sb("SEL", [32, 8])
        BMX = sb("BMX", [32, 9])
        M1 = sb("M1", [32, 1])
        NEGM = sb("NEGM", [32, 1])
        EB = sb("EB", [32, 8])
        LSUM = sb("LSUM", [32, 9])
        LT = sb("LT", [32, 1])
        RL = sb("RL", [64, 1])
        SS = sb("SS", [P, 8])
        MS = sb("MS", [P, 8])
        RSTD = sb("RSTD", [P, 8])
        NHALF = sb("NHALF", [P, 1])
        NMX = sb("NMX", [P, 4])
        PLS = sb("PLS", [P, 4])
        assert top[0] <= nc.sbuf_usable_end, (top[0], nc.sbuf_usable_end)

        o = g_at
        XR = at("XR", [P, 5, DM], F32, o); o += 5 * DM * 4
        GBC = at("GBC", [P, DM], F32, o); o += DM * 4
        JUNK = at("JUNK", [P, DM], F32, o); o += DM * 4
        TS = at("TS", [P, 4, ROWS], F32, o); o += 4 * ROWS * 4
        RS = at("RS", [P, 4, 4, P], F32, o); o += 4 * 4 * P * 4
        RSS = at("RSS", [NSR, 4, P], F32, o); o += 4 * P * 4
        INI = at("INI", [NBUCK, I_COLS], F32, o); o += I_COLS * 4
        TAB = at("TAB", [NBUCK, NH], F32, o); o += NH * 4
        TB = at("TB", [NBUCK, TD, 32], F32, o); o += TD * 32 * 4
        VEC = at("VEC", [NH, VLEN], F32, o); o += VLEN * 4
        assert o <= g_at + 32 * ROWS * 4
        GT = at("GT", [P, 2, 2, ROWS], F32, x_at)
        AT = at("AT", [P, PAIRS, SEQ], F32, x_at + 17408)
        BSB = at("BSB", [P, PAIRS, P], F32, x_at + 32768)
        WSR = at("WSR", [P, NH, P], F32, kv_at + 24576)
        WST = at("WST", [P, NH, P], F32, kv_at + 28672)
        LNG = at("LNG", [P, DA], F32, x_at + 8704)
        LNB = at("LNB", [P, DA], F32, x_at + 8704 + 2048)
        o = kv_at
        VN = at("VN", [P, 4, DA], F32, o); o += 8192
        VNS = at("VNS", [NSR, DA], F32, o); o += 2048
        TZ = at("TZ", [P, 2, PAIRS, P], F32, o); o += 4096
        WSB = at("WSB", [NSR, NH, NSR], F32, o); o += 1024
        BST = at("BST", [P, 2, 8], F32, o); o += 64
        SGC = at("SGC", [P, T_COLS], F32, o); o += T_COLS * 4
        assert o <= kv_at + 16384
        MH = at("MH", [P, KC, ROWS], F32R, kv_at)
        ML = at("ML", [P, KC, ROWS], F32R, kv_at + 17408)
        o = g_at + 8 * ROWS * 4
        FX = at("FX", [P, 5, DM], F32, o); o += 5 * DM * 4
        FG = at("FG", [P, DM], F32, o); o += DM * 4
        FJ = at("FJ", [P, DM], F32, o); o += DM * 4
        assert o <= g_at + 32 * ROWS * 4

        BK = [ctx.enter_context(nc.psum_tensor(f"BK{i}", [P, 512], F32)) for i in range(8)]
        KTP = [BK[2], BK[3]]
        SCB = [BK[4], BK[5]]
        PTP = BK[6][:].rearrange("p (g x) -> p g x", g=NPG)
        OUT = BK[7][0:64, :]
        OTP = BK[7][:, 0:32].rearrange("p (c x) -> p c x", c=PAIRS)
        LOC = BK[7][0:32, 64:96]
        PTLP = BK[7][0:32, 96:128]

        IDN = CST[:, C_ID:C_ID + P]
        OSEL = CST[64:128, C_OSEL:C_OSEL + 32].rearrange("p (c x) -> p c x", c=PAIRS)
        TRI = CST[0:32, C_TRI:C_TRI + 64].rearrange("p (n m) -> p n m", n=8)

        q_d = nc.dram_tensor("q_scratch", [NH, HD, SEQ], F32, kind="Internal").ap()
        k_d = nc.dram_tensor("k_scratch", [NH, HD, SEQ], F32, kind="Internal").ap()
        attn_d = nc.dram_tensor("attn_scratch", [NH, HD, SEQ], F32, kind="Internal").ap()
        skew_d = nc.dram_tensor("skew_scratch", [P, NH, P + VLEN], F32, kind="Internal").ap()

        x_ld = [sem(f"x_ld{r}") for r in range(5)]
        cst_ld, ini_ld, pt_ld, gbc_ld = sem("cst_ld"), sem("ini_ld"), sem("pt_ld"), sem("gbc_ld")
        w_ld = [sem("w_ld0"), sem("w_ld1")]
        k_ld = [sem("k_ld0"), sem("k_ld1")]
        v_ld = [sem("v_ld0"), sem("v_ld1")]
        ss_ok, ms_ok, rstd_ok, xn_ok = sem("ss_ok"), sem("ms_ok"), sem("rstd_ok"), sem("xn_ok")
        xt_pe, xt_hi, xt_lo = sem("xt_pe"), sem("xt_hi"), sem("xt_lo")
        tb_ok, tab_pe, tab_ok, vec_st = sem("tb_ok"), sem("tab_pe"), sem("tab_ok"), sem("vec_st")
        w_hi, w_lo, pj, pj_ev = sem("w_hi"), sem("w_lo"), sem("pj"), sem("pj_ev")
        rows_pe, rs_ev, smp_ok = sem("rows_pe"), sem("rs_ev"), sem("smp_ok")
        ts_st = [sem(f"ts_st{i}") for i in range(4)]
        rs_st = [sem(f"rs_st{i}") for i in range(4)]
        kt_pe, kth, ktl, qk_pe = sem("kt_pe"), sem("kth"), sem("ktl"), sem("qk_pe")
        vh, vl, pv_pe = sem("vh"), sem("vl"), sem("pv_pe")
        qc_ok, loc_pe, sc_ok, eb_ok, ex_ok = sem("qc_ok"), sem("loc_pe"), sem("sc_ok"), sem("eb_ok"), sem("ex_ok")
        ptt_pe, pth_ok, ptl_ok = sem("ptt_pe"), sem("pth_ok"), sem("ptl_ok")
        ots_ok, ot_ev = sem("ots_ok"), sem("ot_ev")
        dchain, pchain, zero_ok = sem("dchain"), sem("pchain"), sem("zero_ok")
        at_ld, qk_ld, av_ld, tp_ld, sgw_ld, ln_ld, bs_ld = (sem(n) for n in ("at_ld", "qk_ld", "av_ld", "tp_ld", "sgw_ld", "ln_ld", "bs_ld"))
        stg_hi, stg_lo = sem("stg_hi"), sem("stg_lo")
        aq_pe, am_ok, ae_ok, ap_ok, at_pe, ath_ok, atl_ok, av_pe, ao_ok = (sem(n) for n in (
            "aq_pe", "am_ok", "ae_ok", "ap_ok", "at_pe", "ath_ok", "atl_ok", "av_pe", "ao_ok"))
        ao_st = sem("ao_st")
        el_act, el_dve, m_ok, y_ok = sem("el_act"), sem("el_dve"), sem("m_ok"), sem("y_ok")
        wst_pe, wst_ok, wsb_pe, wsb_ok = sem("wst_pe"), sem("wst_ok"), sem("wsb_pe"), sem("wsb_ok")
        vr_pe, var_ok, vrs_ok, vn_ok, sgu_st = sem("vr_pe"), sem("var_ok"), sem("vrs_ok"), sem("vn_ok"), sem("sgu_st")
        z_pe, z_ev, y_hi, y_lo = sem("z_pe"), sem("z_ev"), sem("y_hi"), sem("y_lo")
        mix_ok, mx_hi, mx_lo, ug_ok = sem("mix_ok"), sem("mx_hi"), sem("mx_lo"), sem("ug_ok")
        fx_ld, fg_ld, fr_pe, h_ok, fss_ok, fms_ok, frs_ok, fy_ok, y_st = (sem(n) for n in (
            "fx_ld", "fg_ld", "fr_pe", "h_ok", "fss_ok", "fms_ok", "frs_ok", "fy_ok", "y_st"))

        def wait(eng, s, v):
            if not isinstance(v, int) or v > 0:
                eng.wait_ge(s, v)

        def w_need(m):
            if not isinstance(m, int):
                return None
            return sum(32 if N_IN <= 2 * i < N_IN + N_MIX else 16 for i in range(m % 2, m + 1, 2))

        def used(n):
            if not isinstance(n, int) or n < N_IN:
                return 2 * n + 2
            return 2 * N_IN + 4 * min(n - N_IN + 1, N_MIX) + 2 * max(n - N_IN - N_MIX + 1, 0)

        def unit(e):
            t, x, h = e % 16 // 4, e % 4 // 2, e % 2
            return e // 16, N_IN + e // 4, 4 * x, 4 * (t // 2) + 2 * x + t % 2, h

        MBK = [BK[0], BK[1], BK[4], BK[5]]

        block = ctx.enter_context(nc.Block())

        def load_w(sp, m, slot, before):
            wait(sp, w_lo, before)
            if isinstance(m, int) and m >= N_IN // 2:
                if m < (N_IN + N_MIX) // 2:
                    src = (w_pa, w_pb)[(m - N_IN // 2) // 2]
                    for x in range(2):
                        c = (m - N_IN // 2) % 2 * 4 * P + x * 2 * P
                        sp.dma_start(WRAW[:, slot, 4 * x:4 * x + 4, :],
                                     src[0, :, c:c + 2 * P].rearrange("(k p) n -> p k n", p=P)).then_inc(w_ld[slot], 16)
                else:
                    c = (m - (N_IN + N_MIX) // 2) * 2 * P
                    sp.dma_start(WRAW[:, slot], w_o[0, :, c:c + 2 * P].rearrange("(k p) n -> p k n", p=P)).then_inc(w_ld[slot], 16)
            else:
                sp.dma_start(WRAW[:, slot], w_in[0, :, bass.ds(m * 2 * P, 2 * P)].rearrange("(k p) n -> p k n", p=P)).then_inc(w_ld[slot], 16)

        @block.sync
        def _(sp):
            for r in range(5):
                if r < 4:
                    sp.dma_start(XR[:, r, :], x_p[0, r * P:(r + 1) * P, :]).then_inc(x_ld[r], 16)
                else:
                    sp.dma_start(XR[0:NSR, r, :], x_s.rearrange("b t d -> (b t) d")).then_inc(x_ld[r], 16)
                if r == 0:
                    sp.dma_start(GBC[:], bass.AP(norm_g.tensor, norm_g.offset, [[0, P], [1, DM]])).then_inc(gbc_ld, 16)
                    sp.dma_start(CST[:], cst).then_inc(cst_ld, 16)
                if r == 2:
                    load_w(sp, 0, 0, 0)
            load_w(sp, 1, 1, 0)
            sp.dma_start(PTB[:], page_table.rearrange("(a b) n -> a (b n)", a=1)).then_inc(pt_ld, 16)
            sp.dma_start(INI[:], ini).then_inc(ini_ld, 16)
            sp.dma_start(TAB[:], rel_bias).then_inc(ini_ld, 16)
            for m in range(2, N_QKV // 2 + 1):
                load_w(sp, m, m % 2, 2 * m - 2)
            sp.wait_ge(pt_ld, 16)
            k_regs = [sp.alloc_register(f"k_page{j}") for j in range(4)]
            v_regs = [sp.alloc_register(f"v_page{j}") for j in range(4)]

            def load_k(b, q):
                wait(sp, kt_pe, 16 * b + 4 * (q - 1))
                sp.load(k_regs, PTB[0:1, bass.ds(NPG * b + 4 * q, 4)])
                for j in range(4):
                    page = sp.snap(k_regs[j], min_val=0, max_val=cache_k.shape[1] - 1)
                    sp.dma_start(KRAW[:, q % 2, j, :], cache_k[0, bass.ds(page, 1)].rearrange("a p h d -> (a p) (h d)")).then_inc(k_ld[q % 2], 16)

            def load_v(b, q):
                sp.load(v_regs, PTB[0:1, bass.ds(NPG * b + 4 * q, 4)])
                for j in range(4):
                    if j % 2 == 0:
                        wait(sp, vl, 16 * b + 2 * (2 * q + j // 2 - 1))
                    page = sp.snap(v_regs[j], min_val=0, max_val=cache_v.shape[1] - 1)
                    sp.dma_start(VRAW[:, j // 2, j % 2, :], cache_v[0, bass.ds(page, 1)].rearrange("a p h d -> (a p) (h d)")).then_inc(v_ld[j // 2], 16)

            def store_head(a):
                sp.wait_ge(ao_ok, 4 * a + 4)
                sp.dma_start(attn_d[bass.ds(a, 1)].rearrange("a p n -> (a p) n"), AO).then_inc(ao_st, 16)

            def load_head(a):
                wait(sp, aq_pe, 4 * a)
                for x, src in enumerate((q_d, k_d)):
                    sp.dma_start(QKR[:, x, :], src[bass.ds(a, 1)].rearrange("a p n -> (a p) n")).then_inc(qk_ld, 16)
                wait(sp, am_ok, 4 * a)
                sp.dma_start(TPH[:], skew_d[:, bass.ds(a, 1), P - 1:P - 1 + 2 * P].rearrange("p a n -> p (a n)")).then_inc(tp_ld, 16)
                wait(sp, av_pe, 4 * a)
                sp.dma_start(AVR[:], v_p[0, 0].rearrange("(r p) h d -> p r h d", p=P)[:, :, bass.ds(a, 1), :].rearrange("p r a d -> p r (a d)")).then_inc(av_ld, 16)

            def sample(b, pv):
                for q in range(4):
                    if q:
                        load_k(b, q)
                    if pv and q:
                        load_v(b - 1, q)
                    if q == 0:
                        load_w(sp, 2 * b + 7, 1, 4 * b + 12)
                    if q == 2:
                        load_w(sp, 2 * b + 8, 0, 4 * b + 14)
                if not (isinstance(b, int) and b == NB - 1):
                    load_k(b + 1, 0)
                load_v(b, 0)
                if pv:
                    store_head(b - 1)
                else:
                    for i in range(4):
                        sp.wait_ge(ts_st[i], 16 * 2)
                        sp.wait_ge(rs_st[i], 32 * 2)
                    sp.wait_ge(vec_st, 16)
                load_head(b)

            load_k(0, 0)
            sample(0, False)
            sample(1, True)
            with sp.Fori(2, NB - 1) as b:
                sample(b, True)
            sample(NB - 1, True)
            sp.wait_ge(pj, 2 * N_IN)
            sp.wait_ge(qk_pe, 16 * NB)
            sp.dma_start(WSR[:], w_s[0].rearrange("g t s -> t g s")).then_inc(sgw_ld, 16)
            sp.dma_start(SGC[:], sgc).then_inc(sgw_ld, 16)
            load_v(NB - 1, 1)
            sp.dma_start(LNG[:], bass.AP(ln_g.tensor, ln_g.offset, [[0, P], [1, DA]])).then_inc(ln_ld, 16)
            sp.dma_start(LNB[:], bass.AP(ln_b.tensor, ln_b.offset, [[0, P], [1, DA]])).then_inc(ln_ld, 16)
            load_v(NB - 1, 2)
            for e in range(2):
                sp.dma_start(BSB[e * HD:(e + 1) * HD], bass.AP(b_s.tensor, b_s.offset + e * P, [[0, HD], [2 * P, PAIRS], [1, P]])).then_inc(bs_ld, 16)
            load_v(NB - 1, 3)
            sp.wait_ge(ao_st, 16 * (NH - 1))
            for e in range(2):
                heads = attn_d.rearrange("(c e) p n -> e p c n", e=2)[e, :, 0:PAIRS - e, :]
                sp.dma_start(AT[e * HD:(e + 1) * HD, 0:PAIRS - e, :], heads).then_inc(at_ld, 16)
            for m in range(23, N_TILES // 2):
                load_w(sp, m, m % 2, 2 * m - 2)
            sp.wait_ge(mx_lo, 2 * N_MIX)
            for r in range(4):
                sp.dma_start(FX[:, r, :], x_p[0, r * P:(r + 1) * P, :]).then_inc(fx_ld, 16)
            sp.dma_start(FX[0:NSR, 4, :], x_s.rearrange("b t d -> (b t) d")).then_inc(fx_ld, 16)
            sp.dma_start(FG[:], bass.AP(fin_g.tensor, fin_g.offset, [[0, P], [1, DM]])).then_inc(fg_ld, 16)
            for r in range(5):
                sp.wait_ge(fy_ok, r + 1)
                if r < 4:
                    sp.dma_start(y_p[0, r * P:(r + 1) * P, :], FX[:, r, :]).then_inc(y_st, 16)
                else:
                    sp.dma_start(y_s.rearrange("b t d -> (b t) d"), FX[0:NSR, 4, :]).then_inc(y_st, 16)
            sp.wait_ge(y_st, 16 * 5)
            sp.wait_ge(sgu_st, 16)

        @block.tensor
        def _(pe):
            mm = pe.matmul

            def half(n, par, h, XA=XH, XB=XL, read=None):
                if h == 0:
                    pe.wait_ge(w_lo, n + 1)
                wait(pe, pj_ev, 2 * n + h - 1 if read is None else read)
                cols = slice(h * HALF, (h + 1) * HALF)
                for k in range(KC):
                    for w, x in ((WH, XA), (WH, XB), (WL, XA)):
                        last = mm(BK[h][:, 0:HALF], w[:, par, k, :], x[:, k, cols], start=(k == 0 and w is WH and x is XA),
                                  stop=(k == KC - 1 and w is WL))
                    if k == KC - 1:
                        last.then_inc(pj, 1)
                    yield

            def run(g, steps=99):
                for _ in range(steps):
                    if next(g, 0) == 0:
                        break

            pe.wait_ge(cst_ld, 16)
            def turn_x(u):
                r, kk = u // 2, u % 2
                n = P if r < 4 else NSR
                wait(pe, xn_ok, r + 1)
                wait(pe, xt_lo, u - 3)
                for j in range(4):
                    k = 4 * kk + j
                    last = pe.transpose(BK[4 + u % 4][:, j * n:(j + 1) * n], XR[0:n, r, k * P:(k + 1) * P], IDN[0:n, 0:n])
                last.then_inc(xt_pe, 1)

            for u in range(6):
                turn_x(u)

            def rows(n):
                i = n - 4
                pe.wait_ge(pj_ev, 2 * n + 2)
                wait(pe, rs_ev, i - 1)
                bp, bs = BK[4 + 2 * (i % 2)], BK[5 + 2 * (i % 2)]
                for r in range(4):
                    pe.transpose(bp[:, r * P:(r + 1) * P], TS[:, n % 4, r * P:(r + 1) * P], IDN)
                pe.transpose(bs[0:NSR, 0:P], TS[:, n % 4, SEQ:ROWS], IDN).then_inc(rows_pe, 1)

            pe.wait_ge(xt_lo, 6)
            for n in range(N_QKV):
                first = half(n, n % 2, 0)
                if n == 0:
                    for u in range(6, 10):
                        run(first, 2 if u > 7 else 1)
                        turn_x(u)
                run(first)
                if n == 0:
                    pe.wait_ge(xt_lo, 10)
                if n == 1:
                    pe.wait_ge(tb_ok, 1)
                    for t in range(TD):
                        mm(BK[2][0:32, 0:P], TB[:, t, :], INI[:, I_E15 + t * P:I_E15 + (t + 1) * P], start=(t == 0), stop=(t == 3))
                    for t in range(TD):
                        mm(BK[3][0:32, 0:32], TB[:, t, :], INI[:, I_ELOC + t * 32:I_ELOC + (t + 1) * 32], start=(t == 0), stop=(t == 3))
                    mm(BK[3][0:NH, 64:64 + VLEN], TAB[:], INI[:, I_EVEC:I_EVEC + VLEN], start=True, stop=True).then_inc(tab_pe, 1)
                if n - 1 >= 4:
                    rows(n - 1)
                run(half(n, n % 2, 1))
            rows(N_QKV - 1)

            def turn_page(b, p):
                q, i = p // 4, 16 * b + p
                if p % 4 == 0:
                    pe.wait_ge(k_ld[q % 2], 64 * (2 * b + q // 2 + 1))
                wait(pe, ktl, i - 1)
                if isinstance(b, int) and b == 0 and p == 0:
                    pe.wait_ge(tab_ok, 1)
                for c in range(PAIRS):
                    last = pe.transpose(KTP[p % 2][:, c * P:(c + 1) * P], KRAW[:, q % 2, p % 4, c * P:(c + 1) * P], IDN)
                last.then_inc(kt_pe, 1)

            def scores(out, hi, lo):
                for c in range(PAIRS):
                    for w, x in ((0, hi), (0, lo), (1, hi)):
                        last = mm(out, QC[:, c, w, :], x[c], start=(c == 0 and w == 0 and x is hi), stop=(c == PAIRS - 1 and w == 1))
                return last

            def score_page(b, p):
                if p == 0:
                    pe.wait_ge(qc_ok, b + 1)
                    if isinstance(b, int) and b == 0:
                        pe.wait_ge(rs_ev, 8)
                        pe.wait_ge(smp_ok, 12)
                if p % 4 == 0:
                    wait(pe, sc_ok, 4 * b + p // 4 - 1)
                pe.wait_ge(ktl, 16 * b + p + 1)
                hi, lo = ([w[:, p % 2, c * P:(c + 1) * P] for c in range(PAIRS)] for w in (KTH, KTL))
                scores(SCB[p // 4 % 2][0:32, p % 4 * P:(p % 4 + 1) * P], hi, lo).then_inc(qk_pe, 1)

            def value_page(b, p):
                if p == 0:
                    pe.wait_ge(ptl_ok, b + 1)
                    mm(OUT, PTL[:], VSH[:], start=True, stop=False)
                    mm(OUT, PTL[:], VSL[:], start=False, stop=False)
                pe.wait_ge(vl, 16 * b + p + 1)
                mm(OUT, PT[:, p, :], VH[:, p % 2, :], start=False, stop=False)
                mm(OUT, PT[:, p, :], VL[:, p % 2, :], start=False, stop=(p == NPG - 1)).then_inc(pv_pe, 1)

            def turn_out():
                for c in range(PAIRS):
                    last = mm(OTP[:, c, :], OTS[:, c * P:(c + 1) * P], OSEL[:, c, :], start=True, stop=True, skip_group_check=True)
                return last

            def a_scores(a, p):
                i = p // 4
                if p % 4 == 0:
                    if i == 0:
                        pe.wait_ge(stg_lo, 2 * a + 1)
                        pe.wait_ge(ptl_ok, a + 1)
                    else:
                        pe.wait_ge(ao_ok, 4 * a + i)
                    n = (i + 1) * P
                    for w, x in ((QKH, QKH), (QKH, QKL), (QKL, QKH)):
                        last = mm(BK[6][:, 0:n], w[:, 0, i * P:(i + 1) * P], x[:, 1, 0:n], start=(w is QKH and x is QKH), stop=(w is QKL))
                    last.then_inc(aq_pe, 1)

            def a_turn(a, p):
                i = p // 4
                if p % 4 == 2:
                    pe.wait_ge(ap_ok, 4 * a + i + 1)
                    for j in range(i + 1):
                        last = pe.transpose(BK[6][:, j * P:(j + 1) * P], APX[:, j * P:(j + 1) * P], IDN)
                    last.then_inc(at_pe, 1)

            def a_values(a, p):
                i = p // 4
                if p % 4 == 3:
                    if i == 0:
                        pe.wait_ge(stg_lo, 2 * a + 2)
                    pe.wait_ge(atl_ok, 4 * a + i + 1)
                    for j in range(i + 1):
                        for w, x in ((AVH, APH), (AVH, APL), (AVL, APH)):
                            last = mm(BK[6][0:64, 0:P], w[:, j, :], x[:, j * P:(j + 1) * P], start=(j == 0 and w is AVH and x is APH),
                                      stop=(j == i and w is AVL))
                    last.then_inc(av_pe, 1)

            def sample(b, pv):
                n0 = N_QKV + PER * b
                steps_of = (step for j in range(PER) for h in range(2) for step in half(n0 + j, j % 2, h))

                def fill(steps):
                    run(steps_of, steps)

                for p in range(NPG):
                    turn_page(b, p)
                    if pv:
                        a_turn(b - 1, p)
                    fill(FILL[p])
                    if p:
                        score_page(b, p - 1)
                    if pv:
                        a_scores(b - 1, p)
                        a_values(b - 1, p)
                    if p == NPG - 1:
                        fill(1)
                        score_page(b, p)
                    if pv:
                        value_page(b - 1, p)
                fill(5)
                if pv:
                    pe.wait_ge(ots_ok, b)
                    turn_out()
                scores(LOC, [KSH[:, c, :] for c in range(PAIRS)], [KSL[:, c, :] for c in range(PAIRS)]).then_inc(loc_pe, 1)
                fill(REST - 16)
                pe.wait_ge(ex_ok, 2 * b + 1)
                if pv:
                    pe.wait_ge(ao_ok, 4 * b)
                fill(1)
                for p in range(8):
                    pe.transpose(PTP[:, p, :], SC[:, p * P:(p + 1) * P], IDN[0:32, 0:32])
                fill(2)
                pe.wait_ge(ex_ok, 2 * b + 2)
                fill(1)
                for p in range(8, NPG):
                    pe.transpose(PTP[:, p, :], SC[:, p * P:(p + 1) * P], IDN[0:32, 0:32])
                pe.transpose(PTLP, SC[:, NPG * P:NPG * P + 32], IDN[0:32, 0:32]).then_inc(ptt_pe, 1)
                fill(64)

            sample(0, False)
            with pe.Fori(1, NB) as b:
                sample(b, True)

            for p in range(NPG):
                a_turn(NH - 1, p)
                a_scores(NH - 1, p)
                a_values(NH - 1, p)
                value_page(NB - 1, p)
                if p == 3:
                    pe.wait_ge(sgw_ld, 32)
                    for g in range(NH):
                        last = pe.transpose(BK[2 + g // 4][:, g % 4 * P:(g % 4 + 1) * P], WSR[:, g, :], IDN)
                    last.then_inc(wst_pe, 1)
                if p == 5:
                    pe.wait_ge(wst_ok, 1)
                    rep = SGC[:, T_REP:T_REP + 32]
                    mm(BK[2][0:32, 0:256], rep, bass.AP(WST[:].tensor, WST[:].offset, [list(WST[:].ap[0]), [P, NH], [0, NB], [1, TD]]),
                       start=True, stop=True).then_inc(wsb_pe, 1)
                if p >= 7 and p % 2 == 1:
                    r = (p - 7) // 2
                    n = P if r < 4 else NSR
                    pe.wait_ge(el_dve, 4)
                    wait(pe, vn_ok, r - 1)
                    for c in range(PAIRS):
                        last = pe.transpose(BK[4 + r % 2][0:n, c * P:(c + 1) * P], G[:, GV + c, r * P:r * P + n], IDN)
                    last.then_inc(vr_pe, 1)
            pe.wait_ge(ots_ok, NB)
            turn_out().then_inc(loc_pe, 1)

            def spatial(r):
                pe.wait_ge(vn_ok, r + 1)
                wait(pe, z_ev, r - 1)
                if r == 0:
                    pe.wait_ge(wsb_ok, 1)
                for c in range(PAIRS):
                    for e in range(2):
                        g = 2 * c + e
                        last = mm(BK[2 + r % 2][e * HD:(e + 1) * HD, c * P:(c + 1) * P], VN[:, r, g * HD:(g + 1) * HD], WST[:, g, :],
                                  start=True, stop=True, skip_group_check=True)
                last.then_inc(z_pe, 1)

            def mix(units):
                for e in units:
                    br, n, k0, j, h = unit(e)
                    if e % 4 == 0:
                        pe.wait_ge(w_lo, n + 1)
                    if e < 4:
                        pe.wait_ge(pj_ev, 2 * N_IN) if e < 2 else pe.wait_ge(vn_ok, 5)
                    else:
                        pe.wait_ge(mix_ok, e - 3)
                    for k in range(4):
                        for w, x in ((WH, XH), (WH, XL), (WL, XH)):
                            last = mm(MBK[e % 4][:, 0:HALF], w[:, n % 2, k0 + k, :], x[:, 4 * br + k, h * HALF:(h + 1) * HALF],
                                      start=(k == 0 and w is WH and x is XH), stop=(k == 3 and w is WL))
                    last.then_inc(pj, 1)

            spatial(0)
            spatial(1)
            pe.wait_ge(y_lo, 1)
            mix(range(4))
            spatial(2)
            spatial(3)
            pe.wait_ge(z_ev, 3)
            pe.wait_ge(vn_ok, 5)
            for g in range(NH):
                e = g % 2
                last = mm(BK[2][e * HD:(e + 1) * HD, g // 2 * 32:g // 2 * 32 + 32], VNS[:, g * HD:(g + 1) * HD], WSB[:, g, :],
                          start=True, stop=True, skip_group_check=True)
            last.then_inc(z_pe, 1)
            mix(range(4, 16))
            pe.wait_ge(y_lo, 2)
            mix(range(16, 32))
            def out_rows(u):
                kk, r = u // 5, u % 5
                n = P if r < 4 else NSR
                wait(pe, h_ok, u - 3)
                for j in range(4):
                    last = pe.transpose(BK[4 + u % 4][0:n, j * P:(j + 1) * P], G[:, 4 * kk + j, r * P:r * P + n], IDN)
                last.then_inc(fr_pe, 1)

            pe.wait_ge(mx_lo, 2 * N_MIX)
            for j in range(N_OUT):
                n = N_IN + N_MIX + j
                run(half(n, n % 2, 0, MH, ML, 2 * (N_IN + j) - 1))
                if j == 4:
                    pe.wait_ge(pj_ev, 2 * (N_IN + j))
                    for u in range(5):
                        out_rows(u)
                run(half(n, n % 2, 1, MH, ML, 2 * (N_IN + j)))
            pe.wait_ge(pj_ev, 2 * (N_IN + N_OUT))
            for u in range(5, 10):
                out_rows(u)

        @block.scalar
        def _(act):
            def copy(o, i):
                return act.activation(o, i, ACT.Copy)

            def split_hi(n, slot, side, par, need):
                act.wait_ge(w_ld[slot], need)
                wait(act, pj, used(n - 2))
                copy(WH[:, par], WRAW[:, slot, :, side * P:(side + 1) * P]).then_inc(w_hi, 1)

            def squares(r):
                n = P if r < 4 else NSR
                act.wait_ge(x_ld[r], 16)
                if r:
                    act.wait_ge(ss_ok, r)
                act.activation(JUNK[0:n], XR[0:n, r, :], ACT.Square, accum_out=SS[0:n, r:r + 1]).then_inc(ss_ok, 1)

            def x_hi(r):
                n = P if r < 4 else NSR
                for kk in range(2):
                    u = 2 * r + kk
                    act.wait_ge(xt_pe, u + 1)
                    copy(XH[:, 4 * kk:4 * kk + 4, r * P:r * P + n], BK[4 + u % 4][:, 0:4 * n].rearrange("p (k n) -> p k n", k=4)).then_inc(xt_hi, 1)

            squares(0)
            squares(1)
            x_hi(0)
            squares(2)
            x_hi(1)
            split_hi(0, 0, 0, 0, w_need(0))
            x_hi(2)
            squares(3)
            squares(4)
            split_hi(1, 0, 1, 1, w_need(0))
            x_hi(3)
            x_hi(4)
            for n in range(N_QKV):
                for h in range(2):
                    act.wait_ge(pj, 2 * n + h + 1)
                    if h == 0 and n >= 4:
                        if n - 4 < 8:
                            act.wait_ge(ts_st[n % 4], 16 * ((n - 4) // 4 + 1))
                        wait(act, rows_pe, n - 4 - 4 + 1)
                        wait(act, smp_ok, min(n - 3, 8))
                    copy(TS[:, n % 4, h * HALF:(h + 1) * HALF], BK[h][:, 0:HALF]).then_inc(pj_ev, 1)
                m = (n + 2) // 2
                split_hi(n + 2, m % 2, n % 2, n % 2, w_need(m))

            def page_hi(b, p):
                i = 16 * b + p
                act.wait_ge(kt_pe, i + 1)
                wait(act, qk_pe, i - 1)
                copy(KTH[:, p % 2, :], KTP[p % 2][:]).then_inc(kth, 1)

            def a_out(a, i):
                act.wait_ge(av_pe, 4 * a + i + 1)
                if i == 0:
                    wait(act, ao_st, 16 * a)
                copy(AO[:, i * P:(i + 1) * P], BK[6][0:64, 0:P]).then_inc(ao_ok, 1)

            def a_step(a, p):
                i = p // 4
                n = (i + 1) * P
                if p % 4 == 0 and i:
                    a_out(a, i - 1)
                if p % 4 == 1:
                    act.wait_ge(am_ok, 4 * a + i + 1)
                    act.activation(APX[:, 0:n], BK[6][:, 0:n], ACT.Exp, bias=NMX[:, i:i + 1], scale=1.0 / UNIT,
                                   accum_out=PLS[:, i:i + 1]).then_inc(ae_ok, 1)
                if p % 4 == 2:
                    act.wait_ge(at_pe, 4 * a + i + 1)
                    copy(APH[:, 0:n], BK[6][:, 0:n]).then_inc(ath_ok, 1)

            def stage_hi(a):
                act.wait_ge(qk_ld, 32 * (a + 1))
                copy(QKH, QKR).then_inc(stg_hi, 1)
                act.wait_ge(av_ld, 16 * (a + 1))
                copy(AVH[:], AVR[:]).then_inc(stg_hi, 1)

            def page_scores(b, q):
                act.wait_ge(qk_pe, 16 * b + 4 * q + 4)
                if q == 0:
                    wait(act, ptt_pe, b)
                for p in range(4 * q, 4 * q + 4):
                    last = act.activation(SC[:, p * P:(p + 1) * P], SCB[q % 2][0:32, p % 4 * P:(p % 4 + 1) * P], ACT.Copy,
                                          accum_out=KSUM[:, p:p + 1])
                last.then_inc(sc_ok, 1)

            def evac(b, j, h):
                n = N_QKV + PER * b + j
                act.wait_ge(pj, 2 * n + h + 1)
                copy(G[:, bass.ds(PER * b + j, 1), h * HALF:(h + 1) * HALF].rearrange("p a n -> p (a n)"), BK[h][:, 0:HALF]).then_inc(pj_ev, 1)

            def split_loop(b, j):
                m2 = j // 2
                if isinstance(b, int) and b == NB - 1 and j >= 4:
                    need = w_need(N_IN // 2)
                else:
                    need = 16 * (b + 3 + m2)
                split_hi(N_QKV + PER * b + j, m2 % 2, j % 2, j % 2, need)

            def sample(b, pv):
                for p in range(NPG):
                    page_hi(b, p)
                    if pv and p == 0:
                        evac(b - 1, 3, 1)
                    if pv and p == 3:
                        split_loop(b - 1, 5)
                    if pv:
                        a_step(b - 1, p)
                    if isinstance(b, int) and b == 0 and p == 4:
                        for i in range(4):
                            act.wait_ge(ts_st[i], 32)
                            act.wait_ge(rs_st[i], 64)
                        act.wait_ge(rs_ev, 8)
                        act.wait_ge(smp_ok, 12)
                        act.wait_ge(tab_ok, 1)
                        act.wait_ge(vec_st, 16)
                    for h in HALVES_DONE.get(p - 1, ()):
                        evac(b, h // 2, h % 2)
                    if p == 10:
                        split_loop(b, 2)
                    if p in (5, 9, 13):
                        page_scores(b, (p - 5) // 4)
                page_scores(b, 3)
                if pv:
                    a_out(b - 1, 3)
                for h in HALVES_DONE[NPG - 1] + list(range(HALVES_IN_PAGES, 5)):
                    evac(b, h // 2, h % 2)
                    if h == 3:
                        split_loop(b, 3)
                stage_hi(b)
                act.wait_ge(eb_ok, b + 1)
                for n in range(8):
                    blk = SC[:, 2 * n * P:2 * (n + 1) * P]
                    e = act.activation(blk, blk, ACT.Exp, bias=EB[:, n:n + 1], scale=1.0 / UNIT, accum_out=LSUM[:, n:n + 1])
                    if n == 3:
                        e.then_inc(ex_ok, 1)
                loc = SC[:, NPG * P:NPG * P + 32]
                act.activation(loc, loc, ACT.Exp, bias=NEGM[:], scale=1.0 / UNIT, accum_out=LSUM[:, 8:9]).then_inc(ex_ok, 1)
                evac(b, 2, 1)
                split_loop(b, 4)
                act.wait_ge(ptt_pe, b + 1)
                copy(PT[:, :, 0:32], PTP)
                copy(PTL[:, 0:32], PTLP).then_inc(pth_ok, 1)
                evac(b, 3, 0)

            sample(0, False)
            with act.Fori(1, NB - 1) as b:
                sample(b, True)
            sample(NB - 1, True)

            def gate_step(s):
                kind, g0 = GATE_STEPS[s]
                gt = GT[:, s % 2]
                wait(act, el_dve, s - 1)
                if s == 0:
                    act.wait_ge(pj, 2 * N_IN)
                if kind == "square":
                    act.activation(gt, G[:, g0:g0 + 2, :], ACT.Square, scale=math.sqrt(0.044715)).then_inc(el_act, 1)
                elif kind == "gelu":
                    act.activation(gt, gt, ACT.Tanh, scale=GELU_C).then_inc(el_act, 1)
                else:
                    act.activation(gt, G[:, g0:g0 + 2, :], ACT.Tanh, scale=0.5).then_inc(el_act, 1)

            def value_hi(p):
                q = p // 2
                if p % 2 == 0:
                    act.wait_ge(v_ld[q % 2], 32 * (4 * (NB - 1) + q // 2 + 1))
                if p == 1:
                    act.wait_ge(vl, 16 * (NB - 1) + 1)
                act.wait_ge(pv_pe, 16 * (NB - 1) + p - 1)
                copy(VH[:, p % 2, :], VRAW[:, q % 2, p % 2, :]).then_inc(vh, 1)

            evac(NB - 1, 3, 1)
            split_loop(NB - 1, 5)
            for p in range(NPG):
                if p + 1 < NPG:
                    value_hi(p + 1)
                a_step(NH - 1, p)
                if p < len(GATE_STEPS):
                    gate_step(p)
            a_out(NH - 1, 3)

            def tanh_gates(v):
                g0 = GMA + v * 2
                act.activation(G[:, g0:g0 + 2, :], G[:, g0:g0 + 2, :], ACT.Tanh, scale=0.5).then_inc(m_ok, 1)

            for v in range(4):
                tanh_gates(v)
            act.wait_ge(y_ok, 1)
            copy(XH[:, 0:4, :], G[:, GA:GA + 4, :]).then_inc(y_hi, 1)
            for t in range(2):
                tanh_gates(4 + 2 * t)
                tanh_gates(5 + 2 * t)
                n = N_IN + t + 2
                split_hi(n, n // 2 % 2, n % 2, n % 2, w_need(n // 2))
            act.wait_ge(y_ok, 2)
            copy(XH[:, 4:8, :], G[:, GB:GB + 4, :]).then_inc(y_hi, 1)
            for n in range(N_IN + 4, N_IN + 6):
                split_hi(n, n // 2 % 2, n % 2, n % 2, w_need(n // 2))
            act.wait_ge(sgu_st, 16)
            for e in range(16, 32):
                br, n, k0, j, h = unit(e)
                act.wait_ge(mix_ok, e + 1)
                cs = slice(h * HALF, (h + 1) * HALF)
                copy(MH[:, j, cs], G[:, GMA + j, cs]).then_inc(mx_hi, 1)
                if e % 4 == 3:
                    split_hi(n + 2, (n + 2) // 2 % 2, n % 2, n % 2, w_need((n + 2) // 2))
            for j in range(N_OUT):
                n = N_IN + N_MIX + j
                for h in range(2):
                    act.wait_ge(pj, used(n - 1) + h + 1)
                    copy(G[:, j, h * HALF:(h + 1) * HALF], BK[h][:, 0:HALF]).then_inc(pj_ev, 1)
                if j + 2 < N_OUT:
                    split_hi(n + 2, (n + 2) // 2 % 2, n % 2, n % 2, w_need((n + 2) // 2))
            for r in range(5):
                n = P if r < 4 else NSR
                act.wait_ge(h_ok, 5 + r + 1)
                if r:
                    act.wait_ge(fss_ok, r)
                act.activation(FJ[0:n], FX[0:n, r, :], ACT.Square, accum_out=SS[0:n, r:r + 1]).then_inc(fss_ok, 1)

        @block.vector
        def _(dve):
            chain, loop_links, first_links = [0], [0], [0]

            def link(ins, b=None):
                ins.then_inc(dchain, 1)
                chain[0] += 1
                dve.wait_ge(dchain, chain[0] if b is None else (b - 1) * loop_links[0] + chain[0])

            def f32(t):
                return t.bitcast(F32)

            def split_lo(n, slot, side, par):
                dve.wait_ge(w_hi, n + 1)
                dve.tensor_tensor(WL[:, par], WRAW[:, slot, :, side * P:(side + 1) * P], f32(WH[:, par]), ALU.subtract).then_inc(w_lo, 1)

            dve.memset(TB[:], 0.0).then_inc(zero_ok, 1)
            dve.memset(NHALF[:], -0.5).then_inc(zero_ok, 1)
            dve.memset(Q16[:].bitcast(F32), 0.0).then_inc(zero_ok, 1)
            dve.memset(QC[:].bitcast(F32), 0.0).then_inc(zero_ok, 1)
            dve.wait_ge(zero_ok, 4)
            def mean_square(r):
                n = P if r < 4 else NSR
                dve.wait_ge(ss_ok, r + 1)
                dve.tensor_scalar(MS[0:n, r:r + 1], SS[0:n, r:r + 1], 1.0 / DM, EPS, ALU.mult, ALU.add).then_inc(ms_ok, 1)

            def normalise(r):
                n = P if r < 4 else NSR
                if r == 0:
                    dve.wait_ge(gbc_ld, 16)
                dve.wait_ge(rstd_ok, r + 1)
                dve.scalar_tensor_tensor(out=XR[0:n, r, :], in0=XR[0:n, r, :], scalar=RSTD[0:n, r:r + 1], in1=GBC[0:n], op0=ALU.mult,
                                         op1=ALU.mult).then_inc(xn_ok, 1)

            def x_lo(r):
                n = P if r < 4 else NSR
                for kk in range(2):
                    u = 2 * r + kk
                    dve.wait_ge(xt_hi, u + 1)
                    dst = slice(r * P, r * P + n)
                    dve.tensor_tensor(XL[:, 4 * kk:4 * kk + 4, dst], BK[4 + u % 4][:, 0:4 * n].rearrange("p (k n) -> p k n", k=4),
                                      f32(XH[:, 4 * kk:4 * kk + 4, dst]), ALU.subtract).then_inc(xt_lo, 1)

            for r in range(3):
                mean_square(r)
                if r == 2:
                    x_lo(0)
                normalise(r)
            x_lo(1)
            x_lo(2)
            for r in range(3, 5):
                mean_square(r)
                normalise(r)
            x_lo(3)
            x_lo(4)
            dve.wait_ge(ini_ld, 32)
            for t in range(TD):
                last = dve.tensor_copy(TB[:, t, t:t + 29:4], TAB[:])
            last.then_inc(tb_ok, 1)
            dve.wait_ge(tab_pe, 1)
            dve.tensor_copy(B15[:], BK[2][0:32, 0:P])
            lmo = LM[:]
            src = BK[3][0:32, 0:32]
            dve.tensor_tensor(lmo, bass.AP(src.tensor, src.offset, [list(src.ap[0]), [0, NB], [1, 32]]),
                              INI[:, I_LOCM:I_LOCM + 256].rearrange("p (b n) -> p b n", b=NB), ALU.add)
            dve.tensor_tensor(VEC[:], BK[3][0:NH, 64:64 + VLEN], INI[0:NH, I_VMASK:I_VMASK + VLEN], ALU.add).then_inc(tab_ok, 1)

            def rows_out(n):
                i, c = n - 4, n % 4
                bp, bs = BK[4 + 2 * (i % 2)], BK[5 + 2 * (i % 2)]
                dve.wait_ge(rows_pe, i + 1)
                wait(dve, rs_st[n % 4], 32 * (i // 4))
                dve.tensor_copy(RS[:, n % 4], bp[:].rearrange("p (r n) -> p r n", r=4))
                link(dve.tensor_copy(RSS[:, n % 4], bs[0:NSR, 0:P]))
                dve.sem_inc(rs_ev, 1)
                if n >= 8:
                    vc = slice(c * P, (c + 1) * P)
                    link(dve.tensor_copy(VSH[:, vc], RSS[:, n % 4]))
                    dve.tensor_tensor(VSL[:, vc], RSS[:, n % 4], f32(VSH[:, vc]), ALU.subtract).then_inc(smp_ok, 1)

            for n in range(N_QKV):
                c = n % 4
                if n < 8:
                    dve.wait_ge(pj_ev, 2 * n + 2)
                    smp = TS[:, n % 4, SEQ:ROWS]
                    if n < 4:
                        for e in range(2):
                            rr = slice(e * HD, (e + 1) * HD)
                            sv = TS[rr, n % 4, SEQ:ROWS].rearrange("p (b t) -> p b t", t=TD)
                            link(dve.tensor_copy(Q16[rr, c, :, 4 * e:4 * e + 4], sv))
                            last = dve.tensor_tensor(Q16[rr, c, :, 8 + 4 * e:12 + 4 * e], sv, f32(Q16[rr, c, :, 4 * e:4 * e + 4]), ALU.subtract)
                        last.then_inc(smp_ok, 1)
                    else:
                        link(dve.tensor_copy(KSH[:, c, :], smp))
                        dve.tensor_tensor(KSL[:, c, :], smp, f32(KSH[:, c, :]), ALU.subtract).then_inc(smp_ok, 1)
                if n - 1 >= 4:
                    rows_out(n - 1)
                m = (n + 2) // 2
                split_lo(n + 2, m % 2, n % 2, n % 2)
            rows_out(N_QKV - 1)

            before_samples = chain[0]

            def page_lo(b, p):
                i = 16 * b + p
                dve.wait_ge(kth, i + 1)
                dve.tensor_tensor(KTL[:, p % 2, :], KTP[p % 2][:], f32(KTH[:, p % 2, :]), ALU.subtract).then_inc(ktl, 1)

            def value_hi(b, p):
                q, i = p // 2, 16 * b + p
                if p % 2 == 0:
                    dve.wait_ge(v_ld[q % 2], 32 * (4 * b + q // 2 + 1))
                wait(dve, pv_pe, i - 1)
                dve.tensor_copy(VH[:, p % 2, :], VRAW[:, q % 2, p % 2, :]).then_inc(vh, 1)

            def split_loop(b, j):
                m2 = j // 2
                split_lo(N_QKV + PER * b + j, m2 % 2, j % 2, j % 2)

            def a_step(a, p, lb=None):
                i = p // 4
                n = (i + 1) * P
                bk = BK[6]
                if p % 4 == 0:
                    dve.wait_ge(aq_pe, 4 * a + i + 1)
                    if i == 0:
                        dve.wait_ge(tp_ld, 16 * (a + 1))
                    w = min(n, 2 * P)
                    link(dve.tensor_tensor(bk[:, n - w:n], bk[:, n - w:n], TPH[:, 2 * P - w:2 * P], ALU.add), lb)
                    link(dve.tensor_reduce(NMX[:, i:i + 1], bk[:, 0:n], AX.X, ALU.max), lb)
                    dve.tensor_scalar(NMX[:, i:i + 1], NMX[:, i:i + 1], -1.0 / UNIT, None, ALU.mult).then_inc(am_ok, 1)
                if p % 4 == 1:
                    dve.wait_ge(ae_ok, 4 * a + i + 1)
                    link(dve.reciprocal(PLS[:, i:i + 1], PLS[:, i:i + 1]), lb)
                    dve.tensor_scalar(APX[:, 0:n], APX[:, 0:n], PLS[:, i:i + 1], None, ALU.mult).then_inc(ap_ok, 1)
                if p % 4 == 2:
                    dve.wait_ge(ath_ok, 4 * a + i + 1)
                    dve.tensor_tensor(APL[:, 0:n], bk[:, 0:n], f32(APH[:, 0:n]), ALU.subtract).then_inc(atl_ok, 1)

            def page_maxima(b, q, lb):
                dve.wait_ge(sc_ok, 4 * b + q + 1)
                if q == 3:
                    last_page = SC[:, (NPG - 1) * P:NPG * P]
                    link(dve.tensor_tensor(last_page, last_page, B15[:], ALU.add), lb)
                return dve.tensor_reduce(PMX[:, 4 * q:4 * q + 4], SC[:, 4 * q * P:4 * (q + 1) * P].rearrange("p (g n) -> p g n", g=4), AX.X, ALU.max)

            def scale_out(b):
                dve.wait_ge(pv_pe, 16 * (b + 1))
                dve.tensor_scalar(OTS, OUT, RL[:], None, ALU.mult).then_inc(ots_ok, 1)

            def out_sample(b):
                for e in range(2):
                    rr = slice(e * HD, (e + 1) * HD)
                    last = dve.tensor_copy(ATS[rr, :, bass.ds(TD * b, TD)], OTP[rr, :, 4 * e:4 * e + 4])
                last.then_inc(ot_ev, 1)

            def sample(b, pv):
                lb = None if isinstance(b, int) and b == 0 else b
                if lb is not None:
                    chain[0] = first_links[0]
                for p in range(NPG):
                    page_lo(b, p)
                    if pv and p + 1 < NPG:
                        value_hi(b - 1, p + 1)
                    if pv:
                        a_step(b - 1, p, lb)
                        if p == 3:
                            split_loop(b - 1, 5)
                    if p == 11:
                        split_loop(b, 2)
                    if p in (7, 10, 15):
                        page_maxima(b, (p - 6) // 4, lb)
                if pv:
                    scale_out(b - 1)
                link(page_maxima(b, 3, lb), lb)
                dve.wait_ge(loc_pe, b + 1)
                loc = SC[:, NPG * P:NPG * P + 32]
                link(dve.tensor_tensor(loc, LOC, LM[:, bass.ds(b, 1), :].rearrange("p a n -> p (a n)"), ALU.add), lb)
                dve.tensor_reduce(BMX[:, 8:9], loc, AX.X, ALU.max)
                if pv:
                    out_sample(b - 1)
                dve.tensor_tensor(BMX[:, 0:8], PMX[:, 0::2], PMX[:, 1::2], ALU.max)
                link(dve.tensor_tensor(GATE[:], KSUM[:, 0::2], KSUM[:, 1::2], ALU.add), lb)
                ga = GATE[:]
                by_m = bass.AP(ga.tensor, ga.offset, [list(ga.ap[0]), [0, 8], [1, 8]])
                by_n = bass.AP(ga.tensor, ga.offset, [list(ga.ap[0]), [1, 8], [0, 8]])
                dve.tensor_tensor(CM1[:], by_m, by_n, ALU.is_gt)
                link(dve.tensor_tensor(CM2[:], by_m, by_n, ALU.is_equal), lb)
                link(dve.tensor_tensor(CM2[:], CM2[:], TRI, ALU.mult), lb)
                link(dve.tensor_tensor(CM1[:], CM1[:], CM2[:], ALU.add), lb)
                link(dve.tensor_reduce(RANK[:], CM1[:], AX.X, ALU.add), lb)
                link(dve.tensor_scalar(SEL[:], RANK[:], TOPK - 0.5, NEG, ALU.is_ge, ALU.mult), lb)
                link(dve.tensor_tensor(BMX[:, 0:8], BMX[:, 0:8], SEL[:], ALU.add), lb)
                link(dve.tensor_reduce(M1[:], BMX[:], AX.X, ALU.max), lb)
                link(dve.tensor_scalar(NEGM[:], M1[:], -1.0 / UNIT, None, ALU.mult), lb)
                dve.tensor_scalar(EB[:], SEL[:], NEGM[:], None, ALU.add).then_inc(eb_ok, 1)
                split_loop(b, 3)
                value_hi(b, 0)
                split_loop(b, 4)
                dve.wait_ge(ex_ok, 2 * b + 2)
                link(dve.tensor_reduce(LT[:], LSUM[:], AX.X, ALU.add), lb)
                dve.reciprocal(RL[0:32, :], LT[:])
                dve.reciprocal(RL[32:64, :], LT[:])
                dve.wait_ge(pth_ok, b + 1)
                dve.tensor_tensor(PT[:, :, 32:64], PTP, f32(PT[:, :, 0:32]), ALU.subtract)
                dve.tensor_tensor(PTL[:, 32:64], PTLP, f32(PTL[:, 0:32]), ALU.subtract).then_inc(ptl_ok, 1)
                if lb is not None:
                    assert chain[0] - first_links[0] == loop_links[0]

            sample(0, False)
            first_links[0] = chain[0]
            loop_links[0] = chain[0] - before_samples + 12
            with dve.Fori(1, NB) as b:
                sample(b, True)
            chain[0] = first_links[0] + loop_links[0] * (NB - 1)

            split_loop(NB - 1, 5)
            def norm_rows(r):
                n = P if r < 4 else NSR
                bk = BK[4 + r % 2]
                dst = VN[:, r, :] if r < 4 else VNS[:]
                dve.wait_ge(vr_pe, r + 1)
                if r == 0:
                    dve.wait_ge(ln_ld, 32)
                link(dve.bn_stats(BST[0:n, 0, 0:6], bk[0:n, :]))
                link(dve.bn_aggr(BST[0:n, 1, 0:2], BST[0:n, 0, 0:6]))
                dve.tensor_scalar(MS[0:n, r:r + 1], BST[0:n, 1, 1:2], 4.0 * LN_EPS, None, ALU.add).then_inc(var_ok, 1)
                link(dve.scalar_tensor_tensor(out=dst, in0=bk[0:n, :], scalar=BST[0:n, 1, 0:1], in1=LNG[0:n], op0=ALU.subtract, op1=ALU.mult))
                dve.wait_ge(vrs_ok, r + 1)
                dve.scalar_tensor_tensor(out=dst, in0=dst, scalar=RSTD[0:n, r:r + 1], in1=LNB[0:n], op0=ALU.mult, op1=ALU.add).then_inc(vn_ok, 1)

            for p in range(NPG):
                a_step(NH - 1, p)
                if p < len(GATE_STEPS):
                    kind, g0 = GATE_STEPS[p]
                    dve.wait_ge(el_act, p + 1)
                    gx, gt = G[:, g0:g0 + 2, :], GT[:, p % 2]
                    dve.scalar_tensor_tensor(out=gt if kind == "square" else gx, in0=gt, scalar=1.0, in1=gx, op0=ALU.add,
                                             op1=ALU.mult).then_inc(el_dve, 1)
                if p == 3:
                    dve.wait_ge(wst_pe, 1)
                    tr = SGC[:, T_TRIL:T_TRIL + P]
                    trb = bass.AP(tr.tensor, tr.offset, [list(tr.ap[0]), [0, 4], [1, P]])
                    for x in range(2):
                        last = dve.tensor_tensor(WST[:, 4 * x:4 * x + 4, :], BK[2 + x][:].rearrange("p (g n) -> p g n", g=4), trb, ALU.mult)
                    last.then_inc(wst_ok, 1)
                if p == 5:
                    dve.wait_ge(wsb_pe, 1)
                    dg = SGC[0:32, T_DIAG:T_DIAG + 32]
                    dve.tensor_tensor(WSB[:], BK[2][0:32, 0:256].rearrange("p (g n) -> p g n", g=NH),
                                      bass.AP(dg.tensor, dg.offset, [list(dg.ap[0]), [0, NH], [1, 32]]), ALU.mult).then_inc(wsb_ok, 1)
                if p >= 8 and p % 2 == 0:
                    norm_rows((p - 8) // 2)
            scale_out(NB - 1)
            dve.wait_ge(at_ld, 32)
            dve.wait_ge(el_dve, len(GATE_STEPS))
            dve.tensor_tensor(G[:, GA:GA + 3, 0:SEQ], G[:, GA:GA + 3, 0:SEQ], AT[:, 0:3, :], ALU.mult)
            dve.tensor_tensor(G[0:64, GA + 3, 0:SEQ], G[0:64, GA + 3, 0:SEQ], AT[0:64, 3, :], ALU.mult)
            dve.wait_ge(ao_ok, 4 * NH)
            dve.tensor_tensor(G[64:128, GA + 3, 0:SEQ], G[64:128, GA + 3, 0:SEQ], AO, ALU.mult)
            dve.wait_ge(loc_pe, NB + 1)
            out_sample(NB - 1)
            dve.wait_ge(ot_ev, NB)
            dve.tensor_tensor(G[:, GA:GA + 4, SEQ:ROWS], G[:, GA:GA + 4, SEQ:ROWS], ATS[:], ALU.mult).then_inc(y_ok, 1)
            norm_rows(4)

            def y_low(k):
                dve.wait_ge(y_hi, k + 1)
                g0 = (GA, GB)[k]
                dve.tensor_tensor(XL[:, 4 * k:4 * k + 4, :], G[:, g0:g0 + 4, :], f32(XH[:, 4 * k:4 * k + 4, :]), ALU.subtract).then_inc(y_lo, 1)

            def spatial(r):
                dve.wait_ge(z_pe, r + 1)
                if r == 0:
                    dve.wait_ge(bs_ld, 32)
                    dve.wait_ge(ug_ok, 1)
                if r < 4:
                    tz, gb = TZ[:, r % 2], G[:, GB:GB + 4, r * P:(r + 1) * P]
                    dve.tensor_tensor(tz, BK[2 + r % 2][:].rearrange("p (c n) -> p c n", c=PAIRS), BSB[:], ALU.add).then_inc(z_ev, 1)
                    dve.wait_ge(z_ev, r + 1)
                    dve.scalar_tensor_tensor(out=gb, in0=tz, scalar=0.5, in1=gb, op0=ALU.mult, op1=ALU.mult)
                else:
                    gb = G[:, GB:GB + 4, SEQ:ROWS]
                    bsv = BSB[:, :, 0:TD]
                    link(dve.tensor_tensor(TZ[:, 0, :, 0:32].rearrange("p c (b t) -> p c b t", t=TD),
                                           BK[2][:, 0:128].rearrange("p (c b t) -> p c b t", c=PAIRS, t=TD),
                                           bass.AP(bsv.tensor, bsv.offset, [list(bsv.ap[0]), [P, PAIRS], [0, NB], [1, TD]]), ALU.add))
                    dve.scalar_tensor_tensor(out=gb, in0=TZ[:, 0, :, 0:32], scalar=0.5, in1=gb, op0=ALU.mult, op1=ALU.mult).then_inc(y_ok, 1)

            def mixed(units):
                for e in units:
                    br, n, k0, j, h = unit(e)
                    cs = slice(h * HALF, (h + 1) * HALF)
                    dve.wait_ge(pj, 2 * N_IN + e + 1)
                    g = G[:, (GMA, GMB)[br] + j, cs]
                    last = dve.scalar_tensor_tensor(out=g, in0=g, scalar=1.0, in1=MBK[e % 4][:, 0:HALF], op0=ALU.add, op1=ALU.mult)
                    if br == 0:
                        last.then_inc(mix_ok, 1)
                    else:
                        link(last)
                        ga = G[:, GMA + j, cs]
                        dve.tensor_tensor(ga, ga, g, ALU.add).then_inc(mix_ok, 1)
                        if e > 16:
                            mix_low(e - 1)

            def mix_low(e):
                br, n, k0, j, h = unit(e)
                cs = slice(h * HALF, (h + 1) * HALF)
                dve.wait_ge(mx_hi, e - 16 + 1)
                dve.tensor_tensor(ML[:, j, cs], G[:, GMA + j, cs], f32(MH[:, j, cs]), ALU.subtract).then_inc(mx_lo, 1)

            def next_tile(n):
                split_lo(n, n // 2 % 2, n % 2, n % 2)

            y_low(0)
            dve.wait_ge(m_ok, 4)
            spatial(0)
            spatial(1)
            mixed(range(4))
            next_tile(N_IN + 2)
            spatial(2)
            spatial(3)
            mixed(range(4, 8))
            next_tile(N_IN + 3)
            spatial(4)
            y_low(1)
            for t in range(2, 4):
                mixed(range(4 * t, 4 * t + 4))
                next_tile(N_IN + t + 2)
            dve.wait_ge(m_ok, 8)
            for t in range(4, 8):
                mixed(range(4 * t, 4 * t + 4))
                if t == 7:
                    mix_low(31)
                next_tile(N_IN + t + 2)
            def residual(u):
                kk, r = u // 5, u % 5
                n = P if r < 4 else NSR
                dve.wait_ge(fr_pe, u + 1)
                if u == 0:
                    dve.wait_ge(fx_ld, 16 * 5)
                hx = FX[0:n, r, 512 * kk:512 * kk + 512]
                dve.scalar_tensor_tensor(out=hx, in0=BK[4 + u % 4][0:n, :], scalar=0.25, in1=hx, op0=ALU.mult, op1=ALU.add).then_inc(h_ok, 1)

            for j in range(N_OUT):
                n = N_IN + N_MIX + j + 2
                if j == 4:
                    for u in range(5):
                        residual(u)
                if j + 2 < N_OUT:
                    split_lo(n, n // 2 % 2, n % 2, n % 2)
            for u in range(5, 10):
                residual(u)
            for r in range(5):
                n = P if r < 4 else NSR
                dve.wait_ge(fss_ok, r + 1)
                dve.tensor_scalar(MS[0:n, r:r + 1], SS[0:n, r:r + 1], 1.0 / DM, EPS, ALU.mult, ALU.add).then_inc(fms_ok, 1)
            dve.wait_ge(fg_ld, 16)
            for r in range(5):
                n = P if r < 4 else NSR
                dve.wait_ge(frs_ok, r + 1)
                dve.scalar_tensor_tensor(out=FX[0:n, r, :], in0=FX[0:n, r, :], scalar=RSTD[0:n, r:r + 1], in1=FG[0:n], op0=ALU.mult,
                                         op1=ALU.mult).then_inc(fy_ok, 1)

        @block.gpsimd
        def _(pool):
            def f32(t):
                return t.bitcast(F32)

            pool.wait_ge(zero_ok, 4)
            for r in range(5):
                n = P if r < 4 else NSR
                pool.wait_ge(ms_ok, r + 1)
                pool.tensor_tensor(RSTD[0:n, r:r + 1], MS[0:n, r:r + 1], NHALF[0:n], ALU.pow).then_inc(rstd_ok, 1)
                if r == 2 or r == 4:
                    n = r // 2 - 1
                    if n:
                        pool.wait_ge(rstd_ok, 5)
                    pool.wait_ge(w_hi, n + 1)
                    pool.tensor_tensor(WL[:, n], WRAW[:, 0, :, n * P:(n + 1) * P], f32(WH[:, n]), ALU.subtract).then_inc(w_lo, 1)
            pool.wait_ge(tab_ok, 1)
            vec = VEC[:]
            pitch = NH * (P + VLEN)
            pool.dma_start(bass.AP(skew_d.tensor, skew_d.offset, [[P + VLEN, NH], [pitch + 1, P], [1, VLEN]]),
                           bass.AP(vec.tensor, vec.offset, [list(vec.ap[0]), [0, P], [1, VLEN]])).then_inc(vec_st, 16)
            def store_rows(n):
                pool.wait_ge(rs_ev, n - 4 + 1)
                to_p, to_s = ((k_p, k_s), (v_p, v_s))[n // 4 - 1]
                cols = slice(n % 4 * P, (n % 4 + 1) * P)
                pool.dma_start(to_p[0, 0].rearrange("(r p) h d -> p r (h d)", p=P)[:, :, cols], RS[:, n % 4]).then_inc(rs_st[n % 4], 16)
                pool.dma_start(to_s[0].rearrange("b t h d -> (b t) (h d)")[:, cols], RSS[:, n % 4]).then_inc(rs_st[n % 4], 16)

            for n in range(N_QKV):
                c = n % 4
                if n < 8:
                    pool.wait_ge(pj_ev, 2 * n + 2)
                    pool.dma_start((q_d, k_d)[n // 4][2 * c:2 * c + 2].rearrange("e p n -> (e p) n"), TS[:, n % 4, 0:SEQ]).then_inc(ts_st[n % 4], 16)
                if n >= 5:
                    store_rows(n - 1)
            store_rows(N_QKV - 1)
            pool.wait_ge(smp_ok, 4)

            def place_q(b):
                qc = QC[:]
                out = bass.AP(qc.tensor, qc.offset, [list(qc.ap[0]), [64 + 8, PAIRS], [32, 2], [1, 8]])
                pool.tensor_copy(out, Q16[:, :, bass.ds(b, 1), :].rearrange("p c a (w x) -> p c (a w) x", w=2)).then_inc(qc_ok, 1)

            place_q(0)

            def value_lo(b, p):
                pool.wait_ge(vh, 16 * b + p + 1)
                pool.tensor_tensor(VL[:, p % 2, :], VRAW[:, p // 2 % 2, p % 2, :], f32(VH[:, p % 2, :]), ALU.subtract).then_inc(vl, 1)

            def stage_lo(a):
                pool.wait_ge(stg_hi, 2 * a + 1)
                pool.wait_ge(qc_ok, a + 1 if isinstance(a, int) and a == NH - 1 else a + 2)
                wait(pool, vl, 16 * a)
                pool.tensor_tensor(QKL, QKR, f32(QKH), ALU.subtract).then_inc(stg_lo, 1)
                pool.wait_ge(stg_hi, 2 * a + 2)
                pool.wait_ge(stg_lo, 2 * a + 1)
                pool.tensor_tensor(AVL[:], AVR[:], f32(AVH[:]), ALU.subtract).then_inc(stg_lo, 1)

            def sample(b, pv):
                if pv:
                    for p in range(1, NPG):
                        value_lo(b - 1, p)
                if not (isinstance(b, int) and b == NB - 1):
                    pool.wait_ge(loc_pe, b + 1)
                    place_q(b + 1)
                stage_lo(b)
                value_lo(b, 0)

            sample(0, False)
            with pool.Fori(1, NB - 1) as b:
                sample(b, True)
            sample(NB - 1, True)

            def inverse_root(r, ready, done):
                n = P if r < 4 else NSR
                pool.wait_ge(ready, r + 1)
                wait(pool, done, r)
                pool.tensor_tensor(RSTD[0:n, r:r + 1], MS[0:n, r:r + 1], NHALF[0:n], ALU.pow).then_inc(done, 1)

            for p in range(1, NPG):
                value_lo(NB - 1, p)
                if p >= 9 and p % 2 == 1:
                    inverse_root((p - 9) // 2, var_ok, vrs_ok)
            pool.wait_ge(el_dve, 10)
            pool.tensor_tensor(G[:, GB:GB + 4, :], G[:, GB:GB + 4, :], G[:, GU:GU + 4, :], ALU.mult).then_inc(ug_ok, 1)
            pool.wait_ge(ug_ok, 1)
            inverse_root(4, var_ok, vrs_ok)
            pool.wait_ge(vn_ok, 5)
            pool.dma_start(sgu_s.rearrange("a b t d -> (a b t) d"), VNS[:]).then_inc(sgu_st, 16)
            for r in range(5):
                inverse_root(r, fms_ok, frs_ok)


_INS = ["x_prompt", "x_sample", "cache_k", "cache_v", "page_table", "rel_bias", "norm_g", "w_in", "sgu_ln_g", "sgu_ln_b",
        "w_s", "b_s", "w_pa", "w_pb", "w_o", "final_norm_g"]
_OUTS = [(1, SEQ, DM), (NB, TD, DM), (1, 1, SEQ, NH, HD), (1, 1, SEQ, NH, HD), (1, NB, TD, NH, HD), (1, NB, TD, NH, HD), (1, NB, TD, DA)]


def kernel(**inputs):
    import concourse.bacc as _bacc
    from concourse.bass_utils import run_bass_kernel_spmd as _run

    nc = _bacc.Bacc("TRN2", target_bir_lowering=False, num_devices=1)
    arrays, args = {}, []
    named = [(n, np.ascontiguousarray(inputs[n])) for n in _INS]
    named += list(zip(("constants", "setup_constants", "gating_constants"), constants()))
    for name, a in named:
        arrays[f"in_{name}"] = a
        args.append(nc.dram_tensor(f"in_{name}", a.shape, mybir.dt.from_np(a.dtype), kind="ExternalInput").ap())
    for i, shape in enumerate(_OUTS):
        args.append(nc.dram_tensor(f"out_{i}", shape, F32, kind="ExternalOutput").ap())
    build(nc, *args)
    r = _run(nc, [arrays], core_ids=[0])
    return tuple(r.results[0][f"out_{i}"] for i in range(len(_OUTS)))
```
